# Optimizing a Trainium2 kernel written in Bass

```python
import math
import jax, jax.numpy as jnp
from jax import lax
import numpy as np

D_MODEL = 1024
BATCH = 1
SEQ = 512
DEPTH = 2
DEC_BATCH = 8
DEC_SEQ = 8
PAST_LEN = 4096
PAGE_SIZE = 128

N_MIXERS = 2
N_A = (DEPTH + 1) // 2
N_B = DEPTH // 2
H_DN = 8
DK = 128
DV = 128
QKV_DIM = 2 * H_DN * DK + H_DN * DV
A_IN_DIM = QKV_DIM + H_DN * DV + 2 * H_DN
DN_CONV = 4
CHUNK = 64
SC_CONV = 3
D_FF = 2816
FFN_CONV = 3
D_PLE = 256
ALPHA = (2.0 * DEPTH) ** 0.25
BETA_INIT = (8.0 * DEPTH) ** -0.25
LN_EPS = 1e-5
RMS_EPS = 1e-6
L2_EPS = 1e-6

kernel_name = 'hybrid_deltanet_shortconv_convffn_step'

def layer_norm(x, g, b):
    xf = x.astype(jnp.float32)
    mu = jnp.mean(xf, -1, keepdims=True)
    var = jnp.mean(jnp.square(xf - mu), -1, keepdims=True)
    y = (xf - mu) * lax.rsqrt(var + LN_EPS) * g.astype(jnp.float32) + b.astype(jnp.float32)
    return y.astype(x.dtype)

def causal_dwconv(u, w, buf):
    W = w.shape[0]
    L = u.shape[1]
    ext = jnp.concatenate([buf.astype(u.dtype), u], axis=1)
    y = ext[:, 0:L] * w[0]
    for j in range(1, W):
        y = y + ext[:, j:j + L] * w[j]
    return y, ext[:, ext.shape[1] - (W - 1):]

def l2norm(t):
    return t * lax.rsqrt(jnp.sum(t * t, -1, keepdims=True) + L2_EPS)

def gated_delta_chunked(q, k, v, g, beta, S0):
    B, L, H, _ = q.shape
    C = min(CHUNK, L)
    pad = (-L) % C
    if pad:
        pw = ((0, 0), (0, pad), (0, 0), (0, 0))
        q = jnp.pad(q, pw); k = jnp.pad(k, pw); v = jnp.pad(v, pw)
        g = jnp.pad(g, pw[:3]); beta = jnp.pad(beta, pw[:3])
    N = (L + pad) // C

    def chunks(t):
        t = t.reshape((B, N, C, H) + t.shape[3:])
        return jnp.moveaxis(t, (1, 3), (0, 2))

    q = chunks(q) * (DK ** -0.5)
    k = chunks(k)
    v = chunks(v)
    gc = jnp.cumsum(chunks(g), axis=-1)
    bt = chunks(beta)[..., None]
    kb = k * bt
    vb = v * bt
    idx = jnp.arange(C)
    causal = idx[:, None] >= idx[None, :]
    strict = idx[:, None] > idx[None, :]
    decay = jnp.exp(jnp.where(causal, gc[..., :, None] - gc[..., None, :], -jnp.inf))
    A = jnp.where(strict, jnp.einsum('nbhid,nbhjd->nbhij', kb, k) * decay, 0.0)
    rhs = jnp.concatenate([vb, kb * jnp.exp(gc)[..., None]], axis=-1)
    sol = lax.linalg.triangular_solve(A + jnp.eye(C, dtype=A.dtype), rhs,
                                      left_side=True, lower=True, unit_diagonal=True)
    u = sol[..., :DV]
    w = sol[..., DV:]
    att = jnp.einsum('nbhid,nbhjd->nbhij', q, k) * decay

    def step(S, xs):
        q_c, k_c, u_c, w_c, gc_c, att_c = xs
        v_new = u_c - jnp.einsum('bhck,bhkv->bhcv', w_c, S)
        o = (jnp.einsum('bhck,bhkv->bhcv', q_c * jnp.exp(gc_c)[..., None], S)
             + jnp.einsum('bhij,bhjv->bhiv', att_c, v_new))
        g_last = gc_c[..., -1]
        S = (S * jnp.exp(g_last)[..., None, None]
             + jnp.einsum('bhck,bhcv->bhkv', k_c * jnp.exp(g_last[..., None] - gc_c)[..., None], v_new))
        return S, o

    S, o = lax.scan(step, S0, (q, k, u, w, gc, att))
    o = jnp.moveaxis(o, (0, 2), (1, 3)).reshape(B, N * C, H, DV)[:, :L]
    return o, S

def delta_mixer(x, conv_buf, S0, w_in, conv_w, a_log, dt_bias, norm_g, w_out):
    B, L, _ = x.shape
    proj = x @ w_in
    qkv = proj[..., :QKV_DIM]
    z = proj[..., QKV_DIM:QKV_DIM + H_DN * DV]
    ba = proj[..., QKV_DIM + H_DN * DV:].astype(jnp.float32)
    qkv_c, new_buf = causal_dwconv(qkv, conv_w, conv_buf)
    qkv_c = jax.nn.silu(qkv_c.astype(jnp.float32))
    q = l2norm(qkv_c[..., :H_DN * DK].reshape(B, L, H_DN, DK))
    k = l2norm(qkv_c[..., H_DN * DK:2 * H_DN * DK].reshape(B, L, H_DN, DK))
    v = qkv_c[..., 2 * H_DN * DK:].reshape(B, L, H_DN, DV)
    beta = jax.nn.sigmoid(ba[..., :H_DN])
    g = -jnp.exp(a_log.astype(jnp.float32)) * jax.nn.softplus(ba[..., H_DN:] + dt_bias.astype(jnp.float32))
    o, S = gated_delta_chunked(q, k, v, g, beta, S0.astype(jnp.float32))
    o = (o * lax.rsqrt(jnp.mean(o * o, -1, keepdims=True) + RMS_EPS) * norm_g.astype(jnp.float32)
         * jax.nn.silu(z.astype(jnp.float32).reshape(B, L, H_DN, DV)))
    y = o.reshape(B, L, H_DN * DV).astype(x.dtype) @ w_out
    return y, new_buf, S.astype(S0.dtype)

def shortconv_mixer(x, buf, w_in, conv_w, w_out):
    proj = x @ w_in
    b = proj[..., :D_MODEL]
    c = proj[..., D_MODEL:2 * D_MODEL]
    h = proj[..., 2 * D_MODEL:]
    uc, new_buf = causal_dwconv(c * h, conv_w, buf)
    return (b * uc) @ w_out, new_buf

def conv_ffn(x, buf, w_up, conv_w, w_down):
    hc, new_buf = causal_dwconv(x @ w_up, conv_w, buf)
    return (jax.nn.silu(hc[..., D_FF:]) * hc[..., :D_FF]) @ w_down, new_buf

def trunk(x, p, dn_conv, dn_S, sc_conv, ffn_conv,
          dn_w_in, dn_conv_w, dn_a_log, dn_dt_bias, dn_norm_g, dn_w_out,
          sc_w_in, sc_conv_w, sc_w_out, ffn_w_up, ffn_conv_w, ffn_w_down,
          ln_mix_g, ln_mix_b, ln_ffn_g, ln_ffn_b, ple_w_proj, ple_w_gate):
    new_dn_conv, new_dn_S, new_sc, new_ffn = [], [], [], []
    for i in range(DEPTH):
        j = i // N_MIXERS
        if i % N_MIXERS == 0:
            mix, cb, S = delta_mixer(x, dn_conv[j], dn_S[j], dn_w_in[j], dn_conv_w[j], dn_a_log[j],
                                     dn_dt_bias[j], dn_norm_g[j], dn_w_out[j])
            new_dn_conv.append(cb)
            new_dn_S.append(S)
        else:
            mix, sb = shortconv_mixer(x, sc_conv[j], sc_w_in[j], sc_conv_w[j], sc_w_out[j])
            new_sc.append(sb)
        x = layer_norm(ALPHA * x + mix, ln_mix_g[i], ln_mix_b[i])
        f, fb = conv_ffn(x, ffn_conv[i], ffn_w_up[i], ffn_conv_w[i], ffn_w_down[i])
        new_ffn.append(fb)
        x = layer_norm(ALPHA * x + f, ln_ffn_g[i], ln_ffn_b[i])
        x = x + (p[i].astype(x.dtype) @ ple_w_proj[i]) * jax.nn.sigmoid(x @ ple_w_gate[i])
    return x, jnp.stack(new_dn_conv), jnp.stack(new_dn_S), jnp.stack(new_sc), jnp.stack(new_ffn)

def setup_inputs(seed: int = 0) -> dict:
    key = jax.random.key(seed)
    ks = iter(jax.random.split(key, 40))
    f32 = jnp.float32

    def nrm(shape, scale):
        return jax.random.normal(next(ks), shape, f32) * scale

    x_prompt = nrm((BATCH, SEQ, D_MODEL), 1.0)
    x_sample = nrm((DEC_BATCH, DEC_SEQ, D_MODEL), 1.0)
    p_prompt = nrm((DEPTH, BATCH, SEQ, D_PLE), 1.0)
    p_sample = nrm((DEPTH, DEC_BATCH, DEC_SEQ, D_PLE), 1.0)
    state_dn_conv = nrm((N_A, DEC_BATCH, DN_CONV - 1, QKV_DIM), 1.0)
    state_dn_S = nrm((N_A, DEC_BATCH, H_DN, DK, DV), 0.05)
    state_sc_conv = nrm((N_B, DEC_BATCH, SC_CONV - 1, D_MODEL), 1.0)
    state_ffn_conv = nrm((DEPTH, DEC_BATCH, FFN_CONV - 1, 2 * D_FF), 1.0)

    dn_w_in = nrm((N_A, D_MODEL, A_IN_DIM), D_MODEL ** -0.5)
    dn_conv_w = nrm((N_A, DN_CONV, QKV_DIM), DN_CONV ** -0.5)
    dn_a_log = jnp.log(jax.random.uniform(next(ks), (N_A, H_DN), f32, 1.0, 16.0))
    dt = jnp.exp(jax.random.uniform(next(ks), (N_A, H_DN), f32, math.log(1e-3), math.log(1e-1)))
    dn_dt_bias = dt + jnp.log(-jnp.expm1(-dt))
    dn_norm_g = 1.0 + nrm((N_A, DV), 0.02)
    dn_w_out = nrm((N_A, H_DN * DV, D_MODEL), (H_DN * DV) ** -0.5 * BETA_INIT)

    sc_w_in = nrm((N_B, D_MODEL, 3 * D_MODEL), D_MODEL ** -0.5)
    sc_conv_w = nrm((N_B, SC_CONV, D_MODEL), SC_CONV ** -0.5)
    sc_w_out = nrm((N_B, D_MODEL, D_MODEL), D_MODEL ** -0.5 * BETA_INIT)

    ffn_w_up = nrm((DEPTH, D_MODEL, 2 * D_FF), D_MODEL ** -0.5)
    ffn_conv_w = nrm((DEPTH, FFN_CONV, 2 * D_FF), FFN_CONV ** -0.5)
    ffn_w_down = nrm((DEPTH, D_FF, D_MODEL), D_FF ** -0.5 * BETA_INIT)

    ln_mix_g = 1.0 + nrm((DEPTH, D_MODEL), 0.02)
    ln_mix_b = nrm((DEPTH, D_MODEL), 0.02)
    ln_ffn_g = 1.0 + nrm((DEPTH, D_MODEL), 0.02)
    ln_ffn_b = nrm((DEPTH, D_MODEL), 0.02)
    ple_w_proj = nrm((DEPTH, D_PLE, D_MODEL), D_PLE ** -0.5)
    ple_w_gate = nrm((DEPTH, D_MODEL, D_MODEL), D_MODEL ** -0.5)

    return {'x_prompt': x_prompt, 'x_sample': x_sample, 'p_prompt': p_prompt, 'p_sample': p_sample,
            'state_dn_conv': state_dn_conv, 'state_dn_S': state_dn_S,
            'state_sc_conv': state_sc_conv, 'state_ffn_conv': state_ffn_conv,
            'dn_w_in': dn_w_in, 'dn_conv_w': dn_conv_w, 'dn_a_log': dn_a_log, 'dn_dt_bias': dn_dt_bias,
            'dn_norm_g': dn_norm_g, 'dn_w_out': dn_w_out,
            'sc_w_in': sc_w_in, 'sc_conv_w': sc_conv_w, 'sc_w_out': sc_w_out,
            'ffn_w_up': ffn_w_up, 'ffn_conv_w': ffn_conv_w, 'ffn_w_down': ffn_w_down,
            'ln_mix_g': ln_mix_g, 'ln_mix_b': ln_mix_b, 'ln_ffn_g': ln_ffn_g, 'ln_ffn_b': ln_ffn_b,
            'ple_w_proj': ple_w_proj, 'ple_w_gate': ple_w_gate}

def reference(x_prompt, x_sample, p_prompt, p_sample, state_dn_conv, state_dn_S, state_sc_conv, state_ffn_conv,
              dn_w_in, dn_conv_w, dn_a_log, dn_dt_bias, dn_norm_g, dn_w_out,
              sc_w_in, sc_conv_w, sc_w_out, ffn_w_up, ffn_conv_w, ffn_w_down,
              ln_mix_g, ln_mix_b, ln_ffn_g, ln_ffn_b, ple_w_proj, ple_w_gate):
    Bp = x_prompt.shape[0]
    dt_act = x_prompt.dtype
    z_dn_conv = jnp.zeros((N_A, Bp, DN_CONV - 1, QKV_DIM), dt_act)
    z_dn_S = jnp.zeros((N_A, Bp, H_DN, DK, DV), state_dn_S.dtype)
    z_sc_conv = jnp.zeros((N_B, Bp, SC_CONV - 1, D_MODEL), dt_act)
    z_ffn_conv = jnp.zeros((DEPTH, Bp, FFN_CONV - 1, 2 * D_FF), dt_act)

    y_prompt, prompt_dn_conv, prompt_dn_S, prompt_sc_conv, prompt_ffn_conv = trunk(
        x_prompt, p_prompt, z_dn_conv, z_dn_S, z_sc_conv, z_ffn_conv,
        dn_w_in, dn_conv_w, dn_a_log, dn_dt_bias, dn_norm_g, dn_w_out,
        sc_w_in, sc_conv_w, sc_w_out, ffn_w_up, ffn_conv_w, ffn_w_down,
        ln_mix_g, ln_mix_b, ln_ffn_g, ln_ffn_b, ple_w_proj, ple_w_gate)

    y_sample, sample_dn_conv, sample_dn_S, sample_sc_conv, sample_ffn_conv = trunk(
        x_sample, p_sample, state_dn_conv, state_dn_S, state_sc_conv, state_ffn_conv,
        dn_w_in, dn_conv_w, dn_a_log, dn_dt_bias, dn_norm_g, dn_w_out,
        sc_w_in, sc_conv_w, sc_w_out, ffn_w_up, ffn_conv_w, ffn_w_down,
        ln_mix_g, ln_mix_b, ln_ffn_g, ln_ffn_b, ple_w_proj, ple_w_gate)

    return (y_prompt, y_sample,
            prompt_dn_conv, prompt_dn_S, prompt_sc_conv, prompt_ffn_conv,
            sample_dn_conv, sample_dn_S, sample_sc_conv, sample_ffn_conv)


_drawn_inputs = setup_inputs


def setup_inputs(seed=0):
    import zlib

    import numpy as np

    out = dict(_drawn_inputs(seed))
    spreads = {}
    factors = {'dn_norm_g': 22.193}
    for name, (base, spread) in spreads.items():
        noise = np.random.default_rng([zlib.crc32(name.encode()), seed]).standard_normal(out[name].shape)
        drawn = base * np.exp(spread * noise) if base else spread * noise
        out[name] = __import__('jax').numpy.asarray(drawn.astype(out[name].dtype))
    for name, factor in factors.items():
        out[name] = (out[name] * factor).astype(out[name].dtype)
    return out
```

```python
from contextlib import ExitStack

import concourse.bass as bass
from concourse import mybir

F32 = mybir.dt.float32
ACT = mybir.ActivationFunctionType
ALU = mybir.AluOpType

P = 128
D = 1024
DT = D // P
SEQ = 512
NB, NS = 8, 8
SAMP = NB * NS
TOK = SEQ + SAMP
HALF = TOK // 2
H = 8
QKV_T = 3 * H
FF = 2816
FT = FF // P
PLE_T = 2
CH = 128
NCH = SEQ // CH
LEVELS, SAMP_LEVELS = 7, 3
SLOTS = 4
WCOLS = 11 * P
ALPHA = 4.0 ** 0.25
A_ROW = 32


def ext_cols(width):
    return (width - 1) + SEQ + NB * (width - 1 + NS)


def build(nc, I, O):
    with ExitStack() as ctx:
        def sb(name, shape):
            return ctx.enter_context(nc.sbuf_tensor(name, shape, F32))

        def sem(name):
            return ctx.enter_context(nc.semaphore(name))

        shared = {}

        def phase_sems(kind, names):
            if kind not in shared:
                shared[kind] = [sem(f"{kind}_{x}") for x in names]
            else:
                with nc.Block() as block:
                    @block.sync
                    def _(sync):
                        for x in shared[kind]:
                            sync.sem_clear(x)
            return shared[kind]

        X = sb("x", [P, DT, TOK])
        Y = sb("y", [P, DT, TOK])
        Z = sb("z", [P, DT, TOK])
        BIG = sb("big", [P, QKV_T, TOK])
        RING = sb("ring", [P, SLOTS, WCOLS])
        SCR = sb("scratch", [P, 15424])
        MASKT = sb("mask_decay", [P, P])
        MASKS = sb("mask_decay_sample", [P, SAMP])
        MASKL = sb("mask_levels", [P, LEVELS, P])
        IDENT = sb("identity", [P, P])
        ONES = sb("ones", [P, P])
        CV = sb("column_constants", [P, 160])
        TOKS = sb("token_scalars", [P, NCH + 1, 4, H])
        BANK = [ctx.enter_context(nc.psum_tensor(f"bank{i}", [P, 512], F32)) for i in range(8)]

        class Arena:
            def __init__(self):
                self.at = 0

            def __call__(self, *dims):
                n = 1
                for d in dims:
                    n *= d
                a = SCR[:, self.at:self.at + n]
                self.at += n
                assert self.at <= 15424, self.at
                if len(dims) == 1:
                    return a
                names = "abcd"[:len(dims)]
                return a.rearrange(f"p ({' '.join(names)}) -> p {' '.join(names)}",
                                   **{n: d for n, d in zip(names, dims)})

        lnp = CV[:, 0:64].rearrange("p (k t) -> p k t", k=8)
        norm_g = CV[:, 64:65]
        eps_ln, eps_rms, eps_l2, eps_l2q = (CV[:, 65 + i:66 + i] for i in range(4))
        a_log = CV[A_ROW:A_ROW + H, 69:70]
        dt_bias = CV[A_ROW:A_ROW + H, 70:71]
        neg_ea = CV[A_ROW:A_ROW + H, 71:72]

        w_loaded = [sem(f"w_loaded{s}") for s in range(SLOTS)]
        const_in = sem("const_in")
        x_in = sem("x_in")
        out_done = sem("out_done")
        outs = [0]

        def store(eng, dst, src):
            outs[0] += 16
            eng.dma_start(dst, src).then_inc(out_done, 16)

        streams = [(I["w_qkv"], QKV_T, 8), (I["w_z"], H, 8), (I["w_dout"], DT, 8),
                   (I["w_up0"], 2 * FT, 8), (I["w_down0"], 2 * DT, 11), (I["w_ple0"], DT, 10),
                   (I["w_scin"], 3 * DT, 8), (I["w_scout"], DT, 8),
                   (I["w_up1"], 2 * FT, 8), (I["w_down1"], 2 * DT, 11), (I["w_ple1"], DT, 10)]
        uses = [0]
        for _, n, _ in streams:
            uses.append(uses[-1] + n // SLOTS)

        def load_first(sync, ph):
            w, n, kt = streams[ph]
            for s in range(SLOTS):
                sync.dma_start(RING[:, s, 0:kt * P], w[s]).then_inc(w_loaded[s], 16)

        def load_weights(sync, ph, chunk_done):
            w, n, kt = streams[ph]
            with sync.Fori(1, n // SLOTS) as i:
                for s in range(SLOTS):
                    sync.wait_ge(chunk_done, (i - 1) * SLOTS + s + 1)
                    sync.dma_start(RING[:, s, 0:kt * P],
                                   w[bass.ds(i * SLOTS + s, 1)].rearrange("o p n -> p (o n)")
                                   ).then_inc(w_loaded[s], 16)
            if ph + 1 < len(streams):
                w2, n2, kt2 = streams[ph + 1]
                for s in range(SLOTS):
                    sync.wait_ge(chunk_done, n - SLOTS + s + 1)
                    sync.dma_start(RING[:, s, 0:kt2 * P], w2[s]).then_inc(w_loaded[s], 16)

        def tile_w(s, k):
            return RING[:, s, k * P:(k + 1) * P]

        def product(pe, banks, s, rhs, ks, start, stop):
            for n, k in enumerate(ks):
                for half in range(2):
                    last = pe.matmul(banks[half][:, 0:HALF], tile_w(s, n), rhs(k, half),
                                     start=start and n == 0, stop=stop and n == len(ks) - 1)
            return last

        def x_half(buf):
            return lambda k, half: buf[:, k, half * HALF:(half + 1) * HALF]

        load_n = [0]
        with nc.Block() as block:
            @block.sync
            def _(sync):
                sync.dma_start(X[:], I["x"]).then_inc(x_in, 16)
                load_first(sync, 0)
                for dst, name in ((MASKT, "mask_decay"), (MASKS, "mask_sample"), (MASKL, "mask_levels"),
                                  (IDENT, "identity"), (ONES, "ones"), (CV, "columns")):
                    sync.dma_start(dst[:], I[name]).then_inc(const_in, 16)
                    load_n[0] += 16
                sync.wait_ge(x_in, 16)
                sync.wait_ge(const_in, load_n[0])

            @block.vector
            def _(dve):
                dve.memset(TOKS[:], 0.0)

        def fill_ext(act, banks, ext, hist, filled):
            act.activation(ext[:, hist:hist + HALF], banks[0][:, 0:HALF], ACT.Copy).then_inc(filled, 1)
            act.activation(ext[:, hist + HALF:hist + SEQ], banks[1][:, 0:SEQ - HALF], ACT.Copy).then_inc(filled, 1)
            act.activation(sample_part(ext, hist)[:, :, hist:],
                           banks[1][:, SEQ - HALF:HALF].rearrange("p (b t) -> p b t", b=NB),
                           ACT.Copy).then_inc(filled, 1)

        def sample_part(ext, hist):
            return ext[:, hist + SEQ:hist + SEQ + NB * (hist + NS)].rearrange("p (b t) -> p b t", b=NB)

        def tap_run(dve, ext, out, weights, width, g, tap_done, conv_done):
            n = ext_cols(width) - (width - 1)
            per = width - 1
            dve.tensor_scalar(out[:, 0:n], ext[:, 0:n], weights(0), None, ALU.mult).then_inc(tap_done, 1)
            for j in range(1, width):
                dve.wait_ge(tap_done, g * per + j)
                dve.scalar_tensor_tensor(out=out[:, 0:n], in0=ext[:, j:j + n], scalar=weights(j), in1=out[:, 0:n],
                                         op0=ALU.mult, op1=ALU.add).then_inc(conv_done if j == per else tap_done, 1)

        def history_in(pool, ext, state, c, hist, hist_in):
            pool.tensor_copy(sample_part(ext, hist)[:, :, 0:hist],
                             state[:, bass.ds(c, 1), :].rearrange("p o (b t) -> p (o b) t", b=NB)
                             ).then_inc(hist_in, 1)

        def history_out(pool, ext, new_state, c, hist, saved):
            pool.tensor_copy(new_state[:, bass.ds(c, 1), 0:hist].rearrange("p o t -> p (o t)"),
                             ext[:, SEQ:SEQ + hist]).then_inc(saved, 1)
            pool.tensor_copy(new_state[:, bass.ds(c, 1), hist:].rearrange("p o (b t) -> p (o b) t", b=NB),
                             sample_part(ext, hist)[:, :, NS:]).then_inc(saved, 1)

        def qkv_phase(ph):
            W, n, hist = 4, QKV_T, 3
            scr = Arena()
            ext = [scr(ext_cols(W)) for _ in range(SLOTS)]
            y = [scr(ext_cols(W)) for _ in range(SLOTS)]
            state, new_state = scr(n, NB * hist), scr(n, (NB + 1) * hist)
            cw = scr(n, W)
            chunk_done, filled, tap_done, conv_done, silu_done, hist_in, saved, st_in, pads = (
                sem(f"qkv_{x}") for x in ("chunk_done", "ext_filled", "tap_done", "conv_done", "silu_done",
                                          "hist_in", "saved", "state_in", "pads_zero"))
            with nc.Block() as block:
                @block.sync
                def _(sync):
                    sync.dma_start(state, I["st_dn"]).then_inc(st_in, 16)
                    sync.dma_start(cw, I["cw_dn"]).then_inc(st_in, 16)
                    load_weights(sync, ph, chunk_done)
                    sync.wait_ge(saved, 8 + 2 * n)
                    store(sync, O["dn_conv"], new_state)

                @block.tensor
                def _(pe):
                    with pe.Fori(0, n // SLOTS) as i:
                        for s in range(SLOTS):
                            g = i * SLOTS + s
                            pe.wait_ge(w_loaded[s], (i + uses[ph] + 1) * 16)
                            pe.wait_ge(filled, g * 3 + 3)
                            product(pe, BANK[s % 2 * 2:], s, x_half(X), range(8), True, True).then_inc(chunk_done, 1)

                @block.scalar
                def _(act):
                    act.sem_inc(filled, 6)
                    act.sem_inc(silu_done, 8)
                    with act.Fori(0, n // SLOTS) as i:
                        for s in range(SLOTS):
                            g = i * SLOTS + s
                            act.wait_ge(chunk_done, g + 1)
                            act.wait_ge(conv_done, g + 1)
                            act.wait_ge(saved, g * 2 + 2)
                            fill_ext(act, BANK[s % 2 * 2:], ext[s], hist, filled)
                        for s in range(SLOTS):
                            g = i * SLOTS + s
                            act.wait_ge(conv_done, g + 5)
                            out = BIG[:, bass.ds(g, 1), :].rearrange("p o t -> p (o t)")
                            act.activation(out[:, 0:SEQ], y[s][:, 0:SEQ], ACT.Silu).then_inc(silu_done, 1)
                            act.activation(out[:, SEQ:TOK].rearrange("p (b t) -> p b t", b=NB),
                                           y[s][:, SEQ + hist:SEQ + hist + NB * (hist + NS)]
                                           .rearrange("p (b t) -> p b t", b=NB)[:, :, 0:NS],
                                           ACT.Silu).then_inc(silu_done, 1)

                @block.gpsimd
                def _(pool):
                    for s in range(SLOTS):
                        pool.memset(ext[s][:, 0:hist], 0.0).then_inc(pads, 1)
                    pool.sem_inc(saved, 8)
                    pool.wait_ge(st_in, 32)
                    with pool.Fori(0, n // SLOTS) as i:
                        for s in range(SLOTS):
                            pool.wait_ge(conv_done, i * SLOTS + s + 1)
                            pool.wait_ge(saved, (i * SLOTS + s) * 2 + 2)
                            history_in(pool, ext[s], state, i * SLOTS + s, hist, hist_in)
                        for s in range(SLOTS):
                            pool.wait_ge(filled, (i * SLOTS + s) * 3 + 9)
                            history_out(pool, ext[s], new_state, i * SLOTS + s, hist, saved)

                @block.vector
                def _(dve):
                    dve.sem_inc(conv_done, 4)
                    dve.wait_ge(st_in, 32)
                    dve.wait_ge(pads, SLOTS)
                    with dve.Fori(0, n // SLOTS) as i:
                        for s in range(SLOTS):
                            g = i * SLOTS + s
                            dve.wait_ge(filled, g * 3 + 9)
                            dve.wait_ge(hist_in, g + 1)
                            dve.wait_ge(silu_done, g * 2 + 2)
                            tap_run(dve, ext[s], y[s],
                                    lambda j: cw[:, bass.ds(g, 1), j:j + 1].rearrange("p o t -> p (o t)"),
                                    W, g, tap_done, conv_done)

        def gate_phase(ph):
            scr = Arena()
            wba = scr(DT, 40)
            bg = scr(TOK)
            t1, t2, keep = scr(TOK), scr(TOK), scr(TOK)
            sel = scr(H, P)
            chunk_done, z_done, w_in, ba_ready, step, logit, tr_done, tr_out, gc_b, gc_out = (
                sem(f"gate_{x}") for x in ("chunk_done", "z_done", "w_in", "ba_ready", "dve_step", "act_step",
                                           "tr_done", "tr_out", "gc_b", "gc_out"))
            gate = slice(A_ROW, A_ROW + H)
            with nc.Block() as block:
                @block.sync
                def _(sync):
                    sync.dma_start(wba, I["w_ba"]).then_inc(w_in, 16)
                    sync.dma_start(sel[gate], I["select_head"]).then_inc(w_in, 16)
                    sync.dma_start(keep[gate], I["keep"]).then_inc(w_in, 16)
                    load_weights(sync, ph, chunk_done)

                @block.tensor
                def _(pe):
                    pe.wait_ge(w_in, 48)
                    for k in range(DT):
                        for half in range(2):
                            last = pe.matmul(BANK[4 + half][0:40, 0:HALF], wba[:, k, :], x_half(X)(k, half),
                                             start=k == 0, stop=k == DT - 1)
                    last.then_inc(ba_ready, 1)
                    with pe.Fori(0, H // SLOTS) as i:
                        for s in range(SLOTS):
                            g = i * SLOTS + s
                            pe.wait_ge(w_loaded[s], (i + uses[ph] + 1) * 16)
                            pe.wait_ge(z_done, g + 1)
                            product(pe, BANK[s % 2 * 2:], s, x_half(X), range(8), True, True).then_inc(chunk_done, 1)
                    pe.wait_ge(step, 7)
                    pe.wait_ge(logit, 6)
                    for c in range(NCH + 1):
                        w = min(CH, TOK - c * CH)
                        last = pe.transpose(BANK[6][0:w, c * 40:c * 40 + 40], bg[0:40, c * CH:c * CH + w],
                                            IDENT[0:40, 0:40])
                    last.then_inc(tr_done, 1)
                    for h in range(H):
                        b = 0 if h % 2 == 0 else 2
                        pe.wait_ge(z_done, 2 + H)
                        if h >= 2:
                            pe.wait_ge(gc_out, h - 1)
                        for half in range(2):
                            last = pe.matmul(BANK[b + half][:, 0:HALF], sel[gate, h, :],
                                             bg[gate, half * HALF:(half + 1) * HALF], start=True, stop=True)
                        last.then_inc(gc_b, 1)

                @block.scalar
                def _(act):
                    act.sem_inc(z_done, 2)
                    act.activation(neg_ea, a_log, ACT.Exp).then_inc(logit, 1)
                    act.wait_ge(ba_ready, 1)
                    act.wait_ge(step, 1)
                    for half in range(2):
                        cols = slice(half * HALF, (half + 1) * HALF)
                        act.activation(bg[0:H, cols], BANK[4 + half][0:H, 0:HALF], ACT.Sigmoid).then_inc(logit, 1)
                    for half in range(2):
                        cols = slice(half * HALF, (half + 1) * HALF)
                        act.activation(t1[gate, cols], BANK[4 + half][gate, 0:HALF], ACT.Identity,
                                       bias=dt_bias).then_inc(logit, 1)
                    act.wait_ge(step, 3)
                    act.activation(t2[gate], t2[gate], ACT.Exp, scale=-1.0).then_inc(logit, 1)
                    act.wait_ge(logit, 6)
                    act.activation(t2[gate], t2[gate], ACT.Ln, bias=1.0).then_inc(logit, 1)
                    with act.Fori(0, H // SLOTS) as i:
                        for s in range(SLOTS):
                            g = i * SLOTS + s
                            act.wait_ge(chunk_done, g + 1)
                            for half in range(2):
                                last = act.activation(Z[:, bass.ds(g, 1), half * HALF:(half + 1) * HALF]
                                                      .rearrange("p o t -> p (o t)"),
                                                      BANK[s % 2 * 2 + half][:, 0:HALF], ACT.Silu)
                            last.then_inc(z_done, 1)
                    for h in range(H):
                        b = 0 if h % 2 == 0 else 2
                        act.wait_ge(gc_b, h + 1)
                        for half in range(2):
                            last = act.activation(Y[:, h, half * HALF:(half + 1) * HALF],
                                                  BANK[b + half][:, 0:HALF], ACT.Copy)
                        last.then_inc(gc_out, 1)

                @block.vector
                def _(dve):
                    dve.memset(bg[:], 0.0).then_inc(step, 1)
                    dve.wait_ge(logit, 1)
                    dve.tensor_scalar(neg_ea, neg_ea, -1.0, None, ALU.mult).then_inc(step, 1)
                    dve.wait_ge(logit, 5)
                    dve.scalar_tensor_tensor(out=t2[gate], in0=t1[gate], scalar=-1.0, in1=t1[gate],
                                             op0=ALU.mult, op1=ALU.max).then_inc(step, 1)
                    dve.wait_ge(logit, 7)
                    dve.wait_ge(step, 3)
                    dve.scalar_tensor_tensor(out=t1[gate], in0=t1[gate], scalar=0.0, in1=t2[gate],
                                             op0=ALU.max, op1=ALU.add).then_inc(step, 1)
                    dve.wait_ge(step, 4)
                    dve.tensor_scalar(t1[gate], t1[gate], neg_ea, None, ALU.mult).then_inc(step, 1)
                    dve.wait_ge(step, 5)
                    dve.wait_ge(w_in, 48)
                    dve.tensor_tensor_scan(bg[gate], keep[gate], t1[gate], 0.0, ALU.mult, ALU.add).then_inc(step, 1)
                    dve.wait_ge(step, 6)
                    dve.sem_inc(step, 1)
                    dve.wait_ge(tr_done, 1)
                    for n, (rows, cs, ntok) in enumerate(((slice(0, P), slice(0, NCH), NCH),
                                                          (slice(0, SAMP), slice(NCH, NCH + 1), 1))):
                        by_tok = BANK[6][rows, cs.start * 40:cs.stop * 40].rearrange("p (c n) -> p c n", n=40)
                        dve.tensor_copy(TOKS[rows, cs, 0, :], by_tok[:, :, A_ROW:A_ROW + H]).then_inc(step, 1)
                        dve.tensor_copy(TOKS[rows, cs, 1, :], by_tok[:, :, 0:H]).then_inc(step, 1)
                    dve.wait_ge(step, 11)
                    dve.tensor_scalar(TOKS[:, :, 3, :], TOKS[:, :, 1, :], -1.0, None, ALU.mult).then_inc(step, 1)

            e_done, b_done = sem("tok_exp"), sem("tok_mul")
            with nc.Block() as block:
                @block.scalar
                def _(act):
                    act.activation(TOKS[:, :, 2, :], TOKS[:, :, 0, :], ACT.Exp).then_inc(e_done, 1)

                @block.vector
                def _(dve):
                    dve.wait_ge(e_done, 1)
                    dve.tensor_tensor(TOKS[:, :, 2, :], TOKS[:, :, 2, :], TOKS[:, :, 3, :],
                                      ALU.mult).then_inc(b_done, 1)

        def feature_norm(name, n, tile, ones, scale_eps, finish):
            scr = Arena()
            sq = [scr(TOK) for _ in range(4)]
            rs = [scr(TOK) for _ in range(4)]
            sq_done, mm_done, std_done, rec_done, fin_done = (
                phase_sems("norm", ("sq_done", "sum_done", "std_done", "rec_done", "fin_done")))
            with nc.Block() as block:
                @block.gpsimd
                def _(pool):
                    for m in range(n):
                        if m >= 4:
                            pool.wait_ge(mm_done, m - 3)
                        pool.tensor_tensor(sq[m % 4], tile(m), tile(m), ALU.mult).then_inc(sq_done, 1)

                @block.tensor
                def _(pe):
                    for m in range(n):
                        pe.wait_ge(sq_done, m + 1)
                        if m >= 4:
                            pe.wait_ge(std_done, 2 * (m - 3))
                        for half in range(2):
                            last = pe.matmul(BANK[m % 4 * 2 + half][:, 0:HALF], ones[:],
                                             sq[m % 4][:, half * HALF:(half + 1) * HALF], start=True, stop=True)
                        last.then_inc(mm_done, 1)

                @block.scalar
                def _(act):
                    for m in range(n):
                        act.wait_ge(mm_done, m + 1)
                        if m >= 4:
                            act.wait_ge(fin_done, m - 3)
                        scale, eps = scale_eps(m)
                        for half in range(2):
                            act.activation(rs[m % 4][:, half * HALF:(half + 1) * HALF],
                                           BANK[m % 4 * 2 + half][:, 0:HALF], ACT.Sqrt, bias=eps,
                                           scale=scale).then_inc(std_done, 1)

                @block.vector
                def _(dve):
                    for m in range(n):
                        dve.wait_ge(std_done, 2 * m + 2)
                        dve.reciprocal(rs[m % 4], rs[m % 4]).then_inc(rec_done, 1)
                        dve.wait_ge(rec_done, m + 1)
                        finish(dve, m, rs[m % 4], fin_done)

        def delta_prompt():
            scr = Arena()
            S = scr(H, P)
            st = scr(H, 3, CH)
            dec = scr(H, CH)
            ka = scr(H, 2, CH)
            T = scr(H, 2, CH)
            Ys = scr(H, CH)
            ktok, vtok = scr(H, P), scr(H, P)
            vnew, qe = scr(H, P), scr(H, CH)
            sc = scr(4, H)
            eg = scr(H, CH)
            names = ("stage", "scal", "arg", "dec", "kq", "att", "tr", "tok", "eg", "qe", "tinit", "y", "ymask",
                     "d", "t", "ks", "r", "v", "vn", "os", "o_out", "s_out")
            q = {x: sem(f"dp_{x}") for x in names}
            with nc.Block() as block:
                @block.vector
                def _(dve):
                    dve.memset(S, 0.0).then_inc(q["s_out"], H)
                    dve.sem_inc(q["os"], H)
                    with dve.Fori(0, NCH) as c:
                        dve.wait_ge(q["os"], (c + 1) * H)
                        dve.wait_ge(q["s_out"], (c + 1) * H)
                        dve.tensor_copy(st.rearrange("p a b c -> p (a b) c"),
                                        BIG[:, :, bass.ds(c * CH, CH)]).then_inc(q["stage"], 1)
                        dve.tensor_copy(sc, TOKS[:, bass.ds(c, 1), :, :].rearrange("p o a b -> p (o a) b")
                                        ).then_inc(q["scal"], 1)
                        dve.wait_ge(q["scal"], c + 1)
                        for h in range(H):
                            dve.scalar_tensor_tensor(out=dec[:, h, :], in0=Y[:, h, bass.ds(c * CH, CH)],
                                                     scalar=sc[:, 0, h:h + 1], in1=MASKT[:], op0=ALU.subtract,
                                                     op1=ALU.add).then_inc(q["arg"], 1)
                        dve.tensor_copy(T.rearrange("p a b c -> p (a b) c"),
                                        IDENT[:].unsqueeze(1).to_broadcast([P, 2 * H, CH])).then_inc(q["tinit"], 1)
                        dve.wait_ge(q["eg"], c + 1)
                        dve.wait_ge(q["stage"], c + 1)
                        dve.tensor_tensor(qe, st[:, :, 1, :], eg, ALU.mult).then_inc(q["qe"], 1)
                        for h in range(H):
                            dve.wait_ge(q["dec"], c * H + h + 1)
                            dve.wait_ge(q["kq"], c * H + h + 1)
                            dve.tensor_tensor(ka[:, h], BANK[h][:, 256:512].rearrange("p (a b) -> p a b", a=2),
                                              dec[:, h, :].unsqueeze(1).to_broadcast([P, 2, CH]),
                                              ALU.mult).then_inc(q["att"], 1)
                        dve.wait_ge(q["tinit"], c + 1)
                        for lv in range(LEVELS):
                            for h in range(H):
                                dve.wait_ge(q["y"], c * (LEVELS * H) + lv * H + h + 1)
                                dve.scalar_tensor_tensor(out=Ys[:, h, :], in0=BANK[h][:, 0:CH],
                                                         scalar=sc[:, 1, h:h + 1], in1=MASKL[:, lv, :],
                                                         op0=ALU.mult, op1=ALU.mult).then_inc(q["ymask"], 1)
                            for h in range(H):
                                dve.wait_ge(q["d"], c * (LEVELS * H) + lv * H + h + 1)
                                if lv:
                                    dve.wait_ge(q["t"], c * (LEVELS * H) + (lv - 1) * H + h + 1)
                                dve.tensor_tensor(T[:, h], T[:, h],
                                                  BANK[h][:, 256:512].rearrange("p (a b) -> p a b", a=2),
                                                  ALU.subtract).then_inc(q["t"], 1)
                        for h in range(H):
                            dve.wait_ge(q["ks"], c * H + h + 1)
                            dve.wait_ge(q["tok"], c * (2 * H) + 2 * h + 2)
                            dve.scalar_tensor_tensor(out=Ys[:, h, :], in0=BANK[h][:, 0:P],
                                                     scalar=sc[:, 2, h:h + 1], in1=vtok[:, h, :],
                                                     op0=ALU.mult, op1=ALU.add).then_inc(q["r"], 1)
                        for h in range(H):
                            dve.wait_ge(q["os"], c * H + H + h + 1)
                            dve.tensor_copy(BIG[:, 3 * h + 1, bass.ds(c * CH, CH)],
                                            BANK[h][:, 256:384]).then_inc(q["o_out"], 1)
                            dve.scalar_tensor_tensor(out=S[:, h, :], in0=S[:, h, :], scalar=eg[:, h, CH - 1:CH],
                                                     in1=BANK[h][:, 384:512], op0=ALU.mult,
                                                     op1=ALU.add).then_inc(q["s_out"], 1)

                @block.scalar
                def _(act):
                    with act.Fori(0, NCH) as c:
                        act.wait_ge(q["s_out"], (c + 1) * H)
                        act.activation(eg, Y[:, :, bass.ds(c * CH, CH)], ACT.Exp).then_inc(q["eg"], 1)
                        for h in range(H):
                            act.wait_ge(q["arg"], c * H + h + 1)
                            act.activation(dec[:, h, :], dec[:, h, :], ACT.Exp).then_inc(q["dec"], 1)
                        for h in range(H):
                            act.wait_ge(q["tr"], c * H + h + 1)
                            act.activation(ktok[:, h, :], BANK[h][:, 0:P], ACT.Copy).then_inc(q["tok"], 1)
                            act.activation(vtok[:, h, :], BANK[h][:, P:2 * P], ACT.Copy,
                                           scale=sc[:, 1, h:h + 1]).then_inc(q["tok"], 1)
                        for h in range(H):
                            act.wait_ge(q["v"], c * H + h + 1)
                            act.activation(vnew[:, h, :], BANK[h][:, 128:256], ACT.Copy).then_inc(q["vn"], 1)
                            act.activation(vtok[:, h, :], BANK[h][:, 128:256], ACT.Copy,
                                           scale=dec[:, h, CH - 1:CH]).then_inc(q["vn"], 1)

                @block.tensor
                def _(pe):
                    with pe.Fori(0, NCH) as c:
                        pe.wait_ge(q["stage"], c + 1)
                        pe.wait_ge(q["s_out"], (c + 1) * H)
                        for h in range(H):
                            pe.matmul(BANK[h][:, 256:512], st[:, h, 0, :], st[:, h, 0:2, :], start=True,
                                      stop=True).then_inc(q["kq"], 1)
                        for h in range(H):
                            pe.wait_ge(q["att"], c * H + h + 1)
                            pe.transpose(BANK[h][:, 0:P], st[:, h, 0, :], IDENT[:])
                            pe.transpose(BANK[h][:, P:2 * P], st[:, h, 2, :], IDENT[:]).then_inc(q["tr"], 1)
                        pe.wait_ge(q["tinit"], c + 1)
                        for lv in range(LEVELS):
                            for h in range(H):
                                if lv:
                                    pe.wait_ge(q["t"], c * (LEVELS * H) + (lv - 1) * H + h + 1)
                                else:
                                    pe.wait_ge(q["tok"], c * (2 * H) + 2 * h + 2)
                                pe.matmul(BANK[h][:, 0:CH], ka[:, h, 0, :], T[:, h, 0, :], start=True,
                                          stop=True).then_inc(q["y"], 1)
                            for h in range(H):
                                pe.wait_ge(q["ymask"], c * (LEVELS * H) + lv * H + h + 1)
                                pe.matmul(BANK[h][:, 256:384], T[:, h, 1, :], Ys[:, h, :], start=True, stop=True)
                                pe.matmul(BANK[h][:, 384:512], Ys[:, h, :], T[:, h, 1, :], start=True,
                                          stop=True).then_inc(q["d"], 1)
                        for h in range(H):
                            pe.wait_ge(q["t"], c * (LEVELS * H) + (LEVELS - 1) * H + h + 1)
                            pe.matmul(BANK[h][:, 0:P], st[:, h, 0, :], S[:, h, :], start=True,
                                      stop=True).then_inc(q["ks"], 1)
                        for h in range(H):
                            pe.wait_ge(q["r"], c * H + h + 1)
                            pe.matmul(BANK[h][:, 128:256], T[:, h, 1, :], Ys[:, h, :], start=True,
                                      stop=True).then_inc(q["v"], 1)
                        pe.wait_ge(q["qe"], c + 1)
                        for h in range(H):
                            pe.wait_ge(q["vn"], c * (2 * H) + 2 * h + 2)
                            pe.matmul(BANK[h][:, 256:384], S[:, h, :], qe[:, h, :], start=True, stop=False)
                            pe.matmul(BANK[h][:, 256:384], vnew[:, h, :], ka[:, h, 1, :], start=False, stop=True)
                            pe.matmul(BANK[h][:, 384:512], ktok[:, h, :], vtok[:, h, :], start=True,
                                      stop=True).then_inc(q["os"], 1)

                @block.sync
                def _(sync):
                    sync.wait_ge(q["s_out"], (NCH + 1) * H)
                    store(sync, O["dn_S_prompt"], S)

        def delta_sample():
            scr = Arena()
            RS = 4
            S0 = scr(RS, NB, P)
            dec = scr(H, SAMP)
            ka = scr(H, 2, SAMP)
            T = scr(H, 2, SAMP)
            Ys = scr(H, SAMP)
            ktok, vtok, R, vnew = scr(H, P), scr(H, P), scr(H, P), scr(H, P)
            ksq = scr(H, 2, SAMP)
            vb = scr(2, NB, P)
            eg = scr(H, SAMP)
            names = ("in", "arg", "dec", "kq", "att", "tr", "tok", "eg", "tinit", "y", "ymask", "d", "t", "ks",
                     "ksq", "rt", "r", "v", "vn", "o", "o_out", "vb", "sdec", "su", "s_out", "saved")
            q = {x: sem(f"ds_{x}") for x in names}
            sin = [sem(f"ds_state_in{r}") for r in range(RS)]
            A = slice(0, SAMP)
            last_tok = slice(NS - 1, SAMP, NS)

            def smp(r):
                return BIG[:, r, SEQ:TOK]

            with nc.Block() as block:
                @block.sync
                def _(sync):
                    for h in range(H):
                        if h >= RS:
                            sync.wait_ge(q["saved"], 16 * (h - RS + 1))
                        sync.dma_start(S0[:, h % RS], I["st_S"][h]).then_inc(sin[h % RS], 16)

                @block.gpsimd
                def _(pool):
                    for h in range(H):
                        pool.wait_ge(q["s_out"], 2 * h + 2)
                        pool.dma_start(O["dn_S_sample"][h], S0[:, h % RS]).then_inc(q["saved"], 16)
                        pool.wait_ge(q["saved"], 16 * (h + 1))

                @block.scalar
                def _(act):
                    act.activation(eg, Y[:, :, SEQ:TOK], ACT.Exp).then_inc(q["eg"], 1)
                    for h in range(H):
                        act.wait_ge(q["arg"], h + 1)
                        act.activation(dec[A, h, :], dec[A, h, :], ACT.Exp).then_inc(q["dec"], 1)
                    for h in range(H):
                        act.wait_ge(q["tr"], h + 1)
                        act.activation(ktok[A, h, :], BANK[h][A, 0:P], ACT.Copy).then_inc(q["tok"], 1)
                        act.activation(vtok[A, h, :], BANK[h][A, P:2 * P], ACT.Copy,
                                       scale=TOKS[A, NCH, 1, h:h + 1]).then_inc(q["tok"], 1)
                    for h in range(H):
                        act.wait_ge(q["v"], h + 1)
                        act.activation(vnew[A, h, :], BANK[h][A, 256:384], ACT.Copy).then_inc(q["vn"], 1)

                @block.vector
                def _(dve):
                    for h in range(H):
                        dve.scalar_tensor_tensor(out=dec[A, h, :], in0=Y[A, h, SEQ:TOK],
                                                 scalar=TOKS[A, NCH, 0, h:h + 1], in1=MASKS[A], op0=ALU.subtract,
                                                 op1=ALU.add).then_inc(q["arg"], 1)
                    dve.tensor_copy(T[A].rearrange("p a b c -> p (a b) c"),
                                    IDENT[A, A].unsqueeze(1).to_broadcast([SAMP, 2 * H, SAMP])
                                    ).then_inc(q["tinit"], 1)
                    for h in range(H):
                        dve.wait_ge(q["dec"], h + 1)
                        dve.wait_ge(q["kq"], h + 1)
                        dve.tensor_tensor(ka[A, h], BANK[h][A, 256:384].rearrange("p (a b) -> p a b", a=2),
                                          dec[A, h, :].unsqueeze(1).to_broadcast([SAMP, 2, SAMP]),
                                          ALU.mult).then_inc(q["att"], 1)
                    dve.wait_ge(q["tinit"], 1)
                    for lv in range(SAMP_LEVELS):
                        for h in range(H):
                            dve.wait_ge(q["y"], lv * H + h + 1)
                            dve.scalar_tensor_tensor(out=Ys[A, h, :], in0=BANK[h][A, 0:SAMP],
                                                     scalar=TOKS[A, NCH, 1, h:h + 1], in1=MASKL[A, lv, A],
                                                     op0=ALU.mult, op1=ALU.mult).then_inc(q["ymask"], 1)
                        for h in range(H):
                            dve.wait_ge(q["d"], lv * H + h + 1)
                            if lv:
                                dve.wait_ge(q["t"], (lv - 1) * H + h + 1)
                            dve.tensor_tensor(T[A, h], T[A, h],
                                              BANK[h][A, 256:384].rearrange("p (a b) -> p a b", a=2),
                                              ALU.subtract).then_inc(q["t"], 1)
                    dve.wait_ge(q["eg"], 1)
                    for h in range(H):
                        dve.wait_ge(q["ks"], h + 1)
                        dve.tensor_tensor(ksq[:, h].rearrange("p r (b t) -> p b r t", b=NB),
                                          BANK[h][:, 0:128].rearrange("p (b r t) -> p b r t", b=NB, r=2),
                                          eg[:, h, :].rearrange("p (b t) -> p b t", b=NB).unsqueeze(2)
                                          .to_broadcast([P, NB, 2, NS]), ALU.mult).then_inc(q["ksq"], 1)
                        dve.tensor_tensor(S0[:, h % RS], S0[:, h % RS],
                                          eg[:, h, last_tok].unsqueeze(2).to_broadcast([P, NB, P]),
                                          ALU.mult).then_inc(q["sdec"], 1)
                        dve.wait_ge(q["rt"], h + 1)
                        dve.wait_ge(q["tok"], 2 * h + 2)
                        dve.scalar_tensor_tensor(out=R[A, h, :], in0=BANK[h][A, 128:256],
                                                 scalar=TOKS[A, NCH, 3, h:h + 1], in1=vtok[A, h, :], op0=ALU.mult,
                                                 op1=ALU.add).then_inc(q["r"], 1)
                        dve.wait_ge(q["vn"], h + 1)
                        if h >= 2:
                            dve.wait_ge(q["su"], 2 * (h - 1))
                        dve.tensor_tensor(vb[A, h % 2], vnew[A, h, :].unsqueeze(1).to_broadcast([SAMP, NB, P]),
                                          dec[A, h, last_tok].unsqueeze(2).to_broadcast([SAMP, NB, P]),
                                          ALU.mult).then_inc(q["vb"], 1)
                        dve.wait_ge(q["o"], h + 1)
                        dve.wait_ge(q["ksq"], h + 1)
                        dve.tensor_tensor(smp(3 * h + 1), ksq[:, h, 1, :], BANK[h][:, 384:448],
                                          ALU.add).then_inc(q["o_out"], 1)
                        for r in range(2):
                            dve.wait_ge(q["su"], 2 * h + r + 1)
                            dve.wait_ge(q["sdec"], h + 1)
                            part = S0[:, h % RS, 4 * r:4 * r + 4, :]
                            dve.tensor_tensor(part, part, BANK[h][:, :].rearrange("p (b n) -> p b n", b=4),
                                              ALU.add).then_inc(q["s_out"], 1)

                @block.tensor
                def _(pe):
                    for h in range(H):
                        pe.matmul(BANK[h][A, 256:384], smp(3 * h), BIG[:, 3 * h:3 * h + 2, SEQ:TOK], start=True,
                                  stop=True).then_inc(q["kq"], 1)
                    for h in range(H):
                        pe.wait_ge(q["att"], h + 1)
                        pe.transpose(BANK[h][A, 0:P], smp(3 * h), IDENT[:])
                        pe.transpose(BANK[h][A, P:2 * P], smp(3 * h + 2), IDENT[:]).then_inc(q["tr"], 1)
                    pe.wait_ge(q["tinit"], 1)
                    for lv in range(SAMP_LEVELS):
                        for h in range(H):
                            if lv:
                                pe.wait_ge(q["t"], (lv - 1) * H + h + 1)
                            else:
                                pe.wait_ge(q["tok"], 2 * h + 2)
                            pe.matmul(BANK[h][A, 0:SAMP], ka[A, h, 0, :], T[A, h, 0, :], start=True,
                                      stop=True).then_inc(q["y"], 1)
                        for h in range(H):
                            pe.wait_ge(q["ymask"], lv * H + h + 1)
                            pe.matmul(BANK[h][A, 256:320], T[A, h, 1, :], Ys[A, h, :], start=True, stop=True)
                            pe.matmul(BANK[h][A, 320:384], Ys[A, h, :], T[A, h, 1, :], start=True,
                                      stop=True).then_inc(q["d"], 1)
                    for h in range(H):
                        pe.wait_ge(q["t"], (SAMP_LEVELS - 1) * H + h + 1)
                        pe.wait_ge(sin[h % RS], 16 * (h // RS + 1))
                        for b in range(NB):
                            last = pe.matmul(BANK[h][:, 16 * b:16 * b + 16], S0[:, h % RS, b, :],
                                             BIG[:, 3 * h:3 * h + 2, SEQ + NS * b:SEQ + NS * (b + 1)], start=True,
                                             stop=True)
                        last.then_inc(q["ks"], 1)
                        pe.wait_ge(q["ksq"], h + 1)
                        pe.transpose(BANK[h][A, 128:256], ksq[:, h, 0, :], IDENT[:]).then_inc(q["rt"], 1)
                        pe.wait_ge(q["r"], h + 1)
                        pe.matmul(BANK[h][A, 256:384], T[A, h, 1, :], R[A, h, :], start=True,
                                  stop=True).then_inc(q["v"], 1)
                        pe.wait_ge(q["vn"], h + 1)
                        pe.matmul(BANK[h][:, 384:448], vnew[A, h, :], ka[A, h, 1, :], start=True,
                                  stop=True).then_inc(q["o"], 1)
                        pe.wait_ge(q["vb"], h + 1)
                        pe.wait_ge(q["o_out"], h + 1)
                        for r in range(2):
                            if r:
                                pe.wait_ge(q["s_out"], 2 * h + 1)
                            pe.matmul(BANK[h][:, :], ktok[A, h, :],
                                      vb[A, h % 2, 4 * r:4 * r + 4, :], start=True, stop=True).then_inc(q["su"], 1)

        def residual_phase(name, ph, rhs, res, chunks_per_tile=1):
            n = DT * chunks_per_tile
            kt = streams[ph][2]
            chunk_done, added = phase_sems("res", ("chunk_done", "added"))
            with nc.Block() as block:
                @block.sync
                def _(sync):
                    load_weights(sync, ph, chunk_done)

                @block.tensor
                def _(pe):
                    with pe.Fori(0, n // SLOTS) as i:
                        for s in range(SLOTS):
                            part, tile = s % chunks_per_tile, s // chunks_per_tile
                            pe.wait_ge(w_loaded[s], (i + uses[ph] + 1) * 16)
                            if part == 0:
                                pe.wait_ge(added, i * (2 * SLOTS // chunks_per_tile) + 2 * tile + 2)
                            product(pe, BANK[tile % 2 * 2:], s, rhs, range(part * kt, part * kt + kt),
                                    part == 0, part == chunks_per_tile - 1).then_inc(chunk_done, 1)

                @block.vector
                def _(dve):
                    tiles = SLOTS // chunks_per_tile
                    dve.sem_inc(added, 4)
                    with dve.Fori(0, n // SLOTS) as i:
                        for t in range(tiles):
                            dve.wait_ge(chunk_done, i * SLOTS + (t + 1) * chunks_per_tile)
                            m = i * tiles + t
                            for half in range(2):
                                cols = slice(half * HALF, (half + 1) * HALF)
                                dve.scalar_tensor_tensor(
                                    out=Y[:, bass.ds(m, 1), cols].rearrange("p o t -> p (o t)"),
                                    in0=res[:, bass.ds(m, 1), cols].rearrange("p o t -> p (o t)"), scalar=ALPHA,
                                    in1=BANK[t % 2 * 2 + half][:, 0:HALF], op0=ALU.mult,
                                    op1=ALU.add).then_inc(added, 1)

        def layer_norm(name, which, out):
            scr = Arena()
            mu, rs = scr(TOK), scr(TOK)
            sq = [scr(TOK) for _ in range(DT)]
            mean_done, mu_done, cen, sqd, var_done, std_done, rec, nrm, aff = (
                phase_sems("ln", ("mean_done", "mu_done", "centred", "squared", "var_done", "std_done", "rec",
                                  "normed", "affine")))
            with nc.Block() as block:
                @block.tensor
                def _(pe):
                    for half in range(2):
                        for k in range(DT):
                            last = pe.matmul(BANK[half][:, 0:HALF], ONES[:], x_half(Y)(k, half), start=k == 0,
                                             stop=k == DT - 1)
                        last.then_inc(mean_done, 1)
                    for k in range(DT):
                        pe.wait_ge(sqd, k + 1)
                        for half in range(2):
                            last = pe.matmul(BANK[2 + half][:, 0:HALF], ONES[:], sq[k][:, half * HALF:(half + 1) * HALF],
                                             start=k == 0, stop=k == DT - 1)
                    last.then_inc(var_done, 1)

                @block.scalar
                def _(act):
                    for half in range(2):
                        act.wait_ge(mean_done, half + 1)
                        act.activation(mu[:, half * HALF:(half + 1) * HALF], BANK[half][:, 0:HALF], ACT.Copy,
                                       scale=1.0 / D).then_inc(mu_done, 1)
                    for k in range(DT):
                        act.wait_ge(cen, k + 1)
                        act.activation(sq[k], Y[:, k, :], ACT.Square).then_inc(sqd, 1)
                    act.wait_ge(var_done, 1)
                    for half in range(2):
                        act.activation(rs[:, half * HALF:(half + 1) * HALF], BANK[2 + half][:, 0:HALF], ACT.Sqrt,
                                       bias=eps_ln, scale=1.0 / D).then_inc(std_done, 1)
                    for k in range(DT):
                        act.wait_ge(nrm, k + 1)
                        act.activation(out[:, k, :], Y[:, k, :], ACT.Identity, bias=lnp[:, which + 1, k:k + 1],
                                       scale=lnp[:, which, k:k + 1]).then_inc(aff, 1)

                @block.vector
                def _(dve):
                    dve.wait_ge(mu_done, 2)
                    for k in range(DT):
                        dve.tensor_tensor(Y[:, k, :], Y[:, k, :], mu, ALU.subtract).then_inc(cen, 1)
                    dve.wait_ge(std_done, 2)
                    dve.reciprocal(rs, rs).then_inc(rec, 1)
                    dve.wait_ge(rec, 1)
                    for k in range(DT):
                        dve.wait_ge(sqd, k + 1)
                        dve.wait_ge(cen, k + 1)
                        dve.tensor_tensor(Y[:, k, :], Y[:, k, :], rs, ALU.mult).then_inc(nrm, 1)

        def ffn_up(name, ph, x, layer):
            W, n, hist = 3, 2 * FT, 2
            scr = Arena()
            ext = [scr(ext_cols(W)) for _ in range(SLOTS)]
            y = [scr(ext_cols(W)) for _ in range(SLOTS)]
            state, new_state = scr(n, NB * hist), scr(n, (NB + 1) * hist)
            cw = scr(n, W)
            chunk_done, filled, tap_done, conv_done, silu_done, gated, hist_in, saved, st_in, pads = (
                phase_sems("up", ("chunk_done", "ext_filled", "tap_done", "conv_done", "silu_done",
                                  "gated", "hist_in", "saved", "state_in", "pads_zero")))
            cols = SEQ + hist + NB * (hist + NS)
            with nc.Block() as block:
                @block.sync
                def _(sync):
                    sync.dma_start(state, I[f"st_ffn{layer}"]).then_inc(st_in, 16)
                    sync.dma_start(cw, I[f"cw_ffn{layer}"]).then_inc(st_in, 16)
                    load_weights(sync, ph, chunk_done)
                    sync.wait_ge(saved, 8 + 2 * n)
                    store(sync, O[f"ffn_conv{layer}"], new_state)

                @block.tensor
                def _(pe):
                    with pe.Fori(0, n // SLOTS) as i:
                        for s in range(SLOTS):
                            g = i * SLOTS + s
                            pe.wait_ge(w_loaded[s], (i + uses[ph] + 1) * 16)
                            pe.wait_ge(filled, g * 3 + 3)
                            product(pe, BANK[s % 2 * 2:], s, x_half(x), range(8), True, True).then_inc(chunk_done, 1)

                @block.scalar
                def _(act):
                    act.sem_inc(filled, 6)
                    with act.Fori(0, n // SLOTS) as i:
                        for s in range(SLOTS):
                            g = i * SLOTS + s
                            act.wait_ge(chunk_done, g + 1)
                            act.wait_ge(conv_done, g + 1)
                            act.wait_ge(saved, g * 2 + 2)
                            fill_ext(act, BANK[s % 2 * 2:], ext[s], hist, filled)
                            if s % 2:
                                act.wait_ge(conv_done, g + 5)
                                act.activation(y[s][:, 0:cols - hist], y[s][:, 0:cols - hist],
                                               ACT.Silu).then_inc(silu_done, 1)

                @block.gpsimd
                def _(pool):
                    for s in range(SLOTS):
                        pool.memset(ext[s][:, 0:hist], 0.0).then_inc(pads, 1)
                    pool.sem_inc(saved, 8)
                    pool.wait_ge(st_in, 32)
                    with pool.Fori(0, n // SLOTS) as i:
                        for s in range(SLOTS):
                            pool.wait_ge(conv_done, i * SLOTS + s + 1)
                            pool.wait_ge(saved, (i * SLOTS + s) * 2 + 2)
                            history_in(pool, ext[s], state, i * SLOTS + s, hist, hist_in)
                        for s in range(SLOTS):
                            pool.wait_ge(filled, (i * SLOTS + s) * 3 + 9)
                            history_out(pool, ext[s], new_state, i * SLOTS + s, hist, saved)

                @block.vector
                def _(dve):
                    dve.sem_inc(conv_done, 4)
                    dve.sem_inc(gated, 4)
                    dve.wait_ge(st_in, 32)
                    dve.wait_ge(pads, SLOTS)
                    with dve.Fori(0, n // SLOTS) as i:
                        for pair in range(2):
                            for s in (2 * pair, 2 * pair + 1):
                                g = i * SLOTS + s
                                dve.wait_ge(filled, g * 3 + 9)
                                dve.wait_ge(hist_in, g + 1)
                                dve.wait_ge(gated, i * 4 + 2 * pair + 2)
                                tap_run(dve, ext[s], y[s],
                                        lambda j: cw[:, bass.ds(g, 1), j:j + 1].rearrange("p o t -> p (o t)"),
                                        W, g, tap_done, conv_done)
                            dve.wait_ge(conv_done, i * SLOTS + 2 * pair + 6)
                            dve.wait_ge(silu_done, i * 2 + pair + 1)
                            hid = BIG[:, bass.ds(i * 2 + pair, 1), :].rearrange("p o t -> p (o t)")
                            a, b = y[2 * pair], y[2 * pair + 1]
                            dve.tensor_tensor(hid[:, 0:SEQ], a[:, 0:SEQ], b[:, 0:SEQ], ALU.mult).then_inc(gated, 1)

                            def smp(v):
                                return v[:, SEQ + hist:cols].rearrange("p (b t) -> p b t", b=NB)[:, :, 0:NS]
                            dve.tensor_tensor(hid[:, SEQ:TOK].rearrange("p (b t) -> p b t", b=NB), smp(a), smp(b),
                                              ALU.mult).then_inc(gated, 1)

        def ple_phase(name, ph, x, out, layer):
            scr = Arena()
            pe_in = scr(PLE_T, TOK)
            sg = [scr(TOK) for _ in range(2)]
            chunk_done, sig, prod, added, p_in = (
                phase_sems("ple", ("chunk_done", "sigmoid", "product", "added", "p_in")))
            with nc.Block() as block:
                @block.sync
                def _(sync):
                    sync.dma_start(pe_in, I[f"p{layer}"]).then_inc(p_in, 16)
                    load_weights(sync, ph, chunk_done)

                @block.tensor
                def _(pe):
                    pe.wait_ge(p_in, 16)
                    with pe.Fori(0, DT // SLOTS) as i:
                        for s in range(SLOTS):
                            g = i * SLOTS + s
                            b = s % 2 * 4
                            pe.wait_ge(w_loaded[s], (i + uses[ph] + 1) * 16)
                            pe.wait_ge(sig, g * 2 + 2)
                            pe.wait_ge(prod, g * 2 + 2)
                            product(pe, BANK[b:], s, x_half(x), range(8), True, True)
                            for n in range(PLE_T):
                                for half in range(2):
                                    last = pe.matmul(BANK[b + 2 + half][:, 0:HALF], tile_w(s, DT + n),
                                                     x_half(pe_in)(n, half), start=n == 0, stop=n == PLE_T - 1)
                            last.then_inc(chunk_done, 1)

                @block.scalar
                def _(act):
                    act.sem_inc(sig, 4)
                    with act.Fori(0, DT // SLOTS) as i:
                        for s in range(SLOTS):
                            g = i * SLOTS + s
                            act.wait_ge(chunk_done, g + 1)
                            act.wait_ge(added, g + 1)
                            for half in range(2):
                                act.activation(sg[s % 2][:, half * HALF:(half + 1) * HALF],
                                               BANK[s % 2 * 4 + half][:, 0:HALF], ACT.Sigmoid).then_inc(sig, 1)

                @block.vector
                def _(dve):
                    dve.sem_inc(prod, 4)
                    dve.sem_inc(added, 2)
                    with dve.Fori(0, DT // SLOTS) as i:
                        for s in range(SLOTS):
                            g = i * SLOTS + s
                            dve.wait_ge(sig, g * 2 + 6)
                            for half in range(2):
                                cols = slice(half * HALF, (half + 1) * HALF)
                                dve.tensor_tensor(sg[s % 2][:, cols], sg[s % 2][:, cols],
                                                  BANK[s % 2 * 4 + 2 + half][:, 0:HALF], ALU.mult).then_inc(prod, 1)
                            dve.wait_ge(prod, g * 2 + 6)
                            dve.tensor_tensor(out[:, bass.ds(g, 1), :].rearrange("p o t -> p (o t)"),
                                              x[:, bass.ds(g, 1), :].rearrange("p o t -> p (o t)"), sg[s % 2],
                                              ALU.add).then_inc(added, 1)

        def shortconv_phase(ph, x):
            W, n, hist = 3, 3 * DT, 2
            group = 12
            scr = Arena()
            ext = [scr(ext_cols(W)) for _ in range(2)]
            y = [scr(ext_cols(W)) for _ in range(2)]
            cs = [scr(TOK) for _ in range(2)]
            state, new_state = scr(DT, NB * hist), scr(DT, (NB + 1) * hist)
            cw = scr(DT, W)
            chunk_done, c_out, ch_out, tap_done, conv_done, b_out, hist_in, saved, st_in, pads = (
                sem(f"sc_{y}") for y in ("chunk_done", "c_out", "ch_out", "tap_done", "conv_done", "b_out",
                                         "hist_in", "saved", "state_in", "pads_zero"))
            cols = SEQ + hist + NB * (hist + NS)
            with nc.Block() as block:
                @block.sync
                def _(sync):
                    sync.dma_start(state, I["st_sc"]).then_inc(st_in, 16)
                    sync.dma_start(cw, I["cw_sc"]).then_inc(st_in, 16)
                    load_weights(sync, ph, chunk_done)
                    sync.wait_ge(saved, 4 + 2 * DT)
                    store(sync, O["sc_conv"], new_state)

                @block.tensor
                def _(pe):
                    with pe.Fori(0, n // group) as i:
                        for j in range(group):
                            s, t, r = j % SLOTS, j // 3, j % 3
                            m = i * (group // 3) + t
                            pe.wait_ge(w_loaded[s], (i * (group // SLOTS) + (uses[ph] + j // SLOTS + 1)) * 16)
                            if r == 0:
                                pe.wait_ge(c_out, m * 2 + 2)
                            elif r == 1:
                                pe.wait_ge(ch_out, m * 3 + 3)
                            else:
                                pe.wait_ge(b_out, m * 3 + 3)
                            product(pe, BANK[2 * r:], s, x_half(x), range(8), True, True).then_inc(chunk_done, 1)

                @block.scalar
                def _(act):
                    act.sem_inc(c_out, 2)
                    with act.Fori(0, DT // 2) as i:
                        for t in range(2):
                            m = i * 2 + t
                            act.wait_ge(chunk_done, m * 3 + 1)
                            act.wait_ge(ch_out, m * 3 + 3 - (0 if t else 0))
                            for half in range(2):
                                act.activation(cs[t][:, half * HALF:(half + 1) * HALF], BANK[half][:, 0:HALF],
                                               ACT.Copy).then_inc(c_out, 1)

                @block.gpsimd
                def _(pool):
                    for s in range(2):
                        pool.memset(ext[s][:, 0:hist], 0.0).then_inc(pads, 1)
                    pool.sem_inc(saved, 4)
                    pool.wait_ge(st_in, 32)
                    with pool.Fori(0, DT // 2) as i:
                        for s in range(2):
                            m = i * 2 + s
                            pool.wait_ge(conv_done, m + 1)
                            pool.wait_ge(saved, m * 2 + 2)
                            history_in(pool, ext[s], state, m, hist, hist_in)
                        for s in range(2):
                            m = i * 2 + s
                            pool.wait_ge(ch_out, m * 3 + 6)
                            history_out(pool, ext[s], new_state, m, hist, saved)

                @block.vector
                def _(dve):
                    dve.sem_inc(ch_out, 3)
                    dve.sem_inc(b_out, 3)
                    dve.sem_inc(conv_done, 2)
                    dve.wait_ge(st_in, 32)
                    dve.wait_ge(pads, 2)
                    with dve.Fori(0, DT // 2) as i:
                        for t in range(2):
                            m = i * 2 + t
                            dve.wait_ge(chunk_done, m * 3 + 2)
                            dve.wait_ge(c_out, m * 2 + 4)
                            dve.wait_ge(conv_done, m + 1)
                            dve.wait_ge(saved, m * 2 + 2)
                            e = ext[t]
                            dve.tensor_tensor(e[:, hist:hist + HALF], cs[t][:, 0:HALF], BANK[2][:, 0:HALF],
                                              ALU.mult).then_inc(ch_out, 1)
                            dve.tensor_tensor(e[:, hist + HALF:hist + SEQ], cs[t][:, HALF:SEQ],
                                              BANK[3][:, 0:SEQ - HALF], ALU.mult).then_inc(ch_out, 1)
                            dve.tensor_tensor(sample_part(e, hist)[:, :, hist:],
                                              cs[t][:, SEQ:TOK].rearrange("p (b t) -> p b t", b=NB),
                                              BANK[3][:, SEQ - HALF:HALF].rearrange("p (b t) -> p b t", b=NB),
                                              ALU.mult).then_inc(ch_out, 1)
                            dve.wait_ge(ch_out, m * 3 + 6)
                            dve.wait_ge(hist_in, m + 1)
                            dve.wait_ge(b_out, m * 3 + 3)
                            tap_run(dve, e, y[t],
                                    lambda j: cw[:, bass.ds(m, 1), j:j + 1].rearrange("p o t -> p (o t)"),
                                    W, m, tap_done, conv_done)
                            dve.wait_ge(conv_done, m + 3)
                            dve.wait_ge(chunk_done, m * 3 + 3)
                            out = BIG[:, bass.ds(m, 1), :].rearrange("p o t -> p (o t)")
                            dve.tensor_tensor(out[:, 0:HALF], y[t][:, 0:HALF], BANK[4][:, 0:HALF],
                                              ALU.mult).then_inc(b_out, 1)
                            dve.tensor_tensor(out[:, HALF:SEQ], y[t][:, HALF:SEQ], BANK[5][:, 0:SEQ - HALF],
                                              ALU.mult).then_inc(b_out, 1)
                            dve.tensor_tensor(out[:, SEQ:TOK].rearrange("p (b t) -> p b t", b=NB),
                                              y[t][:, SEQ + hist:cols].rearrange("p (b t) -> p b t", b=NB)[:, :, 0:NS],
                                              BANK[5][:, SEQ - HALF:HALF].rearrange("p (b t) -> p b t", b=NB),
                                              ALU.mult).then_inc(b_out, 1)

        def kq_tile(m):
            return BIG[:, 3 * (m // 2) + m % 2, :]

        def kq_finish(dve, m, rstd, done):
            dve.tensor_tensor(kq_tile(m), kq_tile(m), rstd, ALU.mult).then_inc(done, 1)

        o_scaled = sem("o_scaled")

        def o_finish(dve, h, rstd, done):
            o = BIG[:, 3 * h + 1, :]
            dve.tensor_tensor(o, o, rstd, ALU.mult).then_inc(o_scaled, 1)
            dve.wait_ge(o_scaled, h + 1)
            dve.scalar_tensor_tensor(out=o, in0=o, scalar=norm_g, in1=Z[:, h, :], op0=ALU.mult,
                                     op1=ALU.mult).then_inc(done, 1)

        qkv_phase(0)
        feature_norm("l2", 2 * H, kq_tile, ONES, lambda m: ((128.0, eps_l2q) if m % 2 else (1.0, eps_l2)), kq_finish)
        gate_phase(1)
        delta_prompt()
        delta_sample()
        feature_norm("rms", H, lambda h: BIG[:, 3 * h + 1, :], ONES, lambda m: (1.0 / P, eps_rms), o_finish)
        residual_phase("dout", 2, lambda k, half: BIG[:, 3 * k + 1, half * HALF:(half + 1) * HALF], X)
        layer_norm("ln0", 0, X)
        ffn_up("up0", 3, X, 0)
        residual_phase("down0", 4, x_half(BIG), X, 2)
        layer_norm("ln1", 2, X)
        ple_phase("ple0", 5, X, Z, 0)
        shortconv_phase(6, Z)
        residual_phase("scout", 7, x_half(BIG), Z)
        layer_norm("ln2", 4, Z)
        ffn_up("up1", 8, Z, 1)
        residual_phase("down1", 9, x_half(BIG), Z, 2)
        layer_norm("ln3", 6, Z)
        ple_phase("ple1", 10, Z, X, 1)
        with nc.Block() as block:
            @block.sync
            def _(sync):
                store(sync, O["y"], X[:])
                sync.wait_ge(out_done, outs[0])


_OUTS = {"y": (P, DT, TOK), "dn_conv": (P, QKV_T, 27), "dn_S_prompt": (P, H, P), "dn_S_sample": (H, P, NB, P),
         "sc_conv": (P, DT, 18), "ffn_conv0": (P, 2 * FT, 18), "ffn_conv1": (P, 2 * FT, 18)}


def _tiles(w, kt):
    import numpy as np
    K, N = w.shape
    a = w.reshape(K // (kt * P), kt, P, N // P, P).transpose(3, 0, 2, 1, 4)
    return np.ascontiguousarray(a.reshape(-1, P, kt * P))


def _cols(v):
    import numpy as np
    a = np.asarray(v)
    a = a.reshape(a.shape[:-1] + (a.shape[-1] // P, P))
    return np.ascontiguousarray(np.moveaxis(a, (-1, -2), (0, 1)))


def kernel(**inputs):
    import numpy as np
    import concourse.bacc as bacc
    from concourse.bass_utils import run_bass_kernel_spmd

    a = {k: np.asarray(v) for k, v in inputs.items()}
    f32 = np.float32

    def feat(prompt, sample, n):
        rows = np.concatenate([prompt.reshape(SEQ, -1), sample.reshape(SAMP, -1)])
        return np.ascontiguousarray(rows.T.reshape(n, P, TOK).transpose(1, 0, 2))

    def state(s, order):
        t = _cols(s)[:, order]
        return np.ascontiguousarray(t.reshape(P, len(order), -1))

    w_in = a["dn_w_in"][0]
    qkv_order = [x * H + h for h in range(H) for x in (1, 0, 2)]
    up_order = [x * FT + t for t in range(FT) for x in range(2)]
    sc_order = [x * DT + t for t in range(DT) for x in (1, 2, 0)]
    m = {"x": feat(a["x_prompt"], a["x_sample"], DT)}
    m["w_qkv"] = _tiles(w_in[:, :QKV_T * P], 8)[qkv_order]
    m["w_z"] = _tiles(w_in[:, QKV_T * P:4 * D], 8)
    ba = np.zeros((D, 40), f32)
    ba[:, 0:H] = w_in[:, 4 * D:4 * D + H]
    ba[:, A_ROW:] = w_in[:, 4 * D + H:]
    m["w_ba"] = np.ascontiguousarray(ba.reshape(DT, P, 40).transpose(1, 0, 2))
    m["w_dout"] = _tiles(a["dn_w_out"][0], 8)
    m["w_scin"] = _tiles(a["sc_w_in"][0], 8)[sc_order]
    m["w_scout"] = _tiles(a["sc_w_out"][0], 8)
    for l in range(2):
        m[f"w_up{l}"] = _tiles(a["ffn_w_up"][l], 8)[up_order]
        m[f"w_down{l}"] = _tiles(a["ffn_w_down"][l], 11)
        m[f"w_ple{l}"] = np.ascontiguousarray(np.concatenate(
            [_tiles(a["ple_w_gate"][l], 8), _tiles(a["ple_w_proj"][l], PLE_T)], axis=2))
        m[f"p{l}"] = feat(a["p_prompt"][l], a["p_sample"][l], PLE_T)
        m[f"st_ffn{l}"] = state(a["state_ffn_conv"][l], up_order)
        m[f"cw_ffn{l}"] = np.ascontiguousarray(_cols(a["ffn_conv_w"][l])[:, up_order])
    m["st_dn"] = state(a["state_dn_conv"][0], qkv_order)
    m["cw_dn"] = np.ascontiguousarray(_cols(a["dn_conv_w"][0])[:, qkv_order])
    m["st_sc"] = state(a["state_sc_conv"][0], list(range(DT)))
    m["cw_sc"] = _cols(a["sc_conv_w"][0])
    m["st_S"] = np.ascontiguousarray(a["state_dn_S"][0].transpose(1, 2, 0, 3))
    i, j = np.indices((P, P))
    m["mask_decay"] = np.where(j >= i, 0.0, -1e30).astype(f32)
    m["mask_sample"] = np.where((j >= i) & (j // NS == i // NS), 0.0, -1e30).astype(f32)[:, :SAMP].copy()
    m["mask_levels"] = np.ascontiguousarray(np.stack(
        [((i // s // 2 == j // s // 2) & (i // s % 2 == 1) & (j // s % 2 == 0)) for s in
         (1 << lv for lv in range(LEVELS))], axis=1).astype(f32))
    m["identity"] = np.eye(P, dtype=f32)
    m["ones"] = np.ones((P, P), f32)
    sel = np.zeros((H, H, P), f32)
    for h in range(H):
        sel[h, h] = 1.0
    m["select_head"] = sel
    keep = np.ones((H, TOK), f32)
    keep[:, 0:SEQ:CH] = 0.0
    keep[:, SEQ::NS] = 0.0
    m["keep"] = keep
    cv = np.zeros((P, 160), f32)
    for l in range(2):
        for n, name in enumerate(("ln_mix_g", "ln_mix_b", "ln_ffn_g", "ln_ffn_b")):
            at = (4 * l + n) * DT
            cv[:, at:at + DT] = _cols(a[name][l])
    cv[:, 64] = a["dn_norm_g"][0]
    cv[:, 65:69] = [1e-5, 1e-6, 1e-6, 128e-6]
    cv[A_ROW:A_ROW + H, 69] = a["dn_a_log"][0]
    cv[A_ROW:A_ROW + H, 70] = a["dn_dt_bias"][0]
    m["columns"] = cv

    nc = bacc.Bacc("TRN2", target_bir_lowering=False, num_devices=1)
    I = {k: nc.dram_tensor(f"in_{k}", v.shape, F32, kind="ExternalInput").ap() for k, v in m.items()}
    O = {k: nc.dram_tensor(f"out_{k}", s, F32, kind="ExternalOutput").ap() for k, s in _OUTS.items()}
    build(nc, I, O)
    r = run_bass_kernel_spmd(nc, [{f"in_{k}": np.ascontiguousarray(v) for k, v in m.items()}], core_ids=[0])
    got = {k: np.asarray(r.results[0][f"out_{k}"]) for k in _OUTS}

    y = got["y"].transpose(1, 0, 2).reshape(D, TOK).T

    def rows(s, order, hist):
        t = np.empty_like(s)
        t[:, order] = s
        t = t.transpose(2, 1, 0).reshape(NB + 1, hist, -1)
        return t[0:1], t[1:]

    dn = rows(got["dn_conv"], qkv_order, 3)
    sc = rows(got["sc_conv"], list(range(DT)), 2)
    ff = [rows(got[f"ffn_conv{l}"], up_order, 2) for l in range(2)]
    S_prompt = got["dn_S_prompt"].transpose(1, 0, 2)[None, None]
    S_sample = got["dn_S_sample"].transpose(2, 0, 1, 3)[None]
    return (y[:SEQ].reshape(1, SEQ, D).copy(), y[SEQ:].reshape(NB, NS, D).copy(), dn[0][None], S_prompt.copy(),
            sc[0][None], np.stack([f[0] for f in ff]), dn[1][None], S_sample.copy(), sc[1][None],
            np.stack([f[1] for f in ff]))
```

```python
from contextlib import ExitStack

import concourse.bass as bass
from concourse import mybir

F32 = mybir.dt.float32
ACT = mybir.ActivationFunctionType
ALU = mybir.AluOpType

P = 128
D = 1024
DT = D // P
SEQ = 512
NB, NS = 8, 8
SAMP = NB * NS
TOK = SEQ + SAMP
HALF = TOK // 2
H = 8
QKV_T = 3 * H
FF = 2816
FT = FF // P
PLE_T = 2
CH = 128
NCH = SEQ // CH
BL = 32
NBL = CH // BL
LEVELS, SAMP_LEVELS = 2, 3
SLOTS = 4
WCOLS = 11 * P
ALPHA = 4.0 ** 0.25
SCR_COLS = 16448
X_PARTS = 4
A_ROW = 32


def ext_cols(width):
    return (width - 1) + SEQ + NB * (width - 1 + NS)


def build(nc, I, O):
    with ExitStack() as ctx:
        def sb(name, shape):
            return ctx.enter_context(nc.sbuf_tensor(name, shape, F32))

        def sem(name):
            return ctx.enter_context(nc.semaphore(name))

        shared = {}

        in_use, stale = [], []

        def phase_sems(kind, names):
            if kind not in shared:
                shared[kind] = [sem(f"{kind}_{x}") for x in names]
            assert kind not in stale
            in_use.append(kind)
            return shared[kind]

        def clear_stale(sync):
            for kind in stale:
                for x in shared[kind]:
                    sync.sem_clear(x)
            stale[:] = in_use
            in_use.clear()

        X = sb("x", [P, DT, TOK])
        Y = sb("y", [P, DT, TOK])
        Z = sb("z", [P, DT, TOK])
        BIG = sb("big", [P, QKV_T, TOK])
        RING = sb("ring", [P, SLOTS, WCOLS])
        SCR = sb("scratch", [P, SCR_COLS])
        MASKT = sb("mask_decay", [P, P])
        MASKS = sb("mask_decay_sample", [P, SAMP])
        MASKL = sb("mask_levels", [P, SAMP_LEVELS + LEVELS, P])
        IDENT = sb("identity", [P, P])
        ONES = sb("ones", [P, P])
        CV = sb("column_constants", [P, 160])
        TOKS = sb("token_scalars", [P, NCH + 1, 4, H])
        BANK = [ctx.enter_context(nc.psum_tensor(f"bank{i}", [P, 512], F32)) for i in range(8)]

        class Arena:
            def __init__(self):
                self.at = 0

            def __call__(self, *dims):
                n = 1
                for d in dims:
                    n *= d
                a = SCR[:, self.at:self.at + n]
                self.at += n
                assert self.at <= SCR_COLS, self.at
                if len(dims) == 1:
                    return a
                names = "abcd"[:len(dims)]
                return a.rearrange(f"p ({' '.join(names)}) -> p {' '.join(names)}",
                                   **{n: d for n, d in zip(names, dims)})

        stats = SCR[:, SCR_COLS - 4 * TOK:].rearrange("p (s t) -> p s t", s=4)
        sum_y, sum_sq, mu, rs = (stats[:, n, :] for n in range(4))
        TD = SCR[:, SCR_COLS - 2 * BL * BL:].rearrange("p (a b c) -> p a b c", a=2, b=BL)

        S = SCR[:, SCR_COLS - 2 * BL * BL - H * P:SCR_COLS - 2 * BL * BL].rearrange("p (h n) -> p h n", h=H)

        lnp = CV[:, 0:64].rearrange("p (k t) -> p k t", k=8)
        norm_g = CV[:, 64:65]
        eps_ln, eps_rms, eps_l2, eps_l2q = (CV[:, 65 + i:66 + i] for i in range(4))
        a_log = CV[A_ROW:A_ROW + H, 69:70]
        dt_bias = CV[A_ROW:A_ROW + H, 70:71]
        neg_ea = CV[A_ROW:A_ROW + H, 71:72]
        l2_scale, l2_eps = CV[0:2 * H, 72:73], CV[0:2 * H, 73:74]
        one_hot = CV[:, 80:111]

        def sum_column(m, n=2 * H):
            return one_hot[:, 15 - m:15 - m + n]

        w_loaded = [sem(f"w_loaded{s}") for s in range(SLOTS)]
        const_in = sem("const_in")
        x_in = [sem(f"x_in{part}") for part in range(X_PARTS)]
        out_done = sem("out_done")
        outs = [0]

        def store(eng, dst, src):
            outs[0] += 16
            eng.dma_start(dst, src).then_inc(out_done, 16)

        streams = [(I["w_qkv"], QKV_T, 8), (I["w_z"], H, 8), (I["w_dout"], DT, 8),
                   (I["w_up0"], 2 * FT, 8), (I["w_down0"], 2 * DT, 11), (I["w_ple0"], DT, 10),
                   (I["w_scin"], 3 * DT, 8), (I["w_scout"], DT, 8),
                   (I["w_up1"], 2 * FT, 8), (I["w_down1"], 2 * DT, 11), (I["w_ple1"], DT, 10)]
        uses = [0]
        for _, n, _ in streams:
            uses.append(uses[-1] + n // SLOTS)

        def load_x(eng, part):
            tiles = slice(part * DT // X_PARTS, (part + 1) * DT // X_PARTS)
            eng.dma_start(X[:, tiles, :], I["x"][:, tiles]).then_inc(x_in[part], 16)

        def x_ready(pe, k):
            if k % (DT // X_PARTS) == 0:
                pe.wait_ge(x_in[k * X_PARTS // DT], 16)

        def load_weights(sync, ph, chunk_done):
            w, n, kt = streams[ph]
            with sync.Fori(1, n // SLOTS) as i:
                for s in range(SLOTS):
                    sync.wait_ge(chunk_done, (i - 1) * SLOTS + s + 1)
                    sync.dma_start(RING[:, s, 0:kt * P],
                                   w[bass.ds(i * SLOTS + s, 1)].rearrange("o p n -> p (o n)")
                                   ).then_inc(w_loaded[s], 16)
            if ph + 1 < len(streams):
                w2, n2, kt2 = streams[ph + 1]
                for s in range(SLOTS):
                    sync.wait_ge(chunk_done, n - SLOTS + s + 1)
                    sync.dma_start(RING[:, s, 0:kt2 * P], w2[s]).then_inc(w_loaded[s], 16)

        def tile_w(s, k):
            return RING[:, s, k * P:(k + 1) * P]

        def product(pe, banks, s, rhs, ks, start, stop, ready=None):
            for n, k in enumerate(ks):
                if ready is not None:
                    ready(pe, k)
                for half in range(2):
                    last = pe.matmul(banks[half][:, 0:HALF], tile_w(s, n), rhs(k, half),
                                     start=start and n == 0, stop=stop and n == len(ks) - 1)
            return last

        def x_half(buf):
            return lambda k, half: buf[:, k, half * HALF:(half + 1) * HALF]

        load_n = [0]
        with nc.Block() as block:
            @block.sync
            def _(sync):
                w, _, kt = streams[0]
                for s in range(SLOTS):
                    sync.dma_start(RING[:, s, 0:kt * P], w[s]).then_inc(w_loaded[s], 16)
                    if s == 0:
                        for part in range(0, X_PARTS, 2):
                            load_x(sync, part)

            @block.scalar
            def _(act):
                for part in range(1, X_PARTS, 2):
                    load_x(act, part)

            @block.vector
            def _(dve):
                dve.memset(TOKS[:], 0.0)

        class ZTiles:
            PHASE = 1

            def __init__(self, name, tiles):
                self.tiles = tiles
                self.made, self.copied = sem(f"{name}_z_made"), sem(f"{name}_z_copied")

            def pe(self, pe, banks_free, some=slice(None)):
                for n, g in list(enumerate(self.tiles))[some]:
                    pe.wait_ge(w_loaded[g % SLOTS], (uses[self.PHASE] + g // SLOTS + 1) * 16)
                    if n < 2:
                        banks_free(n)
                    else:
                        pe.wait_ge(self.copied, n - 1)
                    product(pe, BANK[n % 2 * 2:], g % SLOTS, x_half(X), range(8), True, True).then_inc(self.made, 1)

            def act(self, act):
                for n, g in enumerate(self.tiles):
                    act.wait_ge(self.made, n + 1)
                    for half in range(2):
                        last = act.activation(Z[:, g, half * HALF:(half + 1) * HALF],
                                              BANK[n % 2 * 2 + half][:, 0:HALF], ACT.Silu)
                    last.then_inc(self.copied, 1)

            def sync(self, sync):
                for n, g in enumerate(self.tiles):
                    sync.wait_ge(self.made, n + 1)
                    w, kt, m = (I["w_z"], DT, g + SLOTS) if g + SLOTS < H else (
                        streams[self.PHASE + 1][0], streams[self.PHASE + 1][2], g + SLOTS - H)
                    sync.dma_start(RING[:, g % SLOTS, 0:kt * P], w[m]).then_inc(w_loaded[g % SLOTS], 16)

        def fill_ext(act, banks, ext, hist, filled):
            act.activation(ext[:, hist:hist + HALF], banks[0][:, 0:HALF], ACT.Copy).then_inc(filled, 1)
            act.activation(ext[:, hist + HALF:hist + SEQ], banks[1][:, 0:SEQ - HALF], ACT.Copy).then_inc(filled, 1)
            act.activation(sample_part(ext, hist)[:, :, hist:],
                           banks[1][:, SEQ - HALF:HALF].rearrange("p (b t) -> p b t", b=NB),
                           ACT.Copy).then_inc(filled, 1)

        def sample_part(ext, hist):
            return ext[:, hist + SEQ:hist + SEQ + NB * (hist + NS)].rearrange("p (b t) -> p b t", b=NB)

        def tap_run(dve, ext, out, weights, width, g, tap_done, conv_done):
            n = ext_cols(width) - (width - 1)
            per = width - 1
            dve.tensor_scalar(out[:, 0:n], ext[:, 0:n], weights(0), None, ALU.mult).then_inc(tap_done, 1)
            for j in range(1, width):
                dve.wait_ge(tap_done, g * per + j)
                dve.scalar_tensor_tensor(out=out[:, 0:n], in0=ext[:, j:j + n], scalar=weights(j), in1=out[:, 0:n],
                                         op0=ALU.mult, op1=ALU.add).then_inc(conv_done if j == per else tap_done, 1)

        def history_in(pool, ext, state, c, hist, hist_in):
            pool.tensor_copy(sample_part(ext, hist)[:, :, 0:hist],
                             state[:, bass.ds(c, 1), :].rearrange("p o (b t) -> p (o b) t", b=NB)
                             ).then_inc(hist_in, 1)

        def history_out(pool, ext, new_state, c, hist, saved):
            pool.tensor_copy(new_state[:, bass.ds(c, 1), 0:hist].rearrange("p o t -> p (o t)"),
                             ext[:, SEQ:SEQ + hist]).then_inc(saved, 1)
            pool.tensor_copy(new_state[:, bass.ds(c, 1), hist:].rearrange("p o (b t) -> p (o b) t", b=NB),
                             sample_part(ext, hist)[:, :, NS:]).then_inc(saved, 1)

        def qkv_phase(ph):
            W, n, hist = 4, QKV_T, 3
            scr = Arena()
            ext = [scr(ext_cols(W)) for _ in range(SLOTS)]
            y = [scr(ext_cols(W)) for _ in range(SLOTS)]
            state, new_state = scr(n, NB * hist), scr(n, (NB + 1) * hist)
            cw = scr(n, W)
            z = ZTiles("qkv", range(0, 2))
            chunk_done, filled, tap_done, conv_done, silu_done, hist_in, saved, st_in, pads = (
                sem(f"qkv_{x}") for x in ("chunk_done", "ext_filled", "tap_done", "conv_done", "silu_done",
                                          "hist_in", "saved", "state_in", "pads_zero"))
            with nc.Block() as block:
                @block.sync
                def _(sync):
                    sync.dma_start(state, I["st_dn"]).then_inc(st_in, 16)
                    sync.dma_start(cw, I["cw_dn"]).then_inc(st_in, 16)
                    for dst, name in ((MASKT, "mask_decay"), (MASKS, "mask_sample"), (MASKL, "mask_levels"),
                                      (IDENT, "identity"), (ONES, "ones"), (CV, "columns")):
                        sync.dma_start(dst[:], I[name]).then_inc(const_in, 16)
                        load_n[0] += 16
                    load_weights(sync, ph, chunk_done)
                    z.sync(sync)
                    sync.wait_ge(saved, 8 + 2 * n)
                    store(sync, O["dn_conv"], new_state)
                    sync.wait_ge(const_in, load_n[0])
                    sync.wait_ge(out_done, outs[0])

                @block.tensor
                def _(pe):
                    with pe.Fori(0, n // SLOTS) as i:
                        for s in range(SLOTS):
                            g = i * SLOTS + s
                            pe.wait_ge(w_loaded[s], (i + uses[ph] + 1) * 16)
                            pe.wait_ge(filled, g * 3 + 3)
                            product(pe, BANK[s % 2 * 2:], s, x_half(X), range(8), True, True,
                                    x_ready if s == 0 else None).then_inc(chunk_done, 1)
                    z.pe(pe, lambda pair: pe.wait_ge(filled, 6 + 3 * (n - 1 + pair)))

                @block.scalar
                def _(act):
                    act.sem_inc(filled, 6)
                    act.sem_inc(silu_done, 8)
                    with act.Fori(0, n // SLOTS) as i:
                        for s in range(SLOTS):
                            g = i * SLOTS + s
                            act.wait_ge(chunk_done, g + 1)
                            act.wait_ge(conv_done, g + 1)
                            act.wait_ge(saved, g * 2 + 2)
                            fill_ext(act, BANK[s % 2 * 2:], ext[s], hist, filled)
                        for s in range(SLOTS):
                            g = i * SLOTS + s
                            act.wait_ge(conv_done, g + 5)
                            out = BIG[:, bass.ds(g, 1), :].rearrange("p o t -> p (o t)")
                            act.activation(out[:, 0:SEQ], y[s][:, 0:SEQ], ACT.Silu).then_inc(silu_done, 1)
                            act.activation(out[:, SEQ:TOK].rearrange("p (b t) -> p b t", b=NB),
                                           y[s][:, SEQ + hist:SEQ + hist + NB * (hist + NS)]
                                           .rearrange("p (b t) -> p b t", b=NB)[:, :, 0:NS],
                                           ACT.Silu).then_inc(silu_done, 1)
                    z.act(act)

                @block.gpsimd
                def _(pool):
                    for s in range(SLOTS):
                        pool.memset(ext[s][:, 0:hist], 0.0).then_inc(pads, 1)
                    pool.sem_inc(saved, 8)
                    pool.wait_ge(st_in, 32)
                    with pool.Fori(0, n // SLOTS) as i:
                        for s in range(SLOTS):
                            pool.wait_ge(conv_done, i * SLOTS + s + 1)
                            pool.wait_ge(saved, (i * SLOTS + s) * 2 + 2)
                            history_in(pool, ext[s], state, i * SLOTS + s, hist, hist_in)
                        for s in range(SLOTS):
                            pool.wait_ge(filled, (i * SLOTS + s) * 3 + 9)
                            history_out(pool, ext[s], new_state, i * SLOTS + s, hist, saved)

                @block.vector
                def _(dve):
                    dve.sem_inc(conv_done, 4)
                    dve.wait_ge(st_in, 32)
                    dve.wait_ge(pads, SLOTS)
                    with dve.Fori(0, n // SLOTS) as i:
                        for s in range(SLOTS):
                            g = i * SLOTS + s
                            dve.wait_ge(filled, g * 3 + 9)
                            dve.wait_ge(hist_in, g + 1)
                            dve.wait_ge(silu_done, g * 2 + 2)
                            tap_run(dve, ext[s], y[s],
                                    lambda j: cw[:, bass.ds(g, 1), j:j + 1].rearrange("p o t -> p (o t)"),
                                    W, g, tap_done, conv_done)

        def gate_phase():
            scr = Arena()
            wba = scr(DT, 40)
            bg = scr(TOK)
            t1, t2, keep = scr(TOK), scr(TOK), scr(TOK)
            sel = scr(2 * H, P)
            sq = [scr(TOK) for _ in range(4)]
            rstd = scr(TOK)
            z = ZTiles("gate", range(2, 4))
            (w_in, ba_ready, step, logit, tr_done, tr_out, gc_b, gc_out, sq_done, sq_read,
             sum_done, std_done, rec_done, rb_done, normed) = (
                sem(f"gate_{x}") for x in ("w_in", "ba_ready", "dve_step", "act_step",
                                           "tr_done", "tr_out", "gc_b", "gc_out", "sq_done", "sq_read", "sum_done",
                                           "std_done", "rec_done", "rstd_bcast", "normed"))
            gate = slice(A_ROW, A_ROW + H)
            NT = 2 * H
            rows = slice(0, NT)

            def kq(m):
                return BIG[:, 3 * (m // 2) + m % 2, :]

            with nc.Block() as block:
                @block.sync
                def _(sync):
                    sync.dma_start(wba, I["w_ba"]).then_inc(w_in, 16)
                    sync.dma_start(sel, I["select"]).then_inc(w_in, 16)
                    sync.dma_start(keep[gate], I["keep"]).then_inc(w_in, 16)
                    z.sync(sync)

                @block.tensor
                def _(pe):
                    z.pe(pe, lambda pair: None, slice(0, 1))
                    pe.wait_ge(w_in, 48)
                    for k in range(DT):
                        for half in range(2):
                            last = pe.matmul(BANK[4 + half][0:40, 0:HALF], wba[:, k, :], x_half(X)(k, half),
                                             start=k == 0, stop=k == DT - 1)
                    last.then_inc(ba_ready, 1)
                    for m in range(NT):
                        pe.wait_ge(sq_done, m + 1)
                        for half in range(2):
                            last = pe.matmul(BANK[6 + half][rows, 0:HALF], sum_column(m),
                                             sq[m % 4][:, half * HALF:(half + 1) * HALF], start=m == 0,
                                             stop=m == NT - 1)
                        last.then_inc(sq_read, 1)
                    z.pe(pe, lambda pair: None, slice(1, None))
                    pe.wait_ge(rec_done, 1)
                    pe.wait_ge(z.copied, len(z.tiles))
                    for m in range(NT):
                        b = m % 3 * 2
                        if m == 2:
                            pe.wait_ge(logit, 5)
                        if m >= 3:
                            pe.wait_ge(normed, 2 * (m - 2))
                        for half in range(2):
                            last = pe.matmul(BANK[b + half][:, 0:HALF], sel[:, m, :],
                                             rstd[:, half * HALF:(half + 1) * HALF], start=True, stop=True)
                        last.then_inc(rb_done, 1)
                    pe.wait_ge(step, 7)
                    pe.wait_ge(std_done, 2)
                    for c in range(NCH + 1):
                        w = min(CH, TOK - c * CH)
                        last = pe.transpose(BANK[6][0:w, c * 40:c * 40 + 40], bg[0:40, c * CH:c * CH + w],
                                            IDENT[0:40, 0:40])
                    last.then_inc(tr_done, 1)
                    for h in range(H):
                        b = 0 if h % 2 == 0 else 2
                        pe.wait_ge(normed, 2 * NT)
                        if h >= 2:
                            pe.wait_ge(gc_out, h - 1)
                        for half in range(2):
                            last = pe.matmul(BANK[b + half][:, 0:HALF], sel[:, H + h, :],
                                             bg[:, half * HALF:(half + 1) * HALF], start=True, stop=True)
                        last.then_inc(gc_b, 1)

                @block.scalar
                def _(act):
                    for m in range(0, NT, 2):
                        if m >= 4:
                            act.wait_ge(sq_read, m - 3)
                        if m:
                            act.wait_ge(sq_done, m)
                        act.activation(sq[m % 4], kq(m), ACT.Square).then_inc(sq_done, 1)
                    act.activation(neg_ea, a_log, ACT.Exp).then_inc(logit, 1)
                    act.wait_ge(ba_ready, 1)
                    act.wait_ge(step, 1)
                    for half in range(2):
                        cols = slice(half * HALF, (half + 1) * HALF)
                        act.activation(bg[0:H, cols], BANK[4 + half][0:H, 0:HALF], ACT.Sigmoid).then_inc(logit, 1)
                    for half in range(2):
                        cols = slice(half * HALF, (half + 1) * HALF)
                        act.activation(t1[gate, cols], BANK[4 + half][gate, 0:HALF], ACT.Identity,
                                       bias=dt_bias).then_inc(logit, 1)
                    act.wait_ge(step, 3)
                    act.activation(t2[gate], t2[gate], ACT.Exp, scale=-1.0).then_inc(logit, 1)
                    act.wait_ge(logit, 6)
                    act.activation(t2[gate], t2[gate], ACT.Ln, bias=1.0).then_inc(logit, 1)
                    act.wait_ge(sq_read, NT)
                    act.wait_ge(step, 1)
                    for half in range(2):
                        act.activation(rstd[rows, half * HALF:(half + 1) * HALF], BANK[6 + half][rows, 0:HALF],
                                       ACT.Sqrt, bias=l2_eps, scale=l2_scale).then_inc(std_done, 1)
                    z.act(act)
                    for h in range(H):
                        b = 0 if h % 2 == 0 else 2
                        act.wait_ge(gc_b, h + 1)
                        for half in range(2):
                            last = act.activation(Y[:, h, half * HALF:(half + 1) * HALF],
                                                  BANK[b + half][:, 0:HALF], ACT.Copy)
                        last.then_inc(gc_out, 1)

                @block.vector
                def _(dve):
                    dve.memset(rstd, 0.0)
                    dve.memset(bg[:], 0.0).then_inc(step, 1)
                    for m in range(1, NT, 2):
                        if m >= 4:
                            dve.wait_ge(sq_read, m - 3)
                        dve.wait_ge(sq_done, m)
                        dve.tensor_tensor(sq[m % 4], kq(m), kq(m), ALU.mult).then_inc(sq_done, 1)
                    dve.wait_ge(logit, 1)
                    dve.tensor_scalar(neg_ea, neg_ea, -1.0, None, ALU.mult).then_inc(step, 1)
                    dve.wait_ge(logit, 5)
                    dve.scalar_tensor_tensor(out=t2[gate], in0=t1[gate], scalar=-1.0, in1=t1[gate],
                                             op0=ALU.mult, op1=ALU.max).then_inc(step, 1)
                    dve.wait_ge(logit, 7)
                    dve.wait_ge(step, 3)
                    dve.scalar_tensor_tensor(out=t1[gate], in0=t1[gate], scalar=0.0, in1=t2[gate],
                                             op0=ALU.max, op1=ALU.add).then_inc(step, 1)
                    dve.wait_ge(step, 4)
                    dve.tensor_scalar(t1[gate], t1[gate], neg_ea, None, ALU.mult).then_inc(step, 1)
                    dve.wait_ge(step, 5)
                    dve.wait_ge(w_in, 48)
                    dve.tensor_tensor_scan(bg[gate], keep[gate], t1[gate], 0.0, ALU.mult, ALU.add).then_inc(step, 1)
                    dve.wait_ge(step, 6)
                    dve.sem_inc(step, 1)
                    dve.wait_ge(std_done, 2)
                    dve.reciprocal(rstd[rows], rstd[rows]).then_inc(rec_done, 1)
                    for m in range(NT):
                        dve.wait_ge(rb_done, m + 1)
                        for half in range(2):
                            cols = slice(half * HALF, (half + 1) * HALF)
                            dve.tensor_tensor(kq(m)[:, cols], kq(m)[:, cols], BANK[m % 3 * 2 + half][:, 0:HALF],
                                              ALU.mult).then_inc(normed, 1)
                    dve.wait_ge(tr_done, 1)
                    for n, (toks, cs) in enumerate(((slice(0, P), slice(0, NCH)),
                                                    (slice(0, SAMP), slice(NCH, NCH + 1)))):
                        by_tok = BANK[6][toks, cs.start * 40:cs.stop * 40].rearrange("p (c n) -> p c n", n=40)
                        dve.tensor_scalar(TOKS[toks, cs, 0, :], by_tok[:, :, A_ROW:A_ROW + H], -1.0, None,
                                          ALU.mult).then_inc(step, 1)
                        dve.tensor_copy(TOKS[toks, cs, 1, :], by_tok[:, :, 0:H]).then_inc(step, 1)
                    dve.wait_ge(step, 11)
                    dve.tensor_scalar(TOKS[:, :, 3, :], TOKS[:, :, 1, :], -1.0, None, ALU.mult).then_inc(step, 1)

        def block_inverses():
            scr = Arena()
            G = scr(BL, NCH * H)
            B = scr(BL, BL)
            Tt = scr(BL, BL)
            prod = scr(BL * BL // 4)
            bt, bT = scr(NCH * H), scr(BL)
            e_done, b_done, kk_done, arg, expd, kkd, moved, row, clr, outp = (
                sem(f"inv_{x}") for x in ("tok_exp", "tok_mul", "kk_done", "arg", "exp", "kkd", "moved", "row",
                                          "cleared", "out"))
            z = ZTiles("inv", range(4, H))

            def quarters(c_h, r):
                return slice(BL * r, BL * (r + 1))

            with nc.Block() as block:
                @block.tensor
                def _(pe):
                    for q in range(NCH * H):
                        c, h = q // H, q % H
                        k = BIG[:, 3 * h, c * CH:(c + 1) * CH]
                        last = pe.matmul(BANK[q // 4][:, q % 4 * CH:(q % 4 + 1) * CH], k, k, start=True, stop=True)
                        if q % 4 == 3:
                            last.then_inc(kk_done, 1)
                    z.pe(pe, lambda pair: pe.wait_ge(kkd, 8 * (pair + 1)))

                @block.sync
                def _(sync):
                    z.sync(sync)

                @block.scalar
                def _(act):
                    act.activation(TOKS[:, :, 2, :], TOKS[:, :, 0, :], ACT.Exp, scale=-1.0).then_inc(e_done, 1)
                    act.wait_ge(arg, NBL + 1)
                    act.activation(G, G, ACT.Exp).then_inc(expd, 1)
                    z.act(act)

                @block.gpsimd
                def _(pool):
                    pool.memset(Tt, 0.0).then_inc(clr, 1)
                    pool.memset(S, 0.0)
                    pool.wait_ge(clr, 1)
                    pool.memset(Tt.rearrange("p a b -> p (a b)")[:, 0:BL * BL:BL + 1], 1.0).then_inc(clr, 1)

                @block.vector
                def _(dve):
                    gv = G.rearrange("p i (c h) -> p i c h", c=NCH)
                    for r in range(NBL):
                        part = slice(BL * r, BL * (r + 1))
                        gc = Y[part, :, 0:SEQ].rearrange("p h (c t) -> p h c t", c=NCH)[:, :, :, part]
                        dve.tensor_tensor(gv[part], gc.rearrange("p h c t -> p t c h"),
                                          TOKS[part, 0:NCH, 0, :].unsqueeze(1).to_broadcast([BL, BL, NCH, H]),
                                          ALU.add).then_inc(arg, 1)
                    dve.wait_ge(arg, NBL)
                    dve.tensor_scalar(G, G, 0.0, None, ALU.min).then_inc(arg, 1)
                    dve.wait_ge(e_done, 1)
                    dve.tensor_tensor(TOKS[:, :, 2, :], TOKS[:, :, 2, :], TOKS[:, :, 3, :],
                                      ALU.mult).then_inc(b_done, 1)
                    dve.tensor_copy(bt.rearrange("p (c h) -> p c h", c=NCH), TOKS[:, 0:NCH, 3, :]).then_inc(moved, 1)
                    dve.wait_ge(moved, 1)
                    dve.transpose(bT, bt).then_inc(moved, 1)
                    dve.wait_ge(expd, 1)
                    for q in range(NCH * H // 4):
                        dve.wait_ge(kk_done, q + 1)
                        for r in range(NBL):
                            part = slice(BL * r, BL * (r + 1))
                            g4 = G[part, :, 4 * q:4 * q + 4]
                            kk = BANK[q][part, :].rearrange("p (h t) -> p h t", h=4)[:, :, part]
                            dve.tensor_tensor(g4, g4, kk.rearrange("p h t -> p t h"), ALU.mult).then_inc(kkd, 1)
                    dve.wait_ge(kkd, NCH * H)
                    dve.transpose(B.rearrange("p a b -> p (a b)"), G.rearrange("p a b -> p (a b)")
                                  ).then_inc(moved, 1)
                    dve.wait_ge(moved, 3)
                    dve.tensor_tensor(B, B, bT.unsqueeze(2).to_broadcast([P, BL, BL]), ALU.mult).then_inc(moved, 1)
                    dve.wait_ge(moved, 4)
                    dve.wait_ge(clr, 2)
                    for i in range(BL - 1):
                        below = BL - 1 - i
                        part = Tt[:, 0:i + 1, i + 1:BL]
                        pr = prod[:, 0:(i + 1) * below].rearrange("p (c r) -> p c r", r=below)
                        if i:
                            dve.wait_ge(row, 2 * i)
                        dve.tensor_tensor(pr, Tt[:, 0:i + 1, i:i + 1].to_broadcast([P, i + 1, below]),
                                          B[:, i + 1:BL, i:i + 1].rearrange("p r o -> p o r")
                                          .to_broadcast([P, i + 1, below]), ALU.mult).then_inc(row, 1)
                        dve.wait_ge(row, 2 * i + 1)
                        dve.tensor_tensor(part, part, pr, ALU.add).then_inc(row, 1)
                    dve.wait_ge(row, 2 * (BL - 1))
                    dve.tensor_copy(B, Tt.rearrange("p c i -> p i c")).then_inc(outp, 1)
                    dve.transpose(TD[:, 0].rearrange("p a b -> p (a b)"), Tt.rearrange("p a b -> p (a b)")
                                  ).then_inc(outp, 1)
                    dve.wait_ge(outp, 2)
                    dve.transpose(TD[:, 1].rearrange("p a b -> p (a b)"), B.rearrange("p a b -> p (a b)")
                                  ).then_inc(outp, 1)

        def delta_prompt():
            scr = Arena()
            st = scr(H, 3, CH)
            dec = scr(H, CH)
            ka = scr(H, 2, CH)
            T = scr(H, 2, CH)
            def qe(h):
                return RING[:, h // 3, DT * P + h % 3 * CH:DT * P + (h % 3 + 1) * CH]

            Ys = scr(H, CH)
            ktok, vtok = scr(H, P), scr(H, P)
            vnew = scr(H, P)
            sc = scr(4, H)
            eg = scr(H, CH)
            names = ("stage", "scal", "arg", "dec", "kq", "att", "tr", "tok", "eg", "qe", "tinit", "y", "ymask",
                     "d", "t", "ks", "r", "v", "vn", "os", "o_out", "s_out")
            q = {x: sem(f"dp_{x}") for x in names}
            with nc.Block() as block:
                @block.vector
                def _(dve):
                    dve.sem_inc(q["s_out"], H)
                    dve.sem_inc(q["qe"], 1)

                    def stage(c):
                        dve.tensor_copy(st.rearrange("p a b c -> p (a b) c"),
                                        BIG[:, :, bass.ds(c * CH, CH)]).then_inc(q["stage"], 1)

                    def attention_and_inverse(c):
                        for h in range(H):
                            dve.wait_ge(q["dec"], c * H + h + 1)
                            dve.wait_ge(q["kq"], c * H + h + 1)
                            dve.tensor_tensor(ka[:, h], BANK[h][:, 256:512].rearrange("p (a b) -> p a b", a=2),
                                              dec[:, h, :].unsqueeze(1).to_broadcast([P, 2, CH]),
                                              ALU.mult).then_inc(q["att"], 1)
                        dve.wait_ge(q["tinit"], (c + 1) * (NBL + 1))
                        for lv in range(LEVELS):
                            for h in range(H):
                                dve.wait_ge(q["y"], c * (LEVELS * H) + lv * H + h + 1)
                                dve.scalar_tensor_tensor(out=Ys[:, h, :], in0=BANK[h][:, 0:CH],
                                                         scalar=sc[:, 1, h:h + 1], in1=MASKL[:, SAMP_LEVELS + lv, :],
                                                         op0=ALU.mult, op1=ALU.mult).then_inc(q["ymask"], 1)
                            first = 1 if lv == LEVELS - 1 else 0
                            for h in range(H):
                                dve.wait_ge(q["d"], c * (LEVELS * H) + lv * H + h + 1)
                                if lv:
                                    dve.wait_ge(q["t"], c * (LEVELS * H) + (lv - 1) * H + h + 1)
                                dve.tensor_tensor(T[:, h, first:2], T[:, h, first:2],
                                                  BANK[h][:, 256 + first * CH:512]
                                                  .rearrange("p (a b) -> p a b", b=CH),
                                                  ALU.subtract).then_inc(q["t"], 1)
                        for h in range(H):
                            dve.wait_ge(q["ks"], c * H + H + h + 1)
                            dve.wait_ge(q["tok"], c * (2 * H) + 2 * h + 2)
                            dve.scalar_tensor_tensor(out=Ys[:, h, :], in0=BANK[h][:, 0:P],
                                                     scalar=sc[:, 2, h:h + 1], in1=vtok[:, h, :],
                                                     op0=ALU.mult, op1=ALU.add).then_inc(q["r"], 1)

                    def state_update(c):
                        for h in range(H):
                            dve.wait_ge(q["os"], c * H + H + h + 1)
                            dve.scalar_tensor_tensor(out=S[:, h, :], in0=S[:, h, :], scalar=eg[:, h, CH - 1:CH],
                                                     in1=BANK[h][:, 384:512], op0=ALU.mult,
                                                     op1=ALU.add).then_inc(q["s_out"], 1)

                    stage(0)
                    attention_and_inverse(0)
                    with dve.Fori(1, NCH) as c:
                        dve.wait_ge(q["qe"], c + 1)
                        dve.wait_ge(q["ks"], (c + 1) * H)
                        stage(c)
                        state_update(c - 1)
                        attention_and_inverse(c)
                    state_update(NCH - 1)

                @block.gpsimd
                def _(pool):
                    with pool.Fori(0, NCH) as c:
                        pool.wait_ge(q["vn"], (c + 1) * (2 * H))
                        pool.tensor_copy(sc, TOKS[:, bass.ds(c, 1), :, :].rearrange("p o a b -> p (o a) b")
                                         ).then_inc(q["scal"], 1)
                        pool.tensor_tensor(dec, Y[:, :, bass.ds(c * CH, CH)],
                                           MASKT[:].unsqueeze(1).to_broadcast([P, H, CH]), ALU.add
                                           ).then_inc(q["arg"], 1)
                        pool.memset(T, 0.0).then_inc(q["tinit"], 1)
                        pool.wait_ge(q["stage"], c + 1)
                        pool.wait_ge(q["arg"], c + 1)
                        pool.wait_ge(q["eg"], c + 1)
                        pool.wait_ge(q["os"], (c + 1) * H)
                        for n, h in enumerate(range(0, H, 3)):
                            heads = min(3, H - h)
                            last = pool.tensor_tensor(RING[:, n, DT * P:DT * P + heads * CH]
                                                      .rearrange("p (h t) -> p h t", h=heads),
                                                      st[:, h:h + heads, 1, :], eg[:, h:h + heads, :], ALU.mult)
                        last.then_inc(q["qe"], 1)

                @block.scalar
                def _(act):
                    act.sem_inc(q["vn"], 2 * H)
                    act.sem_inc(q["o_out"], H)
                    with act.Fori(0, NCH) as c:
                        act.wait_ge(q["scal"], c + 1)
                        act.wait_ge(q["arg"], c + 1)
                        for h in range(H):
                            act.activation(dec[:, h, :], dec[:, h, :], ACT.Exp, bias=sc[:, 0, h:h + 1]
                                           ).then_inc(q["dec"], 1)
                        act.wait_ge(q["tinit"], c * (NBL + 1) + 1)
                        for r in range(NBL):
                            part = slice(BL * r, BL * (r + 1))
                            act.activation(T[part, :, :, part].rearrange("p h a t -> p a t h"),
                                           TD[part, :, :, bass.ds(c * H, H)], ACT.Copy).then_inc(q["tinit"], 1)
                        act.wait_ge(q["s_out"], (c + 1) * H)
                        act.activation(eg, Y[:, :, bass.ds(c * CH, CH)], ACT.Exp).then_inc(q["eg"], 1)
                        for h in range(H):
                            act.wait_ge(q["tr"], c * H + h + 1)
                            act.activation(ktok[:, h, :], BANK[h][:, 0:P], ACT.Copy).then_inc(q["tok"], 1)
                            act.activation(vtok[:, h, :], BANK[h][:, P:2 * P], ACT.Copy,
                                           scale=sc[:, 1, h:h + 1]).then_inc(q["tok"], 1)
                        for h in range(H):
                            act.wait_ge(q["v"], c * H + h + 1)
                            act.activation(vnew[:, h, :], BANK[h][:, 128:256], ACT.Copy).then_inc(q["vn"], 1)
                            act.activation(vtok[:, h, :], BANK[h][:, 128:256], ACT.Copy,
                                           scale=dec[:, h, CH - 1:CH]).then_inc(q["vn"], 1)
                        for h in range(H):
                            act.wait_ge(q["s_out"], c * H + H + h + 1)
                            act.activation(BIG[:, 3 * h + 1, bass.ds(c * CH, CH)], BANK[h][:, 256:384],
                                           ACT.Copy).then_inc(q["o_out"], 1)

                @block.tensor
                def _(pe):
                    pe.sem_inc(q["ks"], H)
                    pe.sem_inc(q["os"], H)
                    with pe.Fori(0, NCH) as c:
                        pe.wait_ge(q["stage"], c + 1)
                        for h in range(H):
                            pe.wait_ge(q["o_out"], c * H + h + 1)
                            pe.wait_ge(q["s_out"], c * H + h + 1)
                            pe.matmul(BANK[h][:, 256:512], st[:, h, 0, :], st[:, h, 0:2, :], start=True,
                                      stop=True).then_inc(q["kq"], 1)
                        for h in range(H):
                            pe.wait_ge(q["att"], c * H + h + 1)
                            pe.transpose(BANK[h][:, 0:P], st[:, h, 0, :], IDENT[:])
                            pe.transpose(BANK[h][:, P:2 * P], st[:, h, 2, :], IDENT[:]).then_inc(q["tr"], 1)
                        pe.wait_ge(q["tinit"], (c + 1) * (NBL + 1))
                        for lv in range(LEVELS):
                            for h in range(H):
                                if lv:
                                    pe.wait_ge(q["t"], c * (LEVELS * H) + (lv - 1) * H + h + 1)
                                else:
                                    pe.wait_ge(q["tok"], c * (2 * H) + 2 * h + 2)
                                pe.matmul(BANK[h][:, 0:CH], ka[:, h, 0, :], T[:, h, 0, :], start=True,
                                          stop=True).then_inc(q["y"], 1)
                            for h in range(H):
                                pe.wait_ge(q["ymask"], c * (LEVELS * H) + lv * H + h + 1)
                                if lv < LEVELS - 1:
                                    pe.matmul(BANK[h][:, 256:384], T[:, h, 1, :], Ys[:, h, :], start=True,
                                              stop=True)
                                pe.matmul(BANK[h][:, 384:512], Ys[:, h, :], T[:, h, 1, :], start=True,
                                          stop=True).then_inc(q["d"], 1)
                        for h in range(H):
                            pe.wait_ge(q["t"], c * (LEVELS * H) + (LEVELS - 1) * H + h + 1)
                            pe.matmul(BANK[h][:, 0:P], st[:, h, 0, :], S[:, h, :], start=True,
                                      stop=True).then_inc(q["ks"], 1)
                        for h in range(H):
                            pe.wait_ge(q["r"], c * H + h + 1)
                            pe.matmul(BANK[h][:, 128:256], T[:, h, 1, :], Ys[:, h, :], start=True,
                                      stop=True).then_inc(q["v"], 1)
                        pe.wait_ge(q["qe"], c + 2)
                        for h in range(H):
                            pe.wait_ge(q["vn"], (c + 1) * (2 * H) + 2 * h + 2)
                            pe.matmul(BANK[h][:, 256:384], S[:, h, :], qe(h), start=True, stop=False)
                            pe.matmul(BANK[h][:, 256:384], vnew[:, h, :], ka[:, h, 1, :], start=False, stop=True)
                            pe.matmul(BANK[h][:, 384:512], ktok[:, h, :], vtok[:, h, :], start=True,
                                      stop=True).then_inc(q["os"], 1)

                @block.sync
                def _(sync):
                    sync.wait_ge(q["s_out"], (NCH + 1) * H)
                    store(sync, O["dn_S_prompt"], S)

        def delta_sample():
            scr = Arena()
            stored = outs[0]
            GROUP = 4
            SH = NB // 2
            dec = scr(H, SAMP)
            ka = scr(H, 2, SAMP)
            T = scr(H, 2, SAMP)
            Ys = scr(H, SAMP)
            ktok, vtok, vnew = scr(H, P), scr(H, P), scr(H, P)
            R = vtok
            ksq = scr(H, 2, SAMP)
            eg = scr(H, SAMP)
            vb = scr(H, NB, P)
            names = ("arg", "dec", "kq", "att", "tr", "tok", "eg", "tinit", "y", "ymask", "d", "t", "ks",
                     "ksq", "rt", "r", "v", "vn", "o", "o_out", "vb0", "vb1", "sdec", "su", "s_out", "pad")
            q = {x: sem(f"ds_{x}") for x in names}
            sin = [sem(f"ds_state_in{h}") for h in range(H)]
            A = slice(0, SAMP)
            last_tok = slice(NS - 1, SAMP, NS)

            def smp(r):
                return BIG[:, r, SEQ:TOK]

            def states(h, r):
                return BIG[:, 3 * h + 2 * r, 0:SH * P].rearrange("p (b n) -> p b n", b=SH)

            def updates(h, r):
                return h // GROUP * 2 * GROUP + r * GROUP + h % GROUP + 1

            with nc.Block() as block:
                @block.sync
                def _(sync):
                    for h in range(H):
                        for r in range(2):
                            sync.dma_start(states(h, r), I["st_S"][h, :, SH * r:SH * (r + 1)]).then_inc(sin[h], 16)
                    for group in range(0, H, GROUP):
                        for r in range(2):
                            for h in range(group, group + GROUP):
                                sync.wait_ge(q["s_out"], updates(h, r))
                                store(sync, O["dn_S_sample"][h, :, SH * r:SH * (r + 1)], states(h, r))

                @block.gpsimd
                def _(pool):
                    pool.memset(ktok[SAMP:P], 0.0).then_inc(q["pad"], 1)
                    pool.wait_ge(out_done, stored)
                    pool.memset(vb[SAMP:P], 0.0).then_inc(q["pad"], 1)
                    pool.wait_ge(q["eg"], 1)
                    for group in range(0, H, GROUP):
                        for r in range(2):
                            for h in range(group, group + GROUP):
                                pool.wait_ge(q["ks"], h + 1)
                                pool.tensor_tensor(states(h, r), states(h, r),
                                                   eg[:, h, last_tok][:, SH * r:SH * (r + 1)].unsqueeze(2)
                                                   .to_broadcast([P, SH, P]), ALU.mult).then_inc(q["sdec"], 1)

                @block.scalar
                def _(act):
                    act.activation(eg, Y[:, :, SEQ:TOK], ACT.Exp).then_inc(q["eg"], 1)
                    for h in range(H):
                        act.wait_ge(q["arg"], h + 1)
                        act.activation(dec[A, h, :], dec[A, h, :], ACT.Exp).then_inc(q["dec"], 1)
                    for h in range(H):
                        act.wait_ge(q["tr"], h + 1)
                        act.activation(ktok[A, h, :], BANK[h][A, 0:P], ACT.Copy).then_inc(q["tok"], 1)
                        act.activation(vtok[A, h, :], BANK[h][A, P:2 * P], ACT.Copy,
                                       scale=TOKS[A, NCH, 1, h:h + 1]).then_inc(q["tok"], 1)
                    for h in range(H):
                        act.wait_ge(q["v"], h + 1)
                        act.activation(vnew[A, h, :], BANK[h][A, 256:384], ACT.Copy).then_inc(q["vn"], 1)
                        act.wait_ge(q["vn"], h + 1)
                        if h == 0:
                            act.wait_ge(out_done, stored)
                        for b in range(SH, NB):
                            last = act.activation(vb[A, h, b, :], vnew[A, h, :], ACT.Copy,
                                                  scale=dec[A, h, NS * b + NS - 1:NS * b + NS])
                        last.then_inc(q["vb1"], 1)

                @block.vector
                def _(dve):
                    for h in range(H):
                        dve.scalar_tensor_tensor(out=dec[A, h, :], in0=Y[A, h, SEQ:TOK],
                                                 scalar=TOKS[A, NCH, 0, h:h + 1], in1=MASKS[A], op0=ALU.add,
                                                 op1=ALU.add).then_inc(q["arg"], 1)
                    dve.tensor_copy(T[A].rearrange("p a b c -> p (a b) c"),
                                    IDENT[A, A].unsqueeze(1).to_broadcast([SAMP, 2 * H, SAMP])
                                    ).then_inc(q["tinit"], 1)
                    for h in range(H):
                        dve.wait_ge(q["dec"], h + 1)
                        dve.wait_ge(q["kq"], h + 1)
                        dve.tensor_tensor(ka[A, h], BANK[h][A, 256:384].rearrange("p (a b) -> p a b", a=2),
                                          dec[A, h, :].unsqueeze(1).to_broadcast([SAMP, 2, SAMP]),
                                          ALU.mult).then_inc(q["att"], 1)
                    dve.wait_ge(q["tinit"], 1)
                    for lv in range(SAMP_LEVELS):
                        for h in range(H):
                            dve.wait_ge(q["y"], lv * H + h + 1)
                            dve.scalar_tensor_tensor(out=Ys[A, h, :], in0=BANK[h][A, 0:SAMP],
                                                     scalar=TOKS[A, NCH, 1, h:h + 1], in1=MASKL[A, lv, A],
                                                     op0=ALU.mult, op1=ALU.mult).then_inc(q["ymask"], 1)
                        for h in range(H):
                            dve.wait_ge(q["d"], lv * H + h + 1)
                            if lv:
                                dve.wait_ge(q["t"], (lv - 1) * H + h + 1)
                            dve.tensor_tensor(T[A, h], T[A, h],
                                              BANK[h][A, 256:384].rearrange("p (a b) -> p a b", a=2),
                                              ALU.subtract).then_inc(q["t"], 1)
                    dve.wait_ge(q["eg"], 1)

                    def scale_products(h):
                        dve.wait_ge(q["ks"], h + 1)
                        dve.tensor_tensor(ksq[:, h].rearrange("p r (b t) -> p b r t", b=NB),
                                          BANK[h][:, 0:128].rearrange("p (b r t) -> p b r t", b=NB, r=2),
                                          eg[:, h, :].rearrange("p (b t) -> p b t", b=NB).unsqueeze(2)
                                          .to_broadcast([P, NB, 2, NS]), ALU.mult).then_inc(q["ksq"], 1)

                    def right_side(h):
                        dve.wait_ge(q["rt"], h + 1)
                        dve.wait_ge(q["tok"], 2 * h + 2)
                        dve.scalar_tensor_tensor(out=R[A, h, :], in0=BANK[h][A, 128:256],
                                                 scalar=TOKS[A, NCH, 3, h:h + 1], in1=vtok[A, h, :],
                                                 op0=ALU.mult, op1=ALU.add).then_inc(q["r"], 1)

                    def outputs(h):
                        dve.wait_ge(q["vn"], h + 1)
                        if h == 0:
                            dve.wait_ge(out_done, stored)
                        dve.tensor_tensor(vb[A, h, 0:SH], vnew[A, h, :].unsqueeze(1).to_broadcast([SAMP, SH, P]),
                                          dec[A, h, last_tok][:, 0:SH].unsqueeze(2).to_broadcast([SAMP, SH, P]),
                                          ALU.mult).then_inc(q["vb0"], 1)
                        dve.wait_ge(q["o"], h + 1)
                        dve.wait_ge(q["ksq"], h + 1)
                        dve.tensor_tensor(smp(3 * h + 1), ksq[:, h, 1, :], BANK[h][:, 384:448],
                                          ALU.add).then_inc(q["o_out"], 1)

                    def add_update(h, r):
                        dve.wait_ge(q["su"], updates(h, r))
                        dve.wait_ge(q["sdec"], updates(h, r))
                        dve.tensor_tensor(states(h, r), states(h, r),
                                          BANK[h][:, :].rearrange("p (b n) -> p b n", b=SH),
                                          ALU.add).then_inc(q["s_out"], 1)

                    for h in range(GROUP + 2):
                        scale_products(h)
                    for h in range(GROUP):
                        right_side(h)
                    for h in range(GROUP + 2, H):
                        scale_products(h)
                    for h in range(GROUP):
                        outputs(h)
                    for h in range(GROUP, H):
                        right_side(h)
                    for h in range(GROUP):
                        add_update(h, 0)
                    for h in range(GROUP, H):
                        outputs(h)
                    for h in range(GROUP):
                        add_update(h, 1)
                    for r in range(2):
                        for h in range(GROUP, H):
                            add_update(h, r)

                @block.tensor
                def _(pe):
                    for h in range(H):
                        pe.matmul(BANK[h][A, 256:384], smp(3 * h), BIG[:, 3 * h:3 * h + 2, SEQ:TOK], start=True,
                                  stop=True).then_inc(q["kq"], 1)
                    for h in range(H):
                        pe.wait_ge(q["att"], h + 1)
                        pe.transpose(BANK[h][A, 0:P], smp(3 * h), IDENT[:])
                        pe.transpose(BANK[h][A, P:2 * P], smp(3 * h + 2), IDENT[:]).then_inc(q["tr"], 1)
                    pe.wait_ge(q["tinit"], 1)
                    for lv in range(SAMP_LEVELS):
                        for h in range(H):
                            if lv:
                                pe.wait_ge(q["t"], (lv - 1) * H + h + 1)
                            else:
                                pe.wait_ge(q["tok"], 2 * h + 2)
                            pe.matmul(BANK[h][A, 0:SAMP], ka[A, h, 0, :], T[A, h, 0, :], start=True,
                                      stop=True).then_inc(q["y"], 1)
                        for h in range(H):
                            pe.wait_ge(q["ymask"], lv * H + h + 1)
                            pe.matmul(BANK[h][A, 256:320], T[A, h, 1, :], Ys[A, h, :], start=True, stop=True)
                            pe.matmul(BANK[h][A, 320:384], Ys[A, h, :], T[A, h, 1, :], start=True,
                                      stop=True).then_inc(q["d"], 1)

                    def state_products(h):
                        pe.wait_ge(q["t"], (SAMP_LEVELS - 1) * H + h + 1)
                        pe.wait_ge(sin[h], 32)
                        for b in range(NB):
                            last = pe.matmul(BANK[h][:, 16 * b:16 * b + 16], states(h, b // SH)[:, b % SH, :],
                                             BIG[:, 3 * h:3 * h + 2, SEQ + NS * b:SEQ + NS * (b + 1)],
                                             start=True, stop=True)
                        last.then_inc(q["ks"], 1)

                    def by_token(h):
                        pe.wait_ge(q["ksq"], h + 1)
                        pe.transpose(BANK[h][A, 128:256], ksq[:, h, 0, :], IDENT[:]).then_inc(q["rt"], 1)

                    def new_values(h):
                        pe.wait_ge(q["r"], h + 1)
                        pe.matmul(BANK[h][A, 256:384], T[A, h, 1, :], R[A, h, :], start=True,
                                  stop=True).then_inc(q["v"], 1)

                    def outputs(h):
                        pe.wait_ge(q["vn"], h + 1)
                        pe.matmul(BANK[h][:, 384:448], vnew[A, h, :], ka[A, h, 1, :], start=True,
                                  stop=True).then_inc(q["o"], 1)

                    def state_update(h, r):
                        if r:
                            pe.wait_ge(q["vb1"], h + 1)
                            pe.wait_ge(q["s_out"], updates(h, 0))
                        else:
                            pe.wait_ge(q["vb0"], h + 1)
                            pe.wait_ge(q["o_out"], h + 1)
                        pe.matmul(BANK[h][:, :], ktok[:, h, :], vb[:, h, SH * r:SH * (r + 1), :], start=True,
                                  stop=True).then_inc(q["su"], 1)

                    pe.wait_ge(q["pad"], 2)
                    for h in range(GROUP + 2):
                        state_products(h)
                    for h in range(GROUP):
                        by_token(h)
                    state_products(GROUP + 2)
                    for h in range(GROUP):
                        new_values(h)
                    state_products(GROUP + 3)
                    for h in range(GROUP):
                        outputs(h)
                    for h in range(GROUP, H):
                        by_token(h)
                    for h in range(GROUP):
                        state_update(h, 0)
                    for h in range(GROUP, H):
                        new_values(h)
                    for h in range(GROUP):
                        state_update(h, 1)
                    for h in range(GROUP, H):
                        outputs(h)
                    for r in range(2):
                        for h in range(GROUP, H):
                            state_update(h, r)

        def residual_phase(name, ph, rhs, res, chunks_per_tile=1, before=None):
            n = DT * chunks_per_tile
            kt = streams[ph][2]
            scr = Arena()
            scr(10 * TOK)
            sq = [scr(TOK) for _ in range(2)]
            chunk_done, added, squared, sum1, sum2 = phase_sems("res", ("chunk_done", "added", "squared", "summed",
                                                                        "sq_summed"))
            tiles = SLOTS // chunks_per_tile
            with nc.Block() as block:
                @block.sync
                def _(sync):
                    clear_stale(sync)
                    if before:
                        before.sync(sync)
                    load_weights(sync, ph, chunk_done)
                    sync.wait_ge(out_done, outs[0])

                @block.tensor
                def _(pe):
                    if before:
                        before.pe(pe)

                    def turn(i, made=0):
                        for s in range(made, SLOTS):
                            part, tile = s % chunks_per_tile, s // chunks_per_tile
                            pe.wait_ge(w_loaded[s], (i + uses[ph] + 1) * 16)
                            if part == 0:
                                pe.wait_ge(added, i * (2 * tiles) + 2 * tile + 2)
                            product(pe, BANK[tile % 2 * 2:], s, rhs, range(part * kt, part * kt + kt),
                                    part == 0, part == chunks_per_tile - 1,
                                    before.tile_ready if before and s == 0 else None).then_inc(chunk_done, 1)

                    if chunks_per_tile > 1:
                        pe.sem_inc(chunk_done, 1)
                        turn(0, 1)
                    with pe.Fori(1 if chunks_per_tile > 1 else 0, n // SLOTS) as i:
                        turn(i)

                @block.gpsimd
                def _(pool):
                    if before:
                        before.pool(pool)
                    pool.memset(stats[:, 0:2, :], 0.0).then_inc(sum1, 1)
                    pool.wait_ge(sum1, 1)
                    with pool.Fori(0, n // SLOTS) as i:
                        for t in range(tiles):
                            m = i * tiles + t
                            pool.wait_ge(added, m * 2 + 6)
                            pool.wait_ge(sum1, m + 1)
                            pool.tensor_tensor(sum_y, sum_y, Y[:, bass.ds(m, 1), :].rearrange("p o t -> p (o t)"),
                                               ALU.add).then_inc(sum1, 1)

                @block.scalar
                def _(act):
                    act.sem_inc(squared, 2)
                    if before:
                        before.act(act)
                    with act.Fori(0, n // SLOTS) as i:
                        for t in range(tiles):
                            m = i * tiles + t
                            act.wait_ge(added, m * 2 + 6)
                            act.wait_ge(sum2, m + 1)
                            act.activation(sq[t % 2], Y[:, bass.ds(m, 1), :].rearrange("p o t -> p (o t)"),
                                           ACT.Square).then_inc(squared, 1)

                @block.vector
                def _(dve):
                    dve.sem_inc(added, 4)
                    dve.sem_inc(sum2, 2)
                    if before:
                        before.dve(dve)
                    dve.wait_ge(sum1, 1)

                    def square_sum(m, t):
                        dve.wait_ge(squared, m + 3)
                        dve.wait_ge(sum2, m + 2)
                        dve.tensor_tensor(sum_sq, sum_sq, sq[t % 2], ALU.add).then_inc(sum2, 1)

                    with dve.Fori(0, n // SLOTS) as i:
                        for t in range(tiles):
                            dve.wait_ge(chunk_done, i * SLOTS + (t + 1) * chunks_per_tile)
                            m = i * tiles + t
                            for half in range(2):
                                cols = slice(half * HALF, (half + 1) * HALF)
                                dve.scalar_tensor_tensor(
                                    out=Y[:, bass.ds(m, 1), cols].rearrange("p o t -> p (o t)"),
                                    in0=res[:, bass.ds(m, 1), cols].rearrange("p o t -> p (o t)"), scalar=ALPHA,
                                    in1=BANK[t % 2 * 2 + half][:, 0:HALF], op0=ALU.mult,
                                    op1=ALU.add).then_inc(added, 1)
                            square_sum(m, t)

        class LayerNorm:
            DVE_TILES = 2

            def __init__(self, which, out):
                self.which, self.out = which, out
                (self.sums, self.mu_done, self.var, self.std_done, self.rec, self.cen, self.nrm, self.ready) = (
                    phase_sems("ln", ("sums", "mu_done", "var", "std_done", "rec", "centred", "normed", "ready")))

            def sync(self, sync):
                pass

            def tile_ready(self, pe, k):
                pe.wait_ge(self.ready, k + 1)

            def pe(self, pe):
                for n, total in enumerate((sum_y, sum_sq)):
                    for half in range(2):
                        last = pe.matmul(BANK[4 + 2 * n + half][:, 0:HALF], ONES[:],
                                         total[:, half * HALF:(half + 1) * HALF], start=True, stop=True)
                    last.then_inc(self.sums, 1)

            def act(self, act):
                act.wait_ge(self.sums, 1)
                for half in range(2):
                    act.activation(rs[:, half * HALF:(half + 1) * HALF], BANK[4 + half][:, 0:HALF], ACT.Square,
                                   scale=1.0 / D).then_inc(self.mu_done, 1)
                for half in range(2):
                    act.activation(mu[:, half * HALF:(half + 1) * HALF], BANK[4 + half][:, 0:HALF], ACT.Copy,
                                   scale=1.0 / D).then_inc(self.mu_done, 1)
                act.wait_ge(self.var, 3)
                act.activation(rs, rs, ACT.Sqrt, bias=eps_ln).then_inc(self.std_done, 1)
                for k in range(DT):
                    act.wait_ge(self.nrm, k + 1)
                    act.activation(self.out[:, k, :], Y[:, k, :], ACT.Identity, bias=lnp[:, self.which + 1, k:k + 1],
                                   scale=lnp[:, self.which, k:k + 1]).then_inc(self.ready, 1)

            def pool(self, pool):
                pool.wait_ge(self.mu_done, 4)
                for k in range(self.DVE_TILES, DT):
                    pool.tensor_tensor(Y[:, k, :], Y[:, k, :], mu, ALU.subtract).then_inc(self.cen, 1)

            def dve(self, dve):
                dve.wait_ge(self.sums, 2)
                for half in range(2):
                    cols = slice(half * HALF, (half + 1) * HALF)
                    dve.wait_ge(self.mu_done, half + 1)
                    dve.scalar_tensor_tensor(out=rs[:, cols], in0=BANK[6 + half][:, 0:HALF], scalar=1.0 / D,
                                             in1=rs[:, cols], op0=ALU.mult, op1=ALU.subtract).then_inc(self.var, 1)
                dve.wait_ge(self.var, 2)
                dve.tensor_scalar(rs, rs, 0.0, None, ALU.max).then_inc(self.var, 1)
                dve.wait_ge(self.mu_done, 4)
                for k in range(self.DVE_TILES):
                    dve.tensor_tensor(Y[:, k, :], Y[:, k, :], mu, ALU.subtract).then_inc(self.rec, 1)
                dve.wait_ge(self.std_done, 1)
                dve.reciprocal(rs, rs).then_inc(self.rec, 1)
                dve.wait_ge(self.rec, self.DVE_TILES + 1)
                for k in range(DT):
                    if k >= self.DVE_TILES:
                        dve.wait_ge(self.cen, k - self.DVE_TILES + 1)
                    dve.tensor_tensor(Y[:, k, :], Y[:, k, :], rs, ALU.mult).then_inc(self.nrm, 1)

        class GatedNorm:
            def __init__(self):
                self.sq_done, self.summed, self.std, self.rec, self.bcast, self.gated, self.ready = (
                    sem(f"rms_{x}") for x in ("sq_done", "summed", "std", "rec", "bcast", "gated", "ready"))
                self.sel_in = sem("rms_select_in")
                scr = Arena()
                self.sq = [scr(TOK) for _ in range(4)]
                self.rstd = scr(TOK)
                self.sel = scr(H, P)
                self.clr = sem("rms_cleared")

            def tile_ready(self, pe, k):
                pe.wait_ge(self.ready, k + 1)

            def sync(self, sync):
                sync.dma_start(self.sel, I["select"][:, 0:H]).then_inc(self.sel_in, 16)

            def pe(self, pe):
                for h in range(H):
                    pe.wait_ge(self.sq_done, h + 1)
                    for half in range(2):
                        last = pe.matmul(BANK[6 + half][0:H, 0:HALF], sum_column(h, H),
                                         self.sq[h % 4][:, half * HALF:(half + 1) * HALF], start=h == 0,
                                         stop=h == H - 1)
                    last.then_inc(self.summed, 1)
                pe.wait_ge(self.rec, 1)
                pe.wait_ge(self.sel_in, 16)
                for h in range(H):
                    b = h % 3 * 2 + 2
                    if h >= 3:
                        pe.wait_ge(self.ready, h - 2)
                    for half in range(2):
                        last = pe.matmul(BANK[b + half][:, 0:HALF], self.sel[:, h, :],
                                         self.rstd[:, half * HALF:(half + 1) * HALF], start=True, stop=True)
                    last.then_inc(self.bcast, 1)

            def act(self, act):
                for h in range(H):
                    if h >= 4:
                        act.wait_ge(self.summed, h - 3)
                    act.activation(self.sq[h % 4], BIG[:, 3 * h + 1, :], ACT.Square).then_inc(self.sq_done, 1)
                act.wait_ge(self.summed, H)
                act.wait_ge(self.clr, 1)
                for half in range(2):
                    act.activation(self.rstd[0:H, half * HALF:(half + 1) * HALF], BANK[6 + half][0:H, 0:HALF],
                                   ACT.Sqrt, bias=eps_rms[0:H], scale=1.0 / P).then_inc(self.std, 1)

            def pool(self, pool):
                pool.memset(self.rstd, 0.0).then_inc(self.clr, 1)

            def dve(self, dve):
                for h in range(H):
                    o = BIG[:, 3 * h + 1, :]
                    dve.wait_ge(self.sq_done, h + 1)
                    dve.scalar_tensor_tensor(out=o, in0=o, scalar=norm_g, in1=Z[:, h, :], op0=ALU.mult,
                                             op1=ALU.mult).then_inc(self.gated, 1)
                dve.wait_ge(self.std, 2)
                dve.reciprocal(self.rstd[0:H], self.rstd[0:H]).then_inc(self.rec, 1)
                dve.wait_ge(self.gated, H)
                for h in range(H):
                    dve.wait_ge(self.bcast, h + 1)
                    for half in range(2):
                        o = BIG[:, 3 * h + 1, half * HALF:(half + 1) * HALF]
                        last = dve.tensor_tensor(o, o, BANK[h % 3 * 2 + 2 + half][:, 0:HALF], ALU.mult)
                    last.then_inc(self.ready, 1)

        def ffn_up(ph, x, layer, before):
            W, n, hist = 3, 2 * FT, 2
            scr = Arena()
            ext = [scr(ext_cols(W)) for _ in range(SLOTS)]
            y = [scr(ext_cols(W)) for _ in range(SLOTS)]
            state, new_state = scr(n, NB * hist), scr(n, (NB + 1) * hist)
            cw = scr(n, W)
            chunk_done, filled, tap_done, conv_done, silu_done, gated, hist_in, saved, st_in, pads = (
                phase_sems("up", ("chunk_done", "ext_filled", "tap_done", "conv_done", "silu_done",
                                  "gated", "hist_in", "saved", "state_in", "pads_zero")))
            cols = SEQ + hist + NB * (hist + NS)
            with nc.Block() as block:
                @block.sync
                def _(sync):
                    clear_stale(sync)
                    sync.dma_start(state, I[f"st_ffn{layer}"]).then_inc(st_in, 16)
                    sync.dma_start(cw, I[f"cw_ffn{layer}"]).then_inc(st_in, 16)
                    load_weights(sync, ph, chunk_done)
                    sync.wait_ge(saved, 8 + 2 * n)
                    store(sync, O[f"ffn_conv{layer}"], new_state)
                    sync.wait_ge(out_done, outs[0])

                @block.tensor
                def _(pe):
                    before.pe(pe)
                    with pe.Fori(0, n // SLOTS) as i:
                        for s in range(SLOTS):
                            g = i * SLOTS + s
                            pe.wait_ge(w_loaded[s], (i + uses[ph] + 1) * 16)
                            pe.wait_ge(filled, g * 3 + 3)
                            product(pe, BANK[s % 2 * 2:], s, x_half(x), range(8), True, True,
                                    before.tile_ready if s == 0 else None).then_inc(chunk_done, 1)
                    pe.wait_ge(w_loaded[0], (uses[ph + 1] + 1) * 16)
                    pe.wait_ge(filled, 3 * n + 3)
                    pe.wait_ge(gated, 4 + 2 * (FT // 2))
                    product(pe, BANK, 0, x_half(BIG), range(FT // 2), True, False)

                @block.scalar
                def _(act):
                    act.sem_inc(filled, 6)
                    before.act(act)
                    with act.Fori(0, n // SLOTS) as i:
                        for s in range(SLOTS):
                            g = i * SLOTS + s
                            act.wait_ge(chunk_done, g + 1)
                            act.wait_ge(conv_done, g + 1)
                            act.wait_ge(saved, g * 2 + 2)
                            fill_ext(act, BANK[s % 2 * 2:], ext[s], hist, filled)
                            if s % 2:
                                act.wait_ge(conv_done, g + 5)
                                act.activation(y[s][:, 0:cols - hist], y[s][:, 0:cols - hist],
                                               ACT.Silu).then_inc(silu_done, 1)

                @block.gpsimd
                def _(pool):
                    for s in range(SLOTS):
                        pool.memset(ext[s][:, 0:hist], 0.0).then_inc(pads, 1)
                    pool.sem_inc(saved, 8)
                    before.pool(pool)
                    pool.wait_ge(st_in, 32)
                    with pool.Fori(0, n // SLOTS) as i:
                        for s in range(SLOTS):
                            pool.wait_ge(conv_done, i * SLOTS + s + 1)
                            pool.wait_ge(saved, (i * SLOTS + s) * 2 + 2)
                            history_in(pool, ext[s], state, i * SLOTS + s, hist, hist_in)
                        for s in range(SLOTS):
                            pool.wait_ge(filled, (i * SLOTS + s) * 3 + 9)
                            history_out(pool, ext[s], new_state, i * SLOTS + s, hist, saved)

                @block.vector
                def _(dve):
                    dve.sem_inc(conv_done, 4)
                    dve.sem_inc(gated, 4)
                    before.dve(dve)
                    dve.wait_ge(st_in, 32)
                    dve.wait_ge(pads, SLOTS)
                    with dve.Fori(0, n // SLOTS) as i:
                        for pair in range(2):
                            for s in (2 * pair, 2 * pair + 1):
                                g = i * SLOTS + s
                                dve.wait_ge(filled, g * 3 + 9)
                                dve.wait_ge(hist_in, g + 1)
                                dve.wait_ge(gated, i * 4 + 2 * pair + 2)
                                tap_run(dve, ext[s], y[s],
                                        lambda j: cw[:, bass.ds(g, 1), j:j + 1].rearrange("p o t -> p (o t)"),
                                        W, g, tap_done, conv_done)
                            dve.wait_ge(conv_done, i * SLOTS + 2 * pair + 6)
                            dve.wait_ge(silu_done, i * 2 + pair + 1)
                            hid = BIG[:, bass.ds(i * 2 + pair, 1), :].rearrange("p o t -> p (o t)")
                            a, b = y[2 * pair], y[2 * pair + 1]
                            dve.tensor_tensor(hid[:, 0:SEQ], a[:, 0:SEQ], b[:, 0:SEQ], ALU.mult).then_inc(gated, 1)

                            def smp(v):
                                return v[:, SEQ + hist:cols].rearrange("p (b t) -> p b t", b=NB)[:, :, 0:NS]
                            dve.tensor_tensor(hid[:, SEQ:TOK].rearrange("p (b t) -> p b t", b=NB), smp(a), smp(b),
                                              ALU.mult).then_inc(gated, 1)

        def ple_phase(ph, x, out, layer, before):
            scr = Arena()
            pe_in = scr(PLE_T, TOK)
            sg = [scr(TOK) for _ in range(2)]
            chunk_done, sig, prod, added, p_in = (
                phase_sems("ple", ("chunk_done", "sigmoid", "product", "added", "p_in")))
            with nc.Block() as block:
                @block.sync
                def _(sync):
                    clear_stale(sync)
                    sync.dma_start(pe_in, I[f"p{layer}"]).then_inc(p_in, 16)
                    load_weights(sync, ph, chunk_done)
                    if layer == 1:
                        for part in range(2):
                            sync.wait_ge(added, 2 + (part + 1) * (DT // 2))
                            tiles = slice(part * (DT // 2), (part + 1) * (DT // 2))
                            store(sync, O["y"][:, tiles], out[:, tiles, :])

                @block.tensor
                def _(pe):
                    before.pe(pe)
                    pe.wait_ge(p_in, 16)
                    with pe.Fori(0, DT // SLOTS) as i:
                        for s in range(SLOTS):
                            g = i * SLOTS + s
                            b = s % 2 * 4
                            pe.wait_ge(w_loaded[s], (i + uses[ph] + 1) * 16)
                            pe.wait_ge(sig, g * 2 + 2)
                            pe.wait_ge(prod, g * 2 + 2)
                            for n in range(PLE_T):
                                for half in range(2):
                                    pe.matmul(BANK[b + 2 + half][:, 0:HALF], tile_w(s, DT + n),
                                              x_half(pe_in)(n, half), start=n == 0, stop=n == PLE_T - 1)
                            product(pe, BANK[b:], s, x_half(x), range(8), True, True,
                                    before.tile_ready if s == 0 else None).then_inc(chunk_done, 1)

                @block.scalar
                def _(act):
                    act.sem_inc(sig, 4)
                    before.act(act)
                    with act.Fori(0, DT // SLOTS) as i:
                        for s in range(SLOTS):
                            g = i * SLOTS + s
                            act.wait_ge(chunk_done, g + 1)
                            act.wait_ge(added, g + 1)
                            for half in range(2):
                                act.activation(sg[s % 2][:, half * HALF:(half + 1) * HALF],
                                               BANK[s % 2 * 4 + half][:, 0:HALF], ACT.Sigmoid).then_inc(sig, 1)

                @block.gpsimd
                def _(pool):
                    before.pool(pool)

                @block.vector
                def _(dve):
                    dve.sem_inc(prod, 4)
                    dve.sem_inc(added, 2)
                    before.dve(dve)
                    with dve.Fori(0, DT // SLOTS) as i:
                        for s in range(SLOTS):
                            g = i * SLOTS + s
                            dve.wait_ge(sig, g * 2 + 6)
                            for half in range(2):
                                cols = slice(half * HALF, (half + 1) * HALF)
                                dve.tensor_tensor(sg[s % 2][:, cols], sg[s % 2][:, cols],
                                                  BANK[s % 2 * 4 + 2 + half][:, 0:HALF], ALU.mult).then_inc(prod, 1)
                            dve.wait_ge(prod, g * 2 + 6)
                            dve.tensor_tensor(out[:, bass.ds(g, 1), :].rearrange("p o t -> p (o t)"),
                                              x[:, bass.ds(g, 1), :].rearrange("p o t -> p (o t)"), sg[s % 2],
                                              ALU.add).then_inc(added, 1)

        def shortconv_phase(ph, x):
            W, n, hist = 3, 3 * DT, 2
            group = 12
            scr = Arena()
            ext = [scr(ext_cols(W)) for _ in range(2)]
            y = [scr(ext_cols(W)) for _ in range(2)]
            cs = [scr(TOK) for _ in range(2)]
            state, new_state = scr(DT, NB * hist), scr(DT, (NB + 1) * hist)
            cw = scr(DT, W)
            chunk_done, c_out, ch_out, tap_done, conv_done, b_out, hist_in, saved, st_in, pads = (
                sem(f"sc_{y}") for y in ("chunk_done", "c_out", "ch_out", "tap_done", "conv_done", "b_out",
                                         "hist_in", "saved", "state_in", "pads_zero"))
            cols = SEQ + hist + NB * (hist + NS)
            with nc.Block() as block:
                @block.sync
                def _(sync):
                    clear_stale(sync)
                    sync.dma_start(state, I["st_sc"]).then_inc(st_in, 16)
                    sync.dma_start(cw, I["cw_sc"]).then_inc(st_in, 16)
                    load_weights(sync, ph, chunk_done)
                    sync.wait_ge(saved, 4 + 2 * DT)
                    store(sync, O["sc_conv"], new_state)
                    sync.wait_ge(out_done, outs[0])

                @block.tensor
                def _(pe):
                    with pe.Fori(0, n // group) as i:
                        for j in range(group):
                            s, t, r = j % SLOTS, j // 3, j % 3
                            m = i * (group // 3) + t
                            pe.wait_ge(w_loaded[s], (i * (group // SLOTS) + (uses[ph] + j // SLOTS + 1)) * 16)
                            if r == 0:
                                pe.wait_ge(c_out, m * 2 + 2)
                            elif r == 1:
                                pe.wait_ge(ch_out, m * 3 + 3)
                            else:
                                pe.wait_ge(b_out, m * 3 + 3)
                            product(pe, BANK[2 * r:], s, x_half(x), range(8), True, True).then_inc(chunk_done, 1)

                @block.scalar
                def _(act):
                    act.sem_inc(c_out, 2)
                    with act.Fori(0, DT // 2) as i:
                        for t in range(2):
                            m = i * 2 + t
                            act.wait_ge(chunk_done, m * 3 + 1)
                            act.wait_ge(ch_out, m * 3 + 3 - (0 if t else 0))
                            for half in range(2):
                                act.activation(cs[t][:, half * HALF:(half + 1) * HALF], BANK[half][:, 0:HALF],
                                               ACT.Copy).then_inc(c_out, 1)

                @block.gpsimd
                def _(pool):
                    for s in range(2):
                        pool.memset(ext[s][:, 0:hist], 0.0).then_inc(pads, 1)
                    pool.sem_inc(saved, 4)
                    pool.wait_ge(st_in, 32)
                    with pool.Fori(0, DT // 2) as i:
                        for s in range(2):
                            m = i * 2 + s
                            pool.wait_ge(conv_done, m + 1)
                            pool.wait_ge(saved, m * 2 + 2)
                            history_in(pool, ext[s], state, m, hist, hist_in)
                        for s in range(2):
                            m = i * 2 + s
                            pool.wait_ge(ch_out, m * 3 + 6)
                            history_out(pool, ext[s], new_state, m, hist, saved)

                @block.vector
                def _(dve):
                    dve.sem_inc(ch_out, 3)
                    dve.sem_inc(b_out, 3)
                    dve.sem_inc(conv_done, 2)
                    dve.wait_ge(st_in, 32)
                    dve.wait_ge(pads, 2)
                    with dve.Fori(0, DT // 2) as i:
                        for t in range(2):
                            m = i * 2 + t
                            dve.wait_ge(chunk_done, m * 3 + 2)
                            dve.wait_ge(c_out, m * 2 + 4)
                            dve.wait_ge(conv_done, m + 1)
                            dve.wait_ge(saved, m * 2 + 2)
                            e = ext[t]
                            dve.tensor_tensor(e[:, hist:hist + HALF], cs[t][:, 0:HALF], BANK[2][:, 0:HALF],
                                              ALU.mult).then_inc(ch_out, 1)
                            dve.tensor_tensor(e[:, hist + HALF:hist + SEQ], cs[t][:, HALF:SEQ],
                                              BANK[3][:, 0:SEQ - HALF], ALU.mult).then_inc(ch_out, 1)
                            dve.tensor_tensor(sample_part(e, hist)[:, :, hist:],
                                              cs[t][:, SEQ:TOK].rearrange("p (b t) -> p b t", b=NB),
                                              BANK[3][:, SEQ - HALF:HALF].rearrange("p (b t) -> p b t", b=NB),
                                              ALU.mult).then_inc(ch_out, 1)
                            dve.wait_ge(ch_out, m * 3 + 6)
                            dve.wait_ge(hist_in, m + 1)
                            dve.wait_ge(b_out, m * 3 + 3)
                            tap_run(dve, e, y[t],
                                    lambda j: cw[:, bass.ds(m, 1), j:j + 1].rearrange("p o t -> p (o t)"),
                                    W, m, tap_done, conv_done)
                            dve.wait_ge(conv_done, m + 3)
                            dve.wait_ge(chunk_done, m * 3 + 3)
                            out = BIG[:, bass.ds(m, 1), :].rearrange("p o t -> p (o t)")
                            dve.tensor_tensor(out[:, 0:HALF], y[t][:, 0:HALF], BANK[4][:, 0:HALF],
                                              ALU.mult).then_inc(b_out, 1)
                            dve.tensor_tensor(out[:, HALF:SEQ], y[t][:, HALF:SEQ], BANK[5][:, 0:SEQ - HALF],
                                              ALU.mult).then_inc(b_out, 1)
                            dve.tensor_tensor(out[:, SEQ:TOK].rearrange("p (b t) -> p b t", b=NB),
                                              y[t][:, SEQ + hist:cols].rearrange("p (b t) -> p b t", b=NB)[:, :, 0:NS],
                                              BANK[5][:, SEQ - HALF:HALF].rearrange("p (b t) -> p b t", b=NB),
                                              ALU.mult).then_inc(b_out, 1)

        qkv_phase(0)
        gate_phase()
        block_inverses()
        delta_prompt()
        delta_sample()
        residual_phase("dout", 2, lambda k, half: BIG[:, 3 * k + 1, half * HALF:(half + 1) * HALF], X,
                       before=GatedNorm())
        ffn_up(3, X, 0, LayerNorm(0, X))
        residual_phase("down0", 4, x_half(BIG), X, 2)
        ple_phase(5, X, Z, 0, LayerNorm(2, X))
        shortconv_phase(6, Z)
        residual_phase("scout", 7, x_half(BIG), Z)
        ffn_up(8, Z, 1, LayerNorm(4, Z))
        residual_phase("down1", 9, x_half(BIG), Z, 2)
        ple_phase(10, Z, X, 1, LayerNorm(6, Z))
        with nc.Block() as block:
            @block.sync
            def _(sync):
                sync.wait_ge(out_done, outs[0])


_OUTS = {"y": (P, DT, TOK), "dn_conv": (P, QKV_T, 27), "dn_S_prompt": (P, H, P), "dn_S_sample": (H, P, NB, P),
         "sc_conv": (P, DT, 18), "ffn_conv0": (P, 2 * FT, 18), "ffn_conv1": (P, 2 * FT, 18)}


def _tiles(w, kt):
    import numpy as np
    K, N = w.shape
    a = w.reshape(K // (kt * P), kt, P, N // P, P).transpose(3, 0, 2, 1, 4)
    return np.ascontiguousarray(a.reshape(-1, P, kt * P))


def _cols(v):
    import numpy as np
    a = np.asarray(v)
    a = a.reshape(a.shape[:-1] + (a.shape[-1] // P, P))
    return np.ascontiguousarray(np.moveaxis(a, (-1, -2), (0, 1)))


def kernel(**inputs):
    import numpy as np
    import concourse.bacc as bacc
    from concourse.bass_utils import run_bass_kernel_spmd

    a = {k: np.asarray(v) for k, v in inputs.items()}
    f32 = np.float32

    def feat(prompt, sample, n):
        rows = np.concatenate([prompt.reshape(SEQ, -1), sample.reshape(SAMP, -1)])
        return np.ascontiguousarray(rows.T.reshape(n, P, TOK).transpose(1, 0, 2))

    def state(s, order):
        t = _cols(s)[:, order]
        return np.ascontiguousarray(t.reshape(P, len(order), -1))

    w_in = a["dn_w_in"][0]
    qkv_order = [x * H + h for h in range(H) for x in (1, 0, 2)]
    up_order = [x * FT + t for t in range(FT) for x in range(2)]
    sc_order = [x * DT + t for t in range(DT) for x in (1, 2, 0)]
    m = {"x": feat(a["x_prompt"], a["x_sample"], DT)}
    m["w_qkv"] = _tiles(w_in[:, :QKV_T * P], 8)[qkv_order]
    m["w_z"] = _tiles(w_in[:, QKV_T * P:4 * D], 8)
    ba = np.zeros((D, 40), f32)
    ba[:, 0:H] = w_in[:, 4 * D:4 * D + H]
    ba[:, A_ROW:] = w_in[:, 4 * D + H:]
    m["w_ba"] = np.ascontiguousarray(ba.reshape(DT, P, 40).transpose(1, 0, 2))
    m["w_dout"] = _tiles(a["dn_w_out"][0], 8)
    m["w_scin"] = _tiles(a["sc_w_in"][0], 8)[sc_order]
    m["w_scout"] = _tiles(a["sc_w_out"][0], 8)
    for l in range(2):
        m[f"w_up{l}"] = _tiles(a["ffn_w_up"][l], 8)[up_order]
        m[f"w_down{l}"] = _tiles(a["ffn_w_down"][l], 11)
        m[f"w_ple{l}"] = np.ascontiguousarray(np.concatenate(
            [_tiles(a["ple_w_gate"][l], 8), _tiles(a["ple_w_proj"][l], PLE_T)], axis=2))
        m[f"p{l}"] = feat(a["p_prompt"][l], a["p_sample"][l], PLE_T)
        m[f"st_ffn{l}"] = state(a["state_ffn_conv"][l], up_order)
        m[f"cw_ffn{l}"] = np.ascontiguousarray(_cols(a["ffn_conv_w"][l])[:, up_order])
    m["st_dn"] = state(a["state_dn_conv"][0], qkv_order)
    m["cw_dn"] = np.ascontiguousarray(_cols(a["dn_conv_w"][0])[:, qkv_order])
    m["st_sc"] = state(a["state_sc_conv"][0], list(range(DT)))
    m["cw_sc"] = _cols(a["sc_conv_w"][0])
    m["st_S"] = np.ascontiguousarray(a["state_dn_S"][0].transpose(1, 2, 0, 3))
    i, j = np.indices((P, P))
    m["mask_decay"] = np.where(j >= i, 0.0, -1e30).astype(f32)
    m["mask_sample"] = np.where((j >= i) & (j // NS == i // NS), 0.0, -1e30).astype(f32)[:, :SAMP].copy()
    m["mask_levels"] = np.ascontiguousarray(np.stack(
        [((i // s // 2 == j // s // 2) & (i // s % 2 == 1) & (j // s % 2 == 0)) for s in
         [1 << lv for lv in range(SAMP_LEVELS)] + [BL << lv for lv in range(LEVELS)]], axis=1).astype(f32))
    m["identity"] = np.eye(P, dtype=f32)
    m["ones"] = np.ones((P, P), f32)
    sel = np.zeros((P, 2 * H, P), f32)
    for n in range(2 * H):
        sel[n, n] = 1.0
    for h in range(H):
        sel[A_ROW + h, H + h] = 1.0
    m["select"] = sel
    keep = np.ones((H, TOK), f32)
    keep[:, 0:SEQ:CH] = 0.0
    keep[:, SEQ::NS] = 0.0
    m["keep"] = keep
    cv = np.zeros((P, 160), f32)
    for l in range(2):
        for n, name in enumerate(("ln_mix_g", "ln_mix_b", "ln_ffn_g", "ln_ffn_b")):
            at = (4 * l + n) * DT
            cv[:, at:at + DT] = _cols(a[name][l])
    cv[:, 64] = a["dn_norm_g"][0]
    cv[:, 65:69] = [1e-5, 1e-6, 1e-6, 128e-6]
    cv[A_ROW:A_ROW + H, 69] = a["dn_a_log"][0]
    cv[A_ROW:A_ROW + H, 70] = a["dn_dt_bias"][0]
    cv[0:2 * H, 72] = [1.0, 128.0] * H
    cv[0:2 * H, 73] = [1e-6, 128e-6] * H
    cv[:, 95] = 1.0
    m["columns"] = cv

    nc = bacc.Bacc("TRN2", target_bir_lowering=False, num_devices=1)
    I = {k: nc.dram_tensor(f"in_{k}", v.shape, F32, kind="ExternalInput").ap() for k, v in m.items()}
    O = {k: nc.dram_tensor(f"out_{k}", s, F32, kind="ExternalOutput").ap() for k, s in _OUTS.items()}
    build(nc, I, O)
    r = run_bass_kernel_spmd(nc, [{f"in_{k}": np.ascontiguousarray(v) for k, v in m.items()}], core_ids=[0])
    got = {k: np.asarray(r.results[0][f"out_{k}"]) for k in _OUTS}

    y = got["y"].transpose(1, 0, 2).reshape(D, TOK).T

    def rows(s, order, hist):
        t = np.empty_like(s)
        t[:, order] = s
        t = t.transpose(2, 1, 0).reshape(NB + 1, hist, -1)
        return t[0:1], t[1:]

    dn = rows(got["dn_conv"], qkv_order, 3)
    sc = rows(got["sc_conv"], list(range(DT)), 2)
    ff = [rows(got[f"ffn_conv{l}"], up_order, 2) for l in range(2)]
    S_prompt = got["dn_S_prompt"].transpose(1, 0, 2)[None, None]
    S_sample = got["dn_S_sample"].transpose(2, 0, 1, 3)[None]
    return (y[:SEQ].reshape(1, SEQ, D).copy(), y[SEQ:].reshape(NB, NS, D).copy(), dn[0][None], S_prompt.copy(),
            sc[0][None], np.stack([f[0] for f in ff]), dn[1][None], S_sample.copy(), sc[1][None],
            np.stack([f[1] for f in ff]))
```

```python
from contextlib import ExitStack

import concourse.bass as bass
from concourse import mybir

F32 = mybir.dt.float32
ACT = mybir.ActivationFunctionType
ALU = mybir.AluOpType

P = 128
D = 1024
DT = D // P
SEQ = 512
NB, NS = 8, 8
SAMP = NB * NS
TOK = SEQ + SAMP
HALF = TOK // 2
H = 8
QKV_T = 3 * H
FF = 2816
FT = FF // P
PLE_T = 2
CH = 128
NCH = SEQ // CH
BL = 32
NBL = CH // BL
LEVELS, SAMP_LEVELS = 2, 3
SLOTS = 4
WCOLS = 11 * P
ALPHA = 4.0 ** 0.25
SCR_COLS = 16448
X_PARTS = 4
A_ROW = 32


def ext_cols(width):
    return (width - 1) + SEQ + NB * (width - 1 + NS)


def build(nc, I, O):
    with ExitStack() as ctx:
        def sb(name, shape):
            return ctx.enter_context(nc.sbuf_tensor(name, shape, F32))

        def sem(name):
            return ctx.enter_context(nc.semaphore(name))

        shared = {}

        in_use, stale = [], []

        def phase_sems(kind, names):
            if kind not in shared:
                shared[kind] = [sem(f"{kind}_{x}") for x in names]
            assert kind not in stale
            in_use.append(kind)
            return shared[kind]

        def clear_stale(sync):
            for kind in stale:
                for x in shared[kind]:
                    sync.sem_clear(x)
            stale[:] = in_use
            in_use.clear()

        X = sb("x", [P, DT, TOK])
        Y = sb("y", [P, DT, TOK])
        Z = sb("z", [P, DT, TOK])
        BIG = sb("big", [P, QKV_T, TOK])
        RING = sb("ring", [P, SLOTS, WCOLS])
        SCR = sb("scratch", [P, SCR_COLS])
        MASKT = sb("mask_decay", [P, P])
        MASKS = sb("mask_decay_sample", [P, SAMP])
        MASKL = sb("mask_levels", [P, SAMP_LEVELS + LEVELS, P])
        IDENT = sb("identity", [P, P])
        ONES = sb("ones", [P, P])
        CV = sb("column_constants", [P, 160])
        TOKS = sb("token_scalars", [P, NCH + 1, 4, H])
        BANK = [ctx.enter_context(nc.psum_tensor(f"bank{i}", [P, 512], F32)) for i in range(8)]

        class Arena:
            def __init__(self):
                self.at = 0

            def __call__(self, *dims):
                n = 1
                for d in dims:
                    n *= d
                a = SCR[:, self.at:self.at + n]
                self.at += n
                assert self.at <= SCR_COLS, self.at
                if len(dims) == 1:
                    return a
                names = "abcd"[:len(dims)]
                return a.rearrange(f"p ({' '.join(names)}) -> p {' '.join(names)}",
                                   **{n: d for n, d in zip(names, dims)})

        stats = SCR[:, SCR_COLS - 4 * TOK:].rearrange("p (s t) -> p s t", s=4)
        sum_y, sum_sq, mu, rs = (stats[:, n, :] for n in range(4))
        TD = SCR[:, SCR_COLS - 2 * BL * BL:].rearrange("p (a b c) -> p a b c", a=2, b=BL)

        S = SCR[:, SCR_COLS - 2 * BL * BL - H * P:SCR_COLS - 2 * BL * BL].rearrange("p (h n) -> p h n", h=H)

        lnp = CV[:, 0:64].rearrange("p (k t) -> p k t", k=8)
        norm_g = CV[:, 64:65]
        eps_ln, eps_rms, eps_l2, eps_l2q = (CV[:, 65 + i:66 + i] for i in range(4))
        a_log = CV[A_ROW:A_ROW + H, 69:70]
        dt_bias = CV[A_ROW:A_ROW + H, 70:71]
        neg_ea = CV[A_ROW:A_ROW + H, 71:72]
        l2_scale, l2_eps = CV[0:2 * H, 72:73], CV[0:2 * H, 73:74]
        one_hot = CV[:, 80:111]

        def sum_column(m, n=2 * H):
            return one_hot[:, 15 - m:15 - m + n]

        BEGUN = DT - 1

        w_loaded = [sem(f"w_loaded{s}") for s in range(SLOTS)]
        const_in = sem("const_in")
        x_in = [sem(f"x_in{part}") for part in range(X_PARTS)]
        out_done = sem("out_done")
        outs = [0]

        def store(eng, dst, src):
            outs[0] += 16
            eng.dma_start(dst, src).then_inc(out_done, 16)

        streams = [(I["w_qkv"], QKV_T, 8), (I["w_z"], H, 8), (I["w_dout"], DT, 8),
                   (I["w_up0"], 2 * FT, 8), (I["w_down0"], 2 * DT, 11), (I["w_ple0"], DT, 10),
                   (I["w_scin"], 3 * DT, 8), (I["w_scout"], DT, 8),
                   (I["w_up1"], 2 * FT, 8), (I["w_down1"], 2 * DT, 11), (I["w_ple1"], DT, 10)]
        uses = [0]
        for _, n, _ in streams:
            uses.append(uses[-1] + n // SLOTS)

        def load_x(eng, part):
            tiles = slice(part * DT // X_PARTS, (part + 1) * DT // X_PARTS)
            eng.dma_start(X[:, tiles, :], I["x"][:, tiles]).then_inc(x_in[part], 16)

        def x_ready(pe, k, half):
            if half == 0 and k % (DT // X_PARTS) == 0:
                pe.wait_ge(x_in[k * X_PARTS // DT], 16)

        def load_weights(sync, ph, chunk_done):
            w, n, kt = streams[ph]
            with sync.Fori(1, n // SLOTS) as i:
                for s in range(SLOTS):
                    sync.wait_ge(chunk_done, (i - 1) * SLOTS + s + 1)
                    sync.dma_start(RING[:, s, 0:kt * P],
                                   w[bass.ds(i * SLOTS + s, 1)].rearrange("o p n -> p (o n)")
                                   ).then_inc(w_loaded[s], 16)
            if ph + 1 < len(streams):
                w2, n2, kt2 = streams[ph + 1]
                for s in range(SLOTS):
                    sync.wait_ge(chunk_done, n - SLOTS + s + 1)
                    sync.dma_start(RING[:, s, 0:kt2 * P], w2[s]).then_inc(w_loaded[s], 16)

        def tile_w(s, k):
            return RING[:, s, k * P:(k + 1) * P]

        def product(pe, banks, s, rhs, ks, start, stop, ready=None, done=0):
            steps = ([(n, k, half) for half in range(2) for n, k in enumerate(ks)] if ready else
                     [(n, k, half) for n, k in enumerate(ks) for half in range(2)])
            for n, k, half in steps:
                if n < done:
                    continue
                if ready:
                    ready(pe, k, half)
                last = pe.matmul(banks[half][:, 0:HALF], tile_w(s, n), rhs(k, half),
                                 start=start and n == 0, stop=stop and n == len(ks) - 1)
            return last

        def begin_next(pe, ph, rhs, tile_done):
            pe.wait_ge(w_loaded[0], (uses[ph] + 1) * 16)
            for k in range(BEGUN):
                tile_done(k)
                for half in range(2):
                    pe.matmul(BANK[half][:, 0:HALF], tile_w(0, k), rhs(k, half), start=k == 0, stop=False)

        def x_half(buf):
            return lambda k, half: buf[:, k, half * HALF:(half + 1) * HALF]

        load_n = [0]
        with nc.Block() as block:
            @block.sync
            def _(sync):
                w, _, kt = streams[0]
                for s in range(SLOTS):
                    sync.dma_start(RING[:, s, 0:kt * P], w[s]).then_inc(w_loaded[s], 16)
                    if s == 0:
                        for part in range(0, X_PARTS, 2):
                            load_x(sync, part)

            @block.scalar
            def _(act):
                for part in range(1, X_PARTS, 2):
                    load_x(act, part)

            @block.vector
            def _(dve):
                dve.memset(TOKS[:], 0.0)

        class ZTiles:
            PHASE = 1

            def __init__(self, name, tiles):
                self.tiles = tiles
                self.made, self.copied = sem(f"{name}_z_made"), sem(f"{name}_z_copied")

            def pe(self, pe, banks_free, some=slice(None)):
                for n, g in list(enumerate(self.tiles))[some]:
                    pe.wait_ge(w_loaded[g % SLOTS], (uses[self.PHASE] + g // SLOTS + 1) * 16)
                    if n < 2:
                        banks_free(n)
                    else:
                        pe.wait_ge(self.copied, n - 1)
                    product(pe, BANK[n % 2 * 2:], g % SLOTS, x_half(X), range(8), True, True).then_inc(self.made, 1)

            def act(self, act):
                for n, g in enumerate(self.tiles):
                    act.wait_ge(self.made, n + 1)
                    for half in range(2):
                        last = act.activation(Z[:, g, half * HALF:(half + 1) * HALF],
                                              BANK[n % 2 * 2 + half][:, 0:HALF], ACT.Silu)
                    last.then_inc(self.copied, 1)

            def sync(self, sync):
                for n, g in enumerate(self.tiles):
                    sync.wait_ge(self.made, n + 1)
                    w, kt, m = (I["w_z"], DT, g + SLOTS) if g + SLOTS < H else (
                        streams[self.PHASE + 1][0], streams[self.PHASE + 1][2], g + SLOTS - H)
                    sync.dma_start(RING[:, g % SLOTS, 0:kt * P], w[m]).then_inc(w_loaded[g % SLOTS], 16)

        def fill_ext(act, banks, ext, hist, filled):
            act.activation(ext[:, hist:hist + HALF], banks[0][:, 0:HALF], ACT.Copy).then_inc(filled, 1)
            act.activation(ext[:, hist + HALF:hist + SEQ], banks[1][:, 0:SEQ - HALF], ACT.Copy).then_inc(filled, 1)
            act.activation(sample_part(ext, hist)[:, :, hist:],
                           banks[1][:, SEQ - HALF:HALF].rearrange("p (b t) -> p b t", b=NB),
                           ACT.Copy).then_inc(filled, 1)

        def sample_part(ext, hist):
            return ext[:, hist + SEQ:hist + SEQ + NB * (hist + NS)].rearrange("p (b t) -> p b t", b=NB)

        def tap_run(dve, ext, out, weights, width, g, tap_done, conv_done):
            n = ext_cols(width) - (width - 1)
            per = width - 1
            dve.tensor_scalar(out[:, 0:n], ext[:, 0:n], weights(0), None, ALU.mult).then_inc(tap_done, 1)
            for j in range(1, width):
                dve.wait_ge(tap_done, g * per + j)
                dve.scalar_tensor_tensor(out=out[:, 0:n], in0=ext[:, j:j + n], scalar=weights(j), in1=out[:, 0:n],
                                         op0=ALU.mult, op1=ALU.add).then_inc(conv_done if j == per else tap_done, 1)

        def history_in(pool, ext, state, c, hist, hist_in):
            pool.tensor_copy(sample_part(ext, hist)[:, :, 0:hist],
                             state[:, bass.ds(c, 1), :].rearrange("p o (b t) -> p (o b) t", b=NB)
                             ).then_inc(hist_in, 1)

        def history_out(pool, ext, new_state, c, hist, saved):
            pool.tensor_copy(new_state[:, bass.ds(c, 1), 0:hist].rearrange("p o t -> p (o t)"),
                             ext[:, SEQ:SEQ + hist]).then_inc(saved, 1)
            pool.tensor_copy(new_state[:, bass.ds(c, 1), hist:].rearrange("p o (b t) -> p (o b) t", b=NB),
                             sample_part(ext, hist)[:, :, NS:]).then_inc(saved, 1)

        def qkv_phase(ph):
            W, n, hist = 4, QKV_T, 3
            scr = Arena()
            ext = [scr(ext_cols(W)) for _ in range(SLOTS)]
            y = [scr(ext_cols(W)) for _ in range(SLOTS)]
            state, new_state = scr(n, NB * hist), scr(n, (NB + 1) * hist)
            cw = scr(n, W)
            z = ZTiles("qkv", range(0, 2))
            chunk_done, filled, tap_done, conv_done, silu_done, hist_in, saved, st_in, pads = (
                sem(f"qkv_{x}") for x in ("chunk_done", "ext_filled", "tap_done", "conv_done", "silu_done",
                                          "hist_in", "saved", "state_in", "pads_zero"))
            with nc.Block() as block:
                @block.sync
                def _(sync):
                    sync.dma_start(state, I["st_dn"]).then_inc(st_in, 16)
                    sync.dma_start(cw, I["cw_dn"]).then_inc(st_in, 16)
                    for dst, name in ((MASKT, "mask_decay"), (MASKS, "mask_sample"), (MASKL, "mask_levels"),
                                      (IDENT, "identity"), (ONES, "ones"), (CV, "columns")):
                        sync.dma_start(dst[:], I[name]).then_inc(const_in, 16)
                        load_n[0] += 16
                    load_weights(sync, ph, chunk_done)
                    sync.wait_ge(saved, 8 + 2 * n)
                    store(sync, O["dn_conv"], new_state)
                    z.sync(sync)
                    sync.wait_ge(const_in, load_n[0])
                    sync.wait_ge(out_done, outs[0])

                @block.tensor
                def _(pe):
                    with pe.Fori(0, n // SLOTS) as i:
                        for s in range(SLOTS):
                            g = i * SLOTS + s
                            pe.wait_ge(w_loaded[s], (i + uses[ph] + 1) * 16)
                            pe.wait_ge(filled, g * 3 + 3)
                            product(pe, BANK[s % 2 * 2:], s, x_half(X), range(8), True, True,
                                    x_ready if s == 0 else None).then_inc(chunk_done, 1)
                    z.pe(pe, lambda pair: pe.wait_ge(filled, 6 + 3 * (n - 1 + pair)))

                @block.scalar
                def _(act):
                    act.sem_inc(filled, 6)
                    act.sem_inc(silu_done, 8)
                    with act.Fori(0, n // SLOTS) as i:
                        for s in range(SLOTS):
                            g = i * SLOTS + s
                            act.wait_ge(chunk_done, g + 1)
                            act.wait_ge(conv_done, g + 1)
                            act.wait_ge(saved, g * 2 + 2)
                            fill_ext(act, BANK[s % 2 * 2:], ext[s], hist, filled)
                        for s in range(SLOTS):
                            g = i * SLOTS + s
                            act.wait_ge(conv_done, g + 5)
                            out = BIG[:, bass.ds(g, 1), :].rearrange("p o t -> p (o t)")
                            act.activation(out[:, 0:SEQ], y[s][:, 0:SEQ], ACT.Silu).then_inc(silu_done, 1)
                            act.activation(out[:, SEQ:TOK].rearrange("p (b t) -> p b t", b=NB),
                                           y[s][:, SEQ + hist:SEQ + hist + NB * (hist + NS)]
                                           .rearrange("p (b t) -> p b t", b=NB)[:, :, 0:NS],
                                           ACT.Silu).then_inc(silu_done, 1)
                    z.act(act)

                @block.gpsimd
                def _(pool):
                    for s in range(SLOTS):
                        pool.memset(ext[s][:, 0:hist], 0.0).then_inc(pads, 1)
                    pool.sem_inc(saved, 8)
                    pool.wait_ge(st_in, 32)
                    with pool.Fori(0, n // SLOTS) as i:
                        for s in range(SLOTS):
                            pool.wait_ge(conv_done, i * SLOTS + s + 1)
                            pool.wait_ge(saved, (i * SLOTS + s) * 2 + 2)
                            history_in(pool, ext[s], state, i * SLOTS + s, hist, hist_in)
                        for s in range(SLOTS):
                            pool.wait_ge(filled, (i * SLOTS + s) * 3 + 9)
                            history_out(pool, ext[s], new_state, i * SLOTS + s, hist, saved)

                @block.vector
                def _(dve):
                    dve.sem_inc(conv_done, 4)
                    dve.wait_ge(st_in, 32)
                    dve.wait_ge(pads, SLOTS)
                    with dve.Fori(0, n // SLOTS) as i:
                        for s in range(SLOTS):
                            g = i * SLOTS + s
                            dve.wait_ge(filled, g * 3 + 9)
                            dve.wait_ge(hist_in, g + 1)
                            dve.wait_ge(silu_done, g * 2 + 2)
                            tap_run(dve, ext[s], y[s],
                                    lambda j: cw[:, bass.ds(g, 1), j:j + 1].rearrange("p o t -> p (o t)"),
                                    W, g, tap_done, conv_done)

        def gate_phase():
            scr = Arena()
            wba = scr(DT, 40)
            bg = scr(TOK)
            t1, t2, keep = scr(TOK), scr(TOK), scr(TOK)
            sel = scr(2 * H, P)
            sq = [scr(TOK) for _ in range(4)]
            rstd = scr(TOK)
            z = ZTiles("gate", range(2, 4))
            (w_in, ba_ready, step, logit, tr_done, gc_b, gc_out, sq_done, sq_read, std_done, rec_done, rb_done,
             normed) = (
                sem(f"gate_{x}") for x in ("w_in", "ba_ready", "dve_step", "act_step", "tr_done", "gc_b", "gc_out",
                                           "sq_done", "sq_read", "std_done", "rec_done", "rstd_bcast", "normed"))
            gate = slice(A_ROW, A_ROW + H)
            NT = 2 * H
            rows = slice(0, NT)

            def kq(m):
                return BIG[:, 3 * (m // 2) + m % 2, :]

            with nc.Block() as block:
                @block.sync
                def _(sync):
                    sync.dma_start(wba, I["w_ba"]).then_inc(w_in, 16)
                    sync.dma_start(sel, I["select"]).then_inc(w_in, 16)
                    sync.dma_start(keep[gate], I["keep"]).then_inc(w_in, 16)
                    z.sync(sync)

                @block.tensor
                def _(pe):
                    z.pe(pe, lambda pair: None, slice(0, 1))
                    pe.wait_ge(w_in, 48)
                    for k in range(DT):
                        for half in range(2):
                            last = pe.matmul(BANK[4 + half][0:40, 0:HALF], wba[:, k, :], x_half(X)(k, half),
                                             start=k == 0, stop=k == DT - 1)
                    last.then_inc(ba_ready, 1)
                    for m in range(NT):
                        pe.wait_ge(sq_done, m + 1)
                        for half in range(2):
                            last = pe.matmul(BANK[6 + half][rows, 0:HALF], sum_column(m),
                                             sq[m % 4][:, half * HALF:(half + 1) * HALF], start=m == 0,
                                             stop=m == NT - 1)
                        last.then_inc(sq_read, 1)
                    z.pe(pe, lambda pair: None, slice(1, None))
                    pe.wait_ge(rec_done, 1)
                    pe.wait_ge(z.copied, len(z.tiles))
                    for m in range(NT):
                        b = m % 3 * 2
                        if m == 2:
                            pe.wait_ge(logit, 5)
                        if m >= 3:
                            pe.wait_ge(normed, 2 * (m - 2))
                        for half in range(2):
                            last = pe.matmul(BANK[b + half][:, 0:HALF], sel[:, m, :],
                                             rstd[:, half * HALF:(half + 1) * HALF], start=True, stop=True)
                        last.then_inc(rb_done, 1)
                    pe.wait_ge(step, 7)
                    pe.wait_ge(std_done, 2)
                    for c in range(NCH + 1):
                        w = min(CH, TOK - c * CH)
                        last = pe.transpose(BANK[6][0:w, c * 40:c * 40 + 40], bg[0:40, c * CH:c * CH + w],
                                            IDENT[0:40, 0:40])
                    last.then_inc(tr_done, 1)
                    for h in range(H):
                        b = 0 if h % 2 == 0 else 2
                        pe.wait_ge(normed, 2 * NT)
                        if h >= 2:
                            pe.wait_ge(gc_out, h - 1)
                        for half in range(2):
                            last = pe.matmul(BANK[b + half][:, 0:HALF], sel[:, H + h, :],
                                             bg[:, half * HALF:(half + 1) * HALF], start=True, stop=True)
                        last.then_inc(gc_b, 1)

                @block.scalar
                def _(act):
                    for m in range(0, NT, 2):
                        if m >= 4:
                            act.wait_ge(sq_read, m - 3)
                        if m:
                            act.wait_ge(sq_done, m)
                        act.activation(sq[m % 4], kq(m), ACT.Square).then_inc(sq_done, 1)
                    act.activation(neg_ea, a_log, ACT.Exp).then_inc(logit, 1)
                    act.wait_ge(ba_ready, 1)
                    act.wait_ge(step, 1)
                    for half in range(2):
                        cols = slice(half * HALF, (half + 1) * HALF)
                        act.activation(bg[0:H, cols], BANK[4 + half][0:H, 0:HALF], ACT.Sigmoid).then_inc(logit, 1)
                    for half in range(2):
                        cols = slice(half * HALF, (half + 1) * HALF)
                        act.activation(t1[gate, cols], BANK[4 + half][gate, 0:HALF], ACT.Identity,
                                       bias=dt_bias).then_inc(logit, 1)
                    act.wait_ge(step, 3)
                    act.activation(t2[gate], t2[gate], ACT.Exp, scale=-1.0).then_inc(logit, 1)
                    act.wait_ge(logit, 6)
                    act.activation(t2[gate], t2[gate], ACT.Ln, bias=1.0).then_inc(logit, 1)
                    act.wait_ge(sq_read, NT)
                    act.wait_ge(step, 1)
                    for half in range(2):
                        act.activation(rstd[rows, half * HALF:(half + 1) * HALF], BANK[6 + half][rows, 0:HALF],
                                       ACT.Sqrt, bias=l2_eps, scale=l2_scale).then_inc(std_done, 1)
                    z.act(act)
                    for h in range(H):
                        b = 0 if h % 2 == 0 else 2
                        act.wait_ge(gc_b, h + 1)
                        for half in range(2):
                            last = act.activation(Y[:, h, half * HALF:(half + 1) * HALF],
                                                  BANK[b + half][:, 0:HALF], ACT.Copy)
                        last.then_inc(gc_out, 1)

                @block.vector
                def _(dve):
                    dve.memset(rstd, 0.0)
                    dve.memset(bg[:], 0.0).then_inc(step, 1)
                    for m in range(1, NT, 2):
                        if m >= 4:
                            dve.wait_ge(sq_read, m - 3)
                        dve.wait_ge(sq_done, m)
                        dve.tensor_tensor(sq[m % 4], kq(m), kq(m), ALU.mult).then_inc(sq_done, 1)
                    dve.wait_ge(logit, 1)
                    dve.tensor_scalar(neg_ea, neg_ea, -1.0, None, ALU.mult).then_inc(step, 1)
                    dve.wait_ge(logit, 5)
                    dve.scalar_tensor_tensor(out=t2[gate], in0=t1[gate], scalar=-1.0, in1=t1[gate],
                                             op0=ALU.mult, op1=ALU.max).then_inc(step, 1)
                    dve.wait_ge(logit, 7)
                    dve.wait_ge(step, 3)
                    dve.scalar_tensor_tensor(out=t1[gate], in0=t1[gate], scalar=0.0, in1=t2[gate],
                                             op0=ALU.max, op1=ALU.add).then_inc(step, 1)
                    dve.wait_ge(step, 4)
                    dve.tensor_scalar(t1[gate], t1[gate], neg_ea, None, ALU.mult).then_inc(step, 1)
                    dve.wait_ge(step, 5)
                    dve.wait_ge(w_in, 48)
                    dve.tensor_tensor_scan(bg[gate], keep[gate], t1[gate], 0.0, ALU.mult, ALU.add).then_inc(step, 1)
                    dve.wait_ge(step, 6)
                    dve.sem_inc(step, 1)
                    dve.wait_ge(std_done, 2)
                    dve.reciprocal(rstd[rows], rstd[rows]).then_inc(rec_done, 1)
                    for m in range(NT):
                        dve.wait_ge(rb_done, m + 1)
                        for half in range(2):
                            cols = slice(half * HALF, (half + 1) * HALF)
                            dve.tensor_tensor(kq(m)[:, cols], kq(m)[:, cols], BANK[m % 3 * 2 + half][:, 0:HALF],
                                              ALU.mult).then_inc(normed, 1)
                    dve.wait_ge(tr_done, 1)
                    for n, (toks, cs) in enumerate(((slice(0, P), slice(0, NCH)),
                                                    (slice(0, SAMP), slice(NCH, NCH + 1)))):
                        by_tok = BANK[6][toks, cs.start * 40:cs.stop * 40].rearrange("p (c n) -> p c n", n=40)
                        dve.tensor_scalar(TOKS[toks, cs, 0, :], by_tok[:, :, A_ROW:A_ROW + H], -1.0, None,
                                          ALU.mult).then_inc(step, 1)
                        dve.tensor_copy(TOKS[toks, cs, 1, :], by_tok[:, :, 0:H]).then_inc(step, 1)
                    dve.wait_ge(step, 11)
                    dve.tensor_scalar(TOKS[:, :, 3, :], TOKS[:, :, 1, :], -1.0, None, ALU.mult).then_inc(step, 1)

        def block_inverses():
            scr = Arena()
            G = scr(BL, NCH * H)
            B = scr(BL, BL)
            Tt = scr(BL, BL)
            prod = scr(BL * BL // 4)
            bt, bT = scr(NCH * H), scr(BL)
            e_done, b_done, kk_done, arg, expd, kkd, moved, row, clr, outp = (
                sem(f"inv_{x}") for x in ("tok_exp", "tok_mul", "kk_done", "arg", "exp", "kkd", "moved", "row",
                                          "cleared", "out"))
            z = ZTiles("inv", range(4, H))

            def quarters(c_h, r):
                return slice(BL * r, BL * (r + 1))

            with nc.Block() as block:
                @block.tensor
                def _(pe):
                    for q in range(NCH * H):
                        c, h = q // H, q % H
                        k = BIG[:, 3 * h, c * CH:(c + 1) * CH]
                        last = pe.matmul(BANK[q // 4][:, q % 4 * CH:(q % 4 + 1) * CH], k, k, start=True, stop=True)
                        if q % 4 == 3:
                            last.then_inc(kk_done, 1)
                    z.pe(pe, lambda pair: pe.wait_ge(kkd, 8 * (pair + 1)))

                @block.sync
                def _(sync):
                    z.sync(sync)

                @block.scalar
                def _(act):
                    act.activation(TOKS[:, :, 2, :], TOKS[:, :, 0, :], ACT.Exp, scale=-1.0).then_inc(e_done, 1)
                    act.wait_ge(arg, NBL + 1)
                    act.activation(G, G, ACT.Exp).then_inc(expd, 1)
                    z.act(act)

                @block.gpsimd
                def _(pool):
                    pool.memset(Tt, 0.0).then_inc(clr, 1)
                    pool.memset(S, 0.0)
                    pool.wait_ge(clr, 1)
                    pool.memset(Tt.rearrange("p a b -> p (a b)")[:, 0:BL * BL:BL + 1], 1.0).then_inc(clr, 1)

                @block.vector
                def _(dve):
                    gv = G.rearrange("p i (c h) -> p i c h", c=NCH)
                    for r in range(NBL):
                        part = slice(BL * r, BL * (r + 1))
                        gc = Y[part, :, 0:SEQ].rearrange("p h (c t) -> p h c t", c=NCH)[:, :, :, part]
                        dve.tensor_tensor(gv[part], gc.rearrange("p h c t -> p t c h"),
                                          TOKS[part, 0:NCH, 0, :].unsqueeze(1).to_broadcast([BL, BL, NCH, H]),
                                          ALU.add).then_inc(arg, 1)
                    dve.wait_ge(arg, NBL)
                    dve.tensor_scalar(G, G, 0.0, None, ALU.min).then_inc(arg, 1)
                    dve.wait_ge(e_done, 1)
                    dve.tensor_tensor(TOKS[:, :, 2, :], TOKS[:, :, 2, :], TOKS[:, :, 3, :],
                                      ALU.mult).then_inc(b_done, 1)
                    dve.tensor_copy(bt.rearrange("p (c h) -> p c h", c=NCH), TOKS[:, 0:NCH, 3, :]).then_inc(moved, 1)
                    dve.wait_ge(moved, 1)
                    dve.transpose(bT, bt).then_inc(moved, 1)
                    dve.wait_ge(expd, 1)
                    for q in range(NCH * H // 4):
                        dve.wait_ge(kk_done, q + 1)
                        for r in range(NBL):
                            part = slice(BL * r, BL * (r + 1))
                            g4 = G[part, :, 4 * q:4 * q + 4]
                            kk = BANK[q][part, :].rearrange("p (h t) -> p h t", h=4)[:, :, part]
                            dve.tensor_tensor(g4, g4, kk.rearrange("p h t -> p t h"), ALU.mult).then_inc(kkd, 1)
                    dve.wait_ge(kkd, NCH * H)
                    dve.transpose(B.rearrange("p a b -> p (a b)"), G.rearrange("p a b -> p (a b)")
                                  ).then_inc(moved, 1)
                    dve.wait_ge(moved, 3)
                    dve.tensor_tensor(B, B, bT.unsqueeze(2).to_broadcast([P, BL, BL]), ALU.mult).then_inc(moved, 1)
                    dve.wait_ge(moved, 4)
                    dve.wait_ge(clr, 2)
                    for i in range(BL - 1):
                        below = BL - 1 - i
                        part = Tt[:, 0:i + 1, i + 1:BL]
                        pr = prod[:, 0:(i + 1) * below].rearrange("p (c r) -> p c r", r=below)
                        if i:
                            dve.wait_ge(row, 2 * i)
                        dve.tensor_tensor(pr, Tt[:, 0:i + 1, i:i + 1].to_broadcast([P, i + 1, below]),
                                          B[:, i + 1:BL, i:i + 1].rearrange("p r o -> p o r")
                                          .to_broadcast([P, i + 1, below]), ALU.mult).then_inc(row, 1)
                        dve.wait_ge(row, 2 * i + 1)
                        dve.tensor_tensor(part, part, pr, ALU.add).then_inc(row, 1)
                    dve.wait_ge(row, 2 * (BL - 1))
                    dve.tensor_copy(B, Tt.rearrange("p c i -> p i c")).then_inc(outp, 1)
                    dve.transpose(TD[:, 0].rearrange("p a b -> p (a b)"), Tt.rearrange("p a b -> p (a b)")
                                  ).then_inc(outp, 1)
                    dve.wait_ge(outp, 2)
                    dve.transpose(TD[:, 1].rearrange("p a b -> p (a b)"), B.rearrange("p a b -> p (a b)")
                                  ).then_inc(outp, 1)

        def delta_prompt():
            scr = Arena()
            st = scr(H, 3, CH)
            dec = scr(H, CH)
            ka = scr(H, 2, CH)
            T = scr(H, 2, CH)

            def qe(h):
                return RING[:, h // 3, DT * P + h % 3 * CH:DT * P + (h % 3 + 1) * CH]

            Ys = scr(H, CH)
            ktok, vtok = scr(H, P), scr(H, P)
            vnew = scr(H, P)
            sc = scr(4, H)
            eg = scr(H, CH)
            names = ("stage", "scal", "arg", "dec", "kq", "att", "tr", "tok", "eg", "qe", "tclear", "tinit", "y",
                     "ymask", "d", "t", "ks", "r", "v", "vn", "os", "o_out", "s_out")
            q = {x: sem(f"dp_{x}") for x in names}
            with nc.Block() as block:
                @block.vector
                def _(dve):
                    dve.sem_inc(q["s_out"], H)
                    dve.sem_inc(q["qe"], 1)

                    def stage(c):
                        dve.tensor_copy(st.rearrange("p a b c -> p (a b) c"),
                                        BIG[:, :, bass.ds(c * CH, CH)]).then_inc(q["stage"], 1)

                    def attention_and_inverse(c):
                        for h in range(H):
                            dve.wait_ge(q["dec"], c * H + h + 1)
                            dve.wait_ge(q["kq"], c * H + h + 1)
                            dve.tensor_tensor(ka[:, h], BANK[h][:, 256:512].rearrange("p (a b) -> p a b", a=2),
                                              dec[:, h, :].unsqueeze(1).to_broadcast([P, 2, CH]),
                                              ALU.mult).then_inc(q["att"], 1)
                        dve.wait_ge(q["tinit"], (c + 1) * NBL)
                        for lv in range(LEVELS):
                            for h in range(H):
                                dve.wait_ge(q["y"], c * (LEVELS * H) + lv * H + h + 1)
                                dve.scalar_tensor_tensor(out=Ys[:, h, :], in0=BANK[h][:, 0:CH],
                                                         scalar=sc[:, 1, h:h + 1], in1=MASKL[:, SAMP_LEVELS + lv, :],
                                                         op0=ALU.mult, op1=ALU.mult).then_inc(q["ymask"], 1)
                            first = 1 if lv == LEVELS - 1 else 0
                            for h in range(H):
                                dve.wait_ge(q["d"], c * (LEVELS * H) + lv * H + h + 1)
                                if lv:
                                    dve.wait_ge(q["t"], c * (LEVELS * H) + (lv - 1) * H + h + 1)
                                dve.tensor_tensor(T[:, h, first:2], T[:, h, first:2],
                                                  BANK[h][:, 256 + first * CH:512]
                                                  .rearrange("p (a b) -> p a b", b=CH),
                                                  ALU.subtract).then_inc(q["t"], 1)
                        for h in range(H):
                            dve.wait_ge(q["ks"], c * H + H + h + 1)
                            dve.wait_ge(q["tok"], c * (2 * H) + 2 * h + 2)
                            dve.scalar_tensor_tensor(out=Ys[:, h, :], in0=BANK[h][:, 0:P],
                                                     scalar=sc[:, 2, h:h + 1], in1=vtok[:, h, :],
                                                     op0=ALU.mult, op1=ALU.add).then_inc(q["r"], 1)

                    def state_update(c):
                        for h in range(H):
                            dve.wait_ge(q["os"], c * H + H + h + 1)
                            dve.scalar_tensor_tensor(out=S[:, h, :], in0=S[:, h, :], scalar=eg[:, h, CH - 1:CH],
                                                     in1=BANK[h][:, 384:512], op0=ALU.mult,
                                                     op1=ALU.add).then_inc(q["s_out"], 1)

                    stage(0)
                    attention_and_inverse(0)
                    with dve.Fori(1, NCH) as c:
                        dve.wait_ge(q["qe"], c + 1)
                        dve.wait_ge(q["ks"], (c + 1) * H)
                        stage(c)
                        state_update(c - 1)
                        attention_and_inverse(c)
                    state_update(NCH - 1)

                @block.gpsimd
                def _(pool):
                    with pool.Fori(0, NCH) as c:
                        pool.wait_ge(q["vn"], (c + 1) * (2 * H))
                        pool.tensor_copy(sc, TOKS[:, bass.ds(c, 1), :, :].rearrange("p o a b -> p (o a) b")
                                         ).then_inc(q["scal"], 1)
                        pool.tensor_tensor(dec, Y[:, :, bass.ds(c * CH, CH)],
                                           MASKT[:].unsqueeze(1).to_broadcast([P, H, CH]), ALU.add
                                           ).then_inc(q["arg"], 1)
                        pool.memset(T, 0.0).then_inc(q["tclear"], 1)
                        pool.wait_ge(q["tclear"], c + 1)
                        for r in range(NBL // 2):
                            part = slice(BL * r, BL * (r + 1))
                            pool.tensor_copy(T[part, :, :, part].rearrange("p h a t -> p a t h"),
                                             TD[part, :, :, bass.ds(c * H, H)]).then_inc(q["tinit"], 1)
                        pool.wait_ge(q["stage"], c + 1)
                        pool.wait_ge(q["arg"], c + 1)
                        pool.wait_ge(q["tinit"], (c + 1) * NBL)
                        pool.wait_ge(q["eg"], c + 1)
                        pool.wait_ge(q["os"], (c + 1) * H)
                        for n, h in enumerate(range(0, H, 3)):
                            heads = min(3, H - h)
                            last = pool.tensor_tensor(RING[:, n, DT * P:DT * P + heads * CH]
                                                      .rearrange("p (h t) -> p h t", h=heads),
                                                      st[:, h:h + heads, 1, :], eg[:, h:h + heads, :], ALU.mult)
                        last.then_inc(q["qe"], 1)

                @block.scalar
                def _(act):
                    act.sem_inc(q["vn"], 2 * H)
                    act.sem_inc(q["o_out"], H)
                    with act.Fori(0, NCH) as c:
                        act.wait_ge(q["scal"], c + 1)
                        act.wait_ge(q["arg"], c + 1)
                        for h in range(H):
                            act.activation(dec[:, h, :], dec[:, h, :], ACT.Exp, bias=sc[:, 0, h:h + 1]
                                           ).then_inc(q["dec"], 1)
                        act.wait_ge(q["tclear"], c + 1)
                        for r in range(NBL // 2, NBL):
                            part = slice(BL * r, BL * (r + 1))
                            act.activation(T[part, :, :, part].rearrange("p h a t -> p a t h"),
                                           TD[part, :, :, bass.ds(c * H, H)], ACT.Copy).then_inc(q["tinit"], 1)
                        for h in range(H):
                            act.wait_ge(q["tr"], c * H + h + 1)
                            act.activation(ktok[:, h, :], BANK[h][:, 0:P], ACT.Copy).then_inc(q["tok"], 1)
                            act.activation(vtok[:, h, :], BANK[h][:, P:2 * P], ACT.Copy,
                                           scale=sc[:, 1, h:h + 1]).then_inc(q["tok"], 1)
                        act.wait_ge(q["s_out"], (c + 1) * H)
                        act.activation(eg, Y[:, :, bass.ds(c * CH, CH)], ACT.Exp).then_inc(q["eg"], 1)
                        for h in range(H):
                            act.wait_ge(q["v"], c * H + h + 1)
                            act.activation(vnew[:, h, :], BANK[h][:, 128:256], ACT.Copy).then_inc(q["vn"], 1)
                            act.activation(vtok[:, h, :], BANK[h][:, 128:256], ACT.Copy,
                                           scale=dec[:, h, CH - 1:CH]).then_inc(q["vn"], 1)
                        for h in range(H):
                            act.wait_ge(q["s_out"], c * H + H + h + 1)
                            act.activation(BIG[:, 3 * h + 1, bass.ds(c * CH, CH)], BANK[h][:, 256:384],
                                           ACT.Copy).then_inc(q["o_out"], 1)

                @block.tensor
                def _(pe):
                    pe.sem_inc(q["ks"], H)
                    pe.sem_inc(q["os"], H)
                    with pe.Fori(0, NCH) as c:
                        pe.wait_ge(q["stage"], c + 1)
                        for h in range(H):
                            pe.wait_ge(q["o_out"], c * H + h + 1)
                            pe.wait_ge(q["s_out"], c * H + h + 1)
                            pe.matmul(BANK[h][:, 256:512], st[:, h, 0, :], st[:, h, 0:2, :], start=True,
                                      stop=True).then_inc(q["kq"], 1)
                        for h in range(H):
                            pe.wait_ge(q["att"], c * H + h + 1)
                            pe.transpose(BANK[h][:, 0:P], st[:, h, 0, :], IDENT[:])
                            pe.transpose(BANK[h][:, P:2 * P], st[:, h, 2, :], IDENT[:]).then_inc(q["tr"], 1)
                        pe.wait_ge(q["tinit"], (c + 1) * NBL)
                        for lv in range(LEVELS):
                            for h in range(H):
                                if lv:
                                    pe.wait_ge(q["t"], c * (LEVELS * H) + (lv - 1) * H + h + 1)
                                else:
                                    pe.wait_ge(q["tok"], c * (2 * H) + 2 * h + 2)
                                pe.matmul(BANK[h][:, 0:CH], ka[:, h, 0, :], T[:, h, 0, :], start=True,
                                          stop=True).then_inc(q["y"], 1)
                            for h in range(H):
                                pe.wait_ge(q["ymask"], c * (LEVELS * H) + lv * H + h + 1)
                                if lv < LEVELS - 1:
                                    pe.matmul(BANK[h][:, 256:384], T[:, h, 1, :], Ys[:, h, :], start=True,
                                              stop=True)
                                pe.matmul(BANK[h][:, 384:512], Ys[:, h, :], T[:, h, 1, :], start=True,
                                          stop=True).then_inc(q["d"], 1)
                        for h in range(H):
                            pe.wait_ge(q["t"], c * (LEVELS * H) + (LEVELS - 1) * H + h + 1)
                            pe.matmul(BANK[h][:, 0:P], st[:, h, 0, :], S[:, h, :], start=True,
                                      stop=True).then_inc(q["ks"], 1)
                        for h in range(H):
                            pe.wait_ge(q["r"], c * H + h + 1)
                            pe.matmul(BANK[h][:, 128:256], T[:, h, 1, :], Ys[:, h, :], start=True,
                                      stop=True).then_inc(q["v"], 1)
                        pe.wait_ge(q["qe"], c + 2)
                        for h in range(H):
                            pe.wait_ge(q["vn"], (c + 1) * (2 * H) + 2 * h + 2)
                            pe.matmul(BANK[h][:, 256:384], S[:, h, :], qe(h), start=True, stop=False)
                            pe.matmul(BANK[h][:, 256:384], vnew[:, h, :], ka[:, h, 1, :], start=False, stop=True)
                            pe.matmul(BANK[h][:, 384:512], ktok[:, h, :], vtok[:, h, :], start=True,
                                      stop=True).then_inc(q["os"], 1)

                @block.sync
                def _(sync):
                    sync.wait_ge(q["s_out"], (NCH + 1) * H)
                    store(sync, O["dn_S_prompt"], S)

        def delta_sample():
            scr = Arena()
            stored = outs[0]
            GROUP = 4
            SH = NB // 2
            dec = scr(H, SAMP)
            ka = scr(H, 2, SAMP)
            T = scr(H, 2, SAMP)
            Ys = scr(H, SAMP)
            ktok, vtok, vnew = scr(H, P), scr(H, P), scr(H, P)
            R = vtok
            eg = scr(H, SAMP)
            NSLOT = 4
            DIAG = 2 * SAMP + NS
            sel_kq = scr(NSLOT, NB * DIAG)
            vb1 = scr(H, NB // 2, P)
            names = ("arg", "dec", "kq", "att", "tr", "tok", "eg", "tinit", "y", "ymask", "d", "t", "sel", "ks",
                     "r", "qs", "v", "vn", "o", "otok", "ot", "o_out", "vb0", "vb1", "sdec", "su", "s_out", "pad")
            q = {x: sem(f"ds_{x}") for x in names}
            sin = [sem(f"ds_state_in{h}") for h in range(H)]
            A = slice(0, SAMP)
            last_tok = slice(NS - 1, SAMP, NS)

            def smp(r):
                return BIG[:, r, SEQ:TOK]

            def states(h, r):
                return BIG[:, 3 * h + 2 * r, 0:SH * P].rearrange("p (b n) -> p b n", b=SH)

            def vb(h, r):
                return (Y[:, h, 0:SH * P] if r == 0 else vb1[:, h].rearrange("p b n -> p (b n)")
                        ).rearrange("p (b n) -> p b n", b=SH)

            def updates(h, r):
                return h // GROUP * 2 * GROUP + r * GROUP + h % GROUP + 1

            with nc.Block() as block:
                @block.sync
                def _(sync):
                    for h in range(H):
                        for r in range(2):
                            sync.dma_start(states(h, r), I["st_S"][h, :, SH * r:SH * (r + 1)]).then_inc(sin[h], 16)
                    for group in range(0, H, GROUP):
                        for r in range(2):
                            for h in range(group, group + GROUP):
                                sync.wait_ge(q["s_out"], updates(h, r))
                                store(sync, O["dn_S_sample"][h, :, SH * r:SH * (r + 1)], states(h, r))

                @block.gpsimd
                def _(pool):
                    pool.memset(sel_kq, 0.0).then_inc(q["pad"], 1)
                    pool.wait_ge(q["pad"], 1)
                    pool.memset(ktok[SAMP:P], 0.0).then_inc(q["pad"], 1)
                    pool.memset(Y[SAMP:P, :, 0:SH * P], 0.0).then_inc(q["pad"], 1)
                    pool.wait_ge(out_done, stored)
                    pool.memset(vb1[SAMP:P], 0.0).then_inc(q["pad"], 1)
                    pool.wait_ge(q["eg"], 1)
                    pool.wait_ge(q["pad"], 4)
                    for h in range(H):
                        if h >= NSLOT:
                            pool.wait_ge(q["ks"], h - NSLOT + 1)
                        own = sel_kq[:, h % NSLOT].rearrange("p (b x) -> p b x", b=NB)
                        pool.tensor_copy(own[:, :, 0:NS], smp(3 * h).rearrange("p (b t) -> p b t", b=NB)
                                         ).then_inc(q["sel"], 1)
                        pool.tensor_tensor(own[:, :, SAMP:SAMP + NS],
                                           smp(3 * h + 1).rearrange("p (b t) -> p b t", b=NB),
                                           eg[:, h, :].rearrange("p (b t) -> p b t", b=NB), ALU.mult
                                           ).then_inc(q["sel"], 1)
                    for group in range(0, H, GROUP):
                        for r in range(2):
                            for h in range(group, group + GROUP):
                                pool.wait_ge(q["ks"], h + 1)
                                pool.tensor_tensor(states(h, r), states(h, r),
                                                   eg[:, h, last_tok][:, SH * r:SH * (r + 1)].unsqueeze(2)
                                                   .to_broadcast([P, SH, P]), ALU.mult).then_inc(q["sdec"], 1)

                @block.scalar
                def _(act):
                    act.activation(eg, Y[:, :, SEQ:TOK], ACT.Exp).then_inc(q["eg"], 1)
                    for h in range(H):
                        act.wait_ge(q["arg"], h + 1)
                        act.activation(dec[A, h, :], dec[A, h, :], ACT.Exp).then_inc(q["dec"], 1)
                    for h in range(H):
                        act.wait_ge(q["tr"], h + 1)
                        act.activation(ktok[A, h, :], BANK[h][A, 0:P], ACT.Copy).then_inc(q["tok"], 1)
                        act.activation(vtok[A, h, :], BANK[h][A, P:2 * P], ACT.Copy,
                                       scale=TOKS[A, NCH, 1, h:h + 1]).then_inc(q["tok"], 1)
                    for h in range(H):
                        act.wait_ge(q["v"], h + 1)
                        act.activation(vnew[A, h, :], BANK[h][A, 256:384], ACT.Copy).then_inc(q["vn"], 1)
                        act.wait_ge(q["vn"], h + 1)
                        if h == 0:
                            act.wait_ge(out_done, stored)
                        for b in range(SH, NB):
                            last = act.activation(vb(h, 1)[A, b - SH, :], vnew[A, h, :], ACT.Copy,
                                                  scale=dec[A, h, NS * b + NS - 1:NS * b + NS])
                        last.then_inc(q["vb1"], 1)

                @block.vector
                def _(dve):
                    for h in range(H):
                        dve.scalar_tensor_tensor(out=dec[A, h, :], in0=Y[A, h, SEQ:TOK],
                                                 scalar=TOKS[A, NCH, 0, h:h + 1], in1=MASKS[A], op0=ALU.add,
                                                 op1=ALU.add).then_inc(q["arg"], 1)
                    dve.tensor_copy(T[A].rearrange("p a b c -> p (a b) c"),
                                    IDENT[A, A].unsqueeze(1).to_broadcast([SAMP, 2 * H, SAMP])
                                    ).then_inc(q["tinit"], 1)
                    for h in range(H):
                        dve.wait_ge(q["dec"], h + 1)
                        dve.wait_ge(q["kq"], h + 1)
                        dve.tensor_tensor(ka[A, h], BANK[h][A, 256:384].rearrange("p (a b) -> p a b", a=2),
                                          dec[A, h, :].unsqueeze(1).to_broadcast([SAMP, 2, SAMP]),
                                          ALU.mult).then_inc(q["att"], 1)
                    dve.wait_ge(q["tinit"], 1)
                    for lv in range(SAMP_LEVELS):
                        for h in range(H):
                            dve.wait_ge(q["y"], lv * H + h + 1)
                            dve.scalar_tensor_tensor(out=Ys[A, h, :], in0=BANK[h][A, 0:SAMP],
                                                     scalar=TOKS[A, NCH, 1, h:h + 1], in1=MASKL[A, lv, A],
                                                     op0=ALU.mult, op1=ALU.mult).then_inc(q["ymask"], 1)
                        for h in range(H):
                            dve.wait_ge(q["d"], lv * H + h + 1)
                            if lv:
                                dve.wait_ge(q["t"], (lv - 1) * H + h + 1)
                            dve.tensor_tensor(T[A, h], T[A, h],
                                              BANK[h][A, 256:384].rearrange("p (a b) -> p a b", a=2),
                                              ALU.subtract).then_inc(q["t"], 1)

                    def right_side(h):
                        dve.wait_ge(q["ks"], h + 1)
                        dve.wait_ge(q["tok"], 2 * h + 2)
                        dve.scalar_tensor_tensor(out=R[A, h, :], in0=BANK[h][A, 0:P],
                                                 scalar=TOKS[A, NCH, 2, h:h + 1], in1=vtok[A, h, :],
                                                 op0=ALU.mult, op1=ALU.add).then_inc(q["r"], 1)

                        dve.tensor_copy(vtok[SAMP:P, h, :], BANK[h][SAMP:P, 0:P]).then_inc(q["qs"], 1)

                    def decayed_values(h):
                        dve.wait_ge(q["vn"], h + 1)
                        if h == 0:
                            dve.wait_ge(q["pad"], 4)
                        dve.tensor_tensor(vb(h, 0)[A], vnew[A, h, :].unsqueeze(1).to_broadcast([SAMP, SH, P]),
                                          dec[A, h, last_tok][:, 0:SH].unsqueeze(2).to_broadcast([SAMP, SH, P]),
                                          ALU.mult).then_inc(q["vb0"], 1)

                    def outputs_by_token(h):
                        dve.wait_ge(q["o"], h + 1)
                        dve.wait_ge(q["qs"], h + 1)
                        dve.tensor_tensor(vtok[SAMP:P, h, :], vtok[SAMP:P, h, :], BANK[h][SAMP:P, 384:512],
                                          ALU.add).then_inc(q["otok"], 1)

                    def outputs(h):
                        dve.wait_ge(q["ot"], h + 1)
                        dve.tensor_copy(smp(3 * h + 1), BANK[h][:, 256:320]).then_inc(q["o_out"], 1)

                    def add_update(h, r):
                        dve.wait_ge(q["su"], updates(h, r))
                        dve.wait_ge(q["sdec"], updates(h, r))
                        dve.tensor_tensor(states(h, r), states(h, r),
                                          BANK[h][:, :].rearrange("p (b n) -> p b n", b=SH),
                                          ALU.add).then_inc(q["s_out"], 1)

                    first, second = range(GROUP), range(GROUP, H)
                    for h in first:
                        right_side(h)
                    for h in first:
                        decayed_values(h)
                    for h in first:
                        outputs_by_token(h)
                    for h in second:
                        right_side(h)
                    for h in first:
                        outputs(h)
                    for h in first:
                        add_update(h, 0)
                    for h in second:
                        decayed_values(h)
                    for h in second:
                        outputs_by_token(h)
                    for h in first:
                        add_update(h, 1)
                    for h in second:
                        outputs(h)
                    for r in range(2):
                        for h in second:
                            add_update(h, r)

                @block.tensor
                def _(pe):
                    for h in range(H):
                        pe.matmul(BANK[h][A, 256:384], smp(3 * h), BIG[:, 3 * h:3 * h + 2, SEQ:TOK], start=True,
                                  stop=True).then_inc(q["kq"], 1)
                    for h in range(H):
                        pe.wait_ge(q["att"], h + 1)
                        pe.transpose(BANK[h][A, 0:P], smp(3 * h), IDENT[:])
                        pe.transpose(BANK[h][A, P:2 * P], smp(3 * h + 2), IDENT[:]).then_inc(q["tr"], 1)
                    pe.wait_ge(q["tinit"], 1)
                    for lv in range(SAMP_LEVELS):
                        for h in range(H):
                            if lv:
                                pe.wait_ge(q["t"], (lv - 1) * H + h + 1)
                            else:
                                pe.wait_ge(q["tok"], 2 * h + 2)
                            pe.matmul(BANK[h][A, 0:SAMP], ka[A, h, 0, :], T[A, h, 0, :], start=True,
                                      stop=True).then_inc(q["y"], 1)
                        for h in range(H):
                            pe.wait_ge(q["ymask"], lv * H + h + 1)
                            pe.matmul(BANK[h][A, 256:320], T[A, h, 1, :], Ys[A, h, :], start=True, stop=True)
                            pe.matmul(BANK[h][A, 320:384], Ys[A, h, :], T[A, h, 1, :], start=True,
                                      stop=True).then_inc(q["d"], 1)

                    def state_products(h):
                        pe.wait_ge(q["t"], (SAMP_LEVELS - 1) * H + h + 1)
                        pe.wait_ge(sin[h], 32)
                        pe.wait_ge(q["sel"], 2 * h + 2)
                        for b in range(NB):
                            last = pe.matmul(BANK[h][:, 0:P], sel_kq[:, h % NSLOT, 2 * SAMP * b:2 * SAMP * (b + 1)],
                                             states(h, b // SH)[:, b % SH, :], start=b == 0, stop=b == NB - 1)
                        last.then_inc(q["ks"], 1)

                    def new_values(h):
                        pe.wait_ge(q["r"], h + 1)
                        pe.matmul(BANK[h][A, 256:384], T[A, h, 1, :], R[A, h, :], start=True,
                                  stop=True).then_inc(q["v"], 1)

                    def outputs(h):
                        pe.wait_ge(q["vn"], h + 1)
                        pe.wait_ge(q["qs"], h + 1)
                        pe.matmul(BANK[h][:, 384:512], ka[A, h, :, :], vnew[A, h, :], start=True,
                                  stop=True).then_inc(q["o"], 1)

                    def by_feature(h):
                        pe.wait_ge(q["otok"], h + 1)
                        pe.transpose(BANK[h][:, 256:320], vtok[SAMP:P, h, :], IDENT[SAMP:P, SAMP:P]
                                     ).then_inc(q["ot"], 1)

                    def state_update(h, r):
                        if r:
                            pe.wait_ge(q["vb1"], h + 1)
                            pe.wait_ge(q["s_out"], updates(h, 0))
                        else:
                            pe.wait_ge(q["vb0"], h + 1)
                            pe.wait_ge(q["o_out"], h + 1)
                        pe.matmul(BANK[h][:, :], ktok[:, h, :], vb(h, r), start=True,
                                  stop=True).then_inc(q["su"], 1)

                    pe.wait_ge(q["pad"], 4)
                    first, second = range(GROUP), range(GROUP, H)
                    for h in range(GROUP + 2):
                        state_products(h)
                    for h in first:
                        new_values(h)
                    state_products(GROUP + 2)
                    for h in first:
                        outputs(h)
                    state_products(GROUP + 3)
                    for h in first:
                        by_feature(h)
                    for h in second:
                        new_values(h)
                    for h in first:
                        state_update(h, 0)
                    for h in second:
                        outputs(h)
                    for h in first:
                        state_update(h, 1)
                    for h in second:
                        by_feature(h)
                    for r in range(2):
                        for h in second:
                            state_update(h, r)

        def residual_phase(ph, rhs, res, chunks_per_tile=1, before=None, begun=0):
            n = DT * chunks_per_tile
            kt = streams[ph][2]
            scr = Arena()
            scr(10 * TOK)
            sq = [scr(TOK) for _ in range(2)]
            chunk_done, added, squared, sum1, sum2 = phase_sems("res", ("chunk_done", "added", "squared", "summed",
                                                                        "sq_summed"))
            tiles = SLOTS // chunks_per_tile
            with nc.Block() as block:
                @block.sync
                def _(sync):
                    clear_stale(sync)
                    if before:
                        before.sync(sync)
                    load_weights(sync, ph, chunk_done)
                    sync.wait_ge(out_done, outs[0])

                @block.tensor
                def _(pe):
                    if before:
                        before.pe(pe)

                    def turn(i, done=0):
                        for s in range(SLOTS):
                            part, tile = s % chunks_per_tile, s // chunks_per_tile
                            if s == 0 and done == kt:
                                pe.sem_inc(chunk_done, 1)
                                continue
                            pe.wait_ge(w_loaded[s], (i + uses[ph] + 1) * 16)
                            if part == 0:
                                pe.wait_ge(added, i * (2 * tiles) + 2 * tile + 2)
                            product(pe, BANK[tile % 2 * 2:], s, rhs, range(part * kt, part * kt + kt),
                                    part == 0, part == chunks_per_tile - 1,
                                    before.tile_ready if before and s == 0 else None,
                                    done if s == 0 else 0).then_inc(chunk_done, 1)

                    if begun:
                        turn(0, begun)
                    with pe.Fori(1 if begun else 0, n // SLOTS) as i:
                        turn(i)

                @block.gpsimd
                def _(pool):
                    if before:
                        before.pool(pool)
                    pool.memset(stats[:, 0:2, :], 0.0).then_inc(sum1, 1)
                    pool.wait_ge(sum1, 1)
                    with pool.Fori(0, n // SLOTS) as i:
                        for t in range(tiles):
                            m = i * tiles + t
                            pool.wait_ge(added, m * 2 + 6)
                            pool.wait_ge(sum1, m + 1)
                            pool.tensor_tensor(sum_y, sum_y, Y[:, bass.ds(m, 1), :].rearrange("p o t -> p (o t)"),
                                               ALU.add).then_inc(sum1, 1)

                @block.scalar
                def _(act):
                    act.sem_inc(squared, 2)
                    if before:
                        before.act(act)
                    with act.Fori(0, n // SLOTS) as i:
                        for t in range(tiles):
                            m = i * tiles + t
                            act.wait_ge(added, m * 2 + 6)
                            act.wait_ge(sum2, m + 1)
                            act.activation(sq[t % 2], Y[:, bass.ds(m, 1), :].rearrange("p o t -> p (o t)"),
                                           ACT.Square).then_inc(squared, 1)

                @block.vector
                def _(dve):
                    dve.sem_inc(added, 4)
                    dve.sem_inc(sum2, 2)
                    if before:
                        before.dve(dve)
                    dve.wait_ge(sum1, 1)

                    def square_sum(m, t):
                        dve.wait_ge(squared, m + 3)
                        dve.wait_ge(sum2, m + 2)
                        dve.tensor_tensor(sum_sq, sum_sq, sq[t % 2], ALU.add).then_inc(sum2, 1)

                    with dve.Fori(0, n // SLOTS) as i:
                        for t in range(tiles):
                            dve.wait_ge(chunk_done, i * SLOTS + (t + 1) * chunks_per_tile)
                            m = i * tiles + t
                            for half in range(2):
                                cols = slice(half * HALF, (half + 1) * HALF)
                                dve.scalar_tensor_tensor(
                                    out=Y[:, bass.ds(m, 1), cols].rearrange("p o t -> p (o t)"),
                                    in0=res[:, bass.ds(m, 1), cols].rearrange("p o t -> p (o t)"), scalar=ALPHA,
                                    in1=BANK[t % 2 * 2 + half][:, 0:HALF], op0=ALU.mult,
                                    op1=ALU.add).then_inc(added, 1)
                            square_sum(m, t)

        class LayerNorm:
            DVE_TILES = 2

            def __init__(self, which, out):
                self.which, self.out = which, out
                (self.sums, self.mu_done, self.var, self.std_done, self.rec, self.cen, self.nrm, self.ready) = (
                    phase_sems("ln", ("sums", "mu_done", "var", "std_done", "rec", "centred", "normed", "ready")))

            def sync(self, sync):
                pass

            def tile_ready(self, pe, k, half):
                pe.wait_ge(self.ready, half * DT + k + 1)

            def pe(self, pe):
                for half in range(2):
                    for n, total in enumerate((sum_y, sum_sq)):
                        last = pe.matmul(BANK[4 + 2 * n + half][:, 0:HALF], ONES[:],
                                         total[:, half * HALF:(half + 1) * HALF], start=True, stop=True)
                    last.then_inc(self.sums, 1)

            def act(self, act):
                for half in range(2):
                    cols = slice(half * HALF, (half + 1) * HALF)
                    act.wait_ge(self.sums, half + 1)
                    act.activation(rs[:, cols], BANK[4 + half][:, 0:HALF], ACT.Square,
                                   scale=1.0 / D).then_inc(self.mu_done, 1)
                    act.activation(mu[:, cols], BANK[4 + half][:, 0:HALF], ACT.Copy,
                                   scale=1.0 / D).then_inc(self.mu_done, 1)
                    act.wait_ge(self.var, 2 * half + 2)
                    act.activation(rs[:, cols], rs[:, cols], ACT.Sqrt, bias=eps_ln).then_inc(self.std_done, 1)
                for half in range(2):
                    cols = slice(half * HALF, (half + 1) * HALF)
                    for k in range(DT):
                        act.wait_ge(self.nrm, half * DT + k + 1)
                        act.activation(self.out[:, k, cols], Y[:, k, cols], ACT.Identity,
                                       bias=lnp[:, self.which + 1, k:k + 1],
                                       scale=lnp[:, self.which, k:k + 1]).then_inc(self.ready, 1)

            def centre(self, eng, half, tiles, done):
                cols = slice(half * HALF, (half + 1) * HALF)
                eng.wait_ge(self.mu_done, 2 * half + 2)
                for k in tiles:
                    eng.tensor_tensor(Y[:, k, cols], Y[:, k, cols], mu[:, cols], ALU.subtract).then_inc(done, 1)

            def pool(self, pool):
                self.centre(pool, 0, range(self.DVE_TILES, DT), self.cen)
                self.centre(pool, 1, range(DT), self.cen)

            def dve(self, dve):
                def variance(half):
                    cols = slice(half * HALF, (half + 1) * HALF)
                    dve.wait_ge(self.sums, half + 1)
                    dve.wait_ge(self.mu_done, 2 * half + 1)
                    dve.scalar_tensor_tensor(out=rs[:, cols], in0=BANK[6 + half][:, 0:HALF], scalar=1.0 / D,
                                             in1=rs[:, cols], op0=ALU.mult, op1=ALU.subtract).then_inc(self.var, 1)
                    dve.wait_ge(self.var, 2 * half + 1)
                    dve.tensor_scalar(rs[:, cols], rs[:, cols], 0.0, None, ALU.max).then_inc(self.var, 1)

                def inverse(half):
                    cols = slice(half * HALF, (half + 1) * HALF)
                    dve.wait_ge(self.std_done, half + 1)
                    dve.reciprocal(rs[:, cols], rs[:, cols]).then_inc(self.rec, 1)

                def normalise(half):
                    cols = slice(half * HALF, (half + 1) * HALF)
                    dve.wait_ge(self.rec, self.DVE_TILES + half + 1)
                    for k in range(DT):
                        if half or k >= self.DVE_TILES:
                            dve.wait_ge(self.cen, half * DT + k - self.DVE_TILES + 1)
                        dve.tensor_tensor(Y[:, k, cols], Y[:, k, cols], rs[:, cols], ALU.mult).then_inc(self.nrm, 1)

                variance(0)
                self.centre(dve, 0, range(self.DVE_TILES), self.rec)
                inverse(0)
                variance(1)
                normalise(0)
                inverse(1)
                normalise(1)

        class GatedNorm:
            def __init__(self):
                self.sq_done, self.summed, self.std, self.rec, self.bcast, self.gated, self.ready = (
                    sem(f"rms_{x}") for x in ("sq_done", "summed", "std", "rec", "bcast", "gated", "ready"))
                self.sel_in = sem("rms_select_in")
                scr = Arena()
                self.sq = [scr(TOK) for _ in range(4)]
                self.rstd = scr(TOK)
                self.sel = scr(H, P)
                self.clr = sem("rms_cleared")

            def tile_ready(self, pe, k, half):
                pe.wait_ge(self.ready, half * DT + k + 1)

            def sync(self, sync):
                sync.dma_start(self.sel, I["select"][:, 0:H]).then_inc(self.sel_in, 16)

            def pe(self, pe):
                for h in range(H):
                    pe.wait_ge(self.sq_done, h + 1)
                    for half in range(2):
                        last = pe.matmul(BANK[6 + half][0:H, 0:HALF], sum_column(h, H),
                                         self.sq[h % 4][:, half * HALF:(half + 1) * HALF], start=h == 0,
                                         stop=h == H - 1)
                    last.then_inc(self.summed, 1)
                pe.wait_ge(self.sel_in, 16)
                for half in range(2):
                    pe.wait_ge(self.rec, half + 1)
                    for h in range(H):
                        n = half * H + h
                        if n > 5:
                            pe.wait_ge(self.ready, n - 5)
                        pe.matmul(BANK[2 + n % 6][:, 0:HALF], self.sel[:, h, :],
                                  self.rstd[:, half * HALF:(half + 1) * HALF], start=True,
                                  stop=True).then_inc(self.bcast, 1)

            def act(self, act):
                for h in range(H):
                    if h >= 4:
                        act.wait_ge(self.summed, h - 3)
                    act.activation(self.sq[h % 4], BIG[:, 3 * h + 1, :], ACT.Square).then_inc(self.sq_done, 1)
                act.wait_ge(self.summed, H)
                act.wait_ge(self.clr, 1)
                for half in range(2):
                    act.activation(self.rstd[0:H, half * HALF:(half + 1) * HALF], BANK[6 + half][0:H, 0:HALF],
                                   ACT.Sqrt, bias=eps_rms[0:H], scale=1.0 / P).then_inc(self.std, 1)

            def pool(self, pool):
                pool.memset(self.rstd, 0.0).then_inc(self.clr, 1)

            def dve(self, dve):
                for h in range(H):
                    o = BIG[:, 3 * h + 1, :]
                    dve.wait_ge(self.sq_done, h + 1)
                    dve.scalar_tensor_tensor(out=o, in0=o, scalar=norm_g, in1=Z[:, h, :], op0=ALU.mult,
                                             op1=ALU.mult).then_inc(self.gated, 1)
                dve.wait_ge(self.std, 2)
                for half in range(2):
                    cols = slice(half * HALF, (half + 1) * HALF)
                    dve.reciprocal(self.rstd[0:H, cols], self.rstd[0:H, cols]).then_inc(self.rec, 1)
                dve.wait_ge(self.gated, H)
                for half in range(2):
                    for h in range(H):
                        dve.wait_ge(self.bcast, half * H + h + 1)
                        o = BIG[:, 3 * h + 1, half * HALF:(half + 1) * HALF]
                        dve.tensor_tensor(o, o, BANK[2 + (half * H + h) % 6][:, 0:HALF],
                                          ALU.mult).then_inc(self.ready, 1)

        def ffn_up(ph, x, layer, before):
            W, n, hist = 3, 2 * FT, 2
            scr = Arena()
            ext = [scr(ext_cols(W)) for _ in range(SLOTS)]
            y = [scr(ext_cols(W)) for _ in range(SLOTS)]
            state, new_state = scr(n, NB * hist), scr(n, (NB + 1) * hist)
            cw = scr(n, W)
            chunk_done, filled, tap_done, conv_done, silu_done, gated, hist_in, saved, st_in, pads = (
                phase_sems("up", ("chunk_done", "ext_filled", "tap_done", "conv_done", "silu_done",
                                  "gated", "hist_in", "saved", "state_in", "pads_zero")))
            cols = SEQ + hist + NB * (hist + NS)
            with nc.Block() as block:
                @block.sync
                def _(sync):
                    clear_stale(sync)
                    sync.dma_start(state, I[f"st_ffn{layer}"]).then_inc(st_in, 16)
                    sync.dma_start(cw, I[f"cw_ffn{layer}"]).then_inc(st_in, 16)
                    load_weights(sync, ph, chunk_done)
                    sync.wait_ge(saved, 8 + 2 * n)
                    store(sync, O[f"ffn_conv{layer}"], new_state)
                    sync.wait_ge(out_done, outs[0])

                @block.tensor
                def _(pe):
                    before.pe(pe)
                    with pe.Fori(0, n // SLOTS) as i:
                        for s in range(SLOTS):
                            g = i * SLOTS + s
                            pe.wait_ge(w_loaded[s], (i + uses[ph] + 1) * 16)
                            pe.wait_ge(filled, g * 3 + 3)
                            product(pe, BANK[s % 2 * 2:], s, x_half(x), range(8), True, True,
                                    before.tile_ready if s == 0 else None).then_inc(chunk_done, 1)
                    pe.wait_ge(w_loaded[0], (uses[ph + 1] + 1) * 16)
                    pe.wait_ge(filled, 3 * n + 3)
                    pe.wait_ge(gated, 4 + 2 * (FT // 2))
                    product(pe, BANK, 0, x_half(BIG), range(FT // 2), True, False)

                @block.scalar
                def _(act):
                    act.sem_inc(filled, 6)
                    before.act(act)
                    with act.Fori(0, n // SLOTS) as i:
                        for s in range(SLOTS):
                            g = i * SLOTS + s
                            act.wait_ge(chunk_done, g + 1)
                            act.wait_ge(conv_done, g + 1)
                            act.wait_ge(saved, g * 2 + 2)
                            fill_ext(act, BANK[s % 2 * 2:], ext[s], hist, filled)
                            if s % 2:
                                act.wait_ge(conv_done, g + 5)
                                act.activation(y[s][:, 0:cols - hist], y[s][:, 0:cols - hist],
                                               ACT.Silu).then_inc(silu_done, 1)

                @block.gpsimd
                def _(pool):
                    for s in range(SLOTS):
                        pool.memset(ext[s][:, 0:hist], 0.0).then_inc(pads, 1)
                    pool.sem_inc(saved, 8)
                    before.pool(pool)
                    pool.wait_ge(st_in, 32)
                    with pool.Fori(0, n // SLOTS) as i:
                        for s in range(SLOTS):
                            pool.wait_ge(conv_done, i * SLOTS + s + 1)
                            pool.wait_ge(saved, (i * SLOTS + s) * 2 + 2)
                            history_in(pool, ext[s], state, i * SLOTS + s, hist, hist_in)
                        for s in range(SLOTS):
                            pool.wait_ge(filled, (i * SLOTS + s) * 3 + 9)
                            history_out(pool, ext[s], new_state, i * SLOTS + s, hist, saved)

                @block.vector
                def _(dve):
                    dve.sem_inc(conv_done, 4)
                    dve.sem_inc(gated, 4)
                    before.dve(dve)
                    dve.wait_ge(st_in, 32)
                    dve.wait_ge(pads, SLOTS)
                    with dve.Fori(0, n // SLOTS) as i:
                        for pair in range(2):
                            for s in (2 * pair, 2 * pair + 1):
                                g = i * SLOTS + s
                                dve.wait_ge(filled, g * 3 + 9)
                                dve.wait_ge(hist_in, g + 1)
                                dve.wait_ge(gated, i * 4 + 2 * pair + 2)
                                tap_run(dve, ext[s], y[s],
                                        lambda j: cw[:, bass.ds(g, 1), j:j + 1].rearrange("p o t -> p (o t)"),
                                        W, g, tap_done, conv_done)
                            dve.wait_ge(conv_done, i * SLOTS + 2 * pair + 6)
                            dve.wait_ge(silu_done, i * 2 + pair + 1)
                            hid = BIG[:, bass.ds(i * 2 + pair, 1), :].rearrange("p o t -> p (o t)")
                            a, b = y[2 * pair], y[2 * pair + 1]
                            dve.tensor_tensor(hid[:, 0:SEQ], a[:, 0:SEQ], b[:, 0:SEQ], ALU.mult).then_inc(gated, 1)

                            def smp(v):
                                return v[:, SEQ + hist:cols].rearrange("p (b t) -> p b t", b=NB)[:, :, 0:NS]
                            dve.tensor_tensor(hid[:, SEQ:TOK].rearrange("p (b t) -> p b t", b=NB), smp(a), smp(b),
                                              ALU.mult).then_inc(gated, 1)

        def ple_phase(ph, x, out, layer, before):
            scr = Arena()
            pe_in = scr(PLE_T, TOK)
            sg = [scr(TOK) for _ in range(2)]
            chunk_done, sig, prod, added, p_in = (
                phase_sems("ple", ("chunk_done", "sigmoid", "product", "added", "p_in")))
            with nc.Block() as block:
                @block.sync
                def _(sync):
                    clear_stale(sync)
                    sync.dma_start(pe_in, I[f"p{layer}"]).then_inc(p_in, 16)
                    load_weights(sync, ph, chunk_done)
                    if layer == 1:
                        for part in range(2):
                            sync.wait_ge(added, 2 + (part + 1) * (DT // 2))
                            tiles = slice(part * (DT // 2), (part + 1) * (DT // 2))
                            store(sync, O["y"][:, tiles], out[:, tiles, :])

                @block.tensor
                def _(pe):
                    before.pe(pe)
                    pe.wait_ge(p_in, 16)
                    with pe.Fori(0, DT // SLOTS) as i:
                        for s in range(SLOTS):
                            g = i * SLOTS + s
                            b = s % 2 * 4
                            pe.wait_ge(w_loaded[s], (i + uses[ph] + 1) * 16)
                            pe.wait_ge(sig, g * 2 + 2)
                            pe.wait_ge(prod, g * 2 + 2)
                            for n in range(PLE_T):
                                for half in range(2):
                                    pe.matmul(BANK[b + 2 + half][:, 0:HALF], tile_w(s, DT + n),
                                              x_half(pe_in)(n, half), start=n == 0, stop=n == PLE_T - 1)
                            product(pe, BANK[b:], s, x_half(x), range(8), True, True,
                                    before.tile_ready if s == 0 else None).then_inc(chunk_done, 1)
                    if layer == 0:
                        pe.wait_ge(sig, 2 * DT + 2)
                        begin_next(pe, ph + 1, x_half(out), lambda k: pe.wait_ge(added, k + 3))

                @block.scalar
                def _(act):
                    act.sem_inc(sig, 4)
                    before.act(act)
                    with act.Fori(0, DT // SLOTS) as i:
                        for s in range(SLOTS):
                            g = i * SLOTS + s
                            act.wait_ge(chunk_done, g + 1)
                            act.wait_ge(added, g + 1)
                            for half in range(2):
                                act.activation(sg[s % 2][:, half * HALF:(half + 1) * HALF],
                                               BANK[s % 2 * 4 + half][:, 0:HALF], ACT.Sigmoid).then_inc(sig, 1)

                @block.gpsimd
                def _(pool):
                    before.pool(pool)

                @block.vector
                def _(dve):
                    dve.sem_inc(prod, 4)
                    dve.sem_inc(added, 2)
                    before.dve(dve)
                    with dve.Fori(0, DT // SLOTS) as i:
                        for s in range(SLOTS):
                            g = i * SLOTS + s
                            dve.wait_ge(sig, g * 2 + 6)
                            for half in range(2):
                                cols = slice(half * HALF, (half + 1) * HALF)
                                dve.tensor_tensor(sg[s % 2][:, cols], sg[s % 2][:, cols],
                                                  BANK[s % 2 * 4 + 2 + half][:, 0:HALF], ALU.mult).then_inc(prod, 1)
                            dve.wait_ge(prod, g * 2 + 6)
                            dve.tensor_tensor(out[:, bass.ds(g, 1), :].rearrange("p o t -> p (o t)"),
                                              x[:, bass.ds(g, 1), :].rearrange("p o t -> p (o t)"), sg[s % 2],
                                              ALU.add).then_inc(added, 1)

        def shortconv_phase(ph, x):
            W, n, hist = 3, 3 * DT, 2
            group = 12
            scr = Arena()
            ext = [scr(ext_cols(W)) for _ in range(2)]
            y = [scr(ext_cols(W)) for _ in range(2)]
            cs = [scr(TOK) for _ in range(2)]
            state, new_state = scr(DT, NB * hist), scr(DT, (NB + 1) * hist)
            cw = scr(DT, W)
            chunk_done, c_out, ch_out, tap_done, conv_done, b_out, hist_in, saved, st_in, pads = (
                sem(f"sc_{y}") for y in ("chunk_done", "c_out", "ch_out", "tap_done", "conv_done", "b_out",
                                         "hist_in", "saved", "state_in", "pads_zero"))
            cols = SEQ + hist + NB * (hist + NS)
            with nc.Block() as block:
                @block.sync
                def _(sync):
                    clear_stale(sync)
                    sync.dma_start(state, I["st_sc"]).then_inc(st_in, 16)
                    sync.dma_start(cw, I["cw_sc"]).then_inc(st_in, 16)
                    load_weights(sync, ph, chunk_done)
                    sync.wait_ge(saved, 4 + 2 * DT)
                    store(sync, O["sc_conv"], new_state)
                    sync.wait_ge(out_done, outs[0])

                @block.tensor
                def _(pe):
                    def turn(i, done=0):
                        for j in range(group):
                            s, t, r = j % SLOTS, j // 3, j % 3
                            m = i * (group // 3) + t
                            pe.wait_ge(w_loaded[s], (i * (group // SLOTS) + (uses[ph] + j // SLOTS + 1)) * 16)
                            if r == 0:
                                pe.wait_ge(c_out, m * 2 + 2)
                            elif r == 1:
                                pe.wait_ge(ch_out, m * 3 + 3)
                            else:
                                pe.wait_ge(b_out, m * 3 + 3)
                            product(pe, BANK[2 * r:], s, x_half(x), range(8), True, True,
                                    done=done if j == 0 else 0).then_inc(chunk_done, 1)

                    turn(0, BEGUN)
                    with pe.Fori(1, n // group) as i:
                        turn(i)
                    pe.wait_ge(c_out, 2 * DT + 2)
                    begin_next(pe, ph + 1, x_half(BIG), lambda k: pe.wait_ge(b_out, 3 * k + 6))

                @block.scalar
                def _(act):
                    act.sem_inc(c_out, 2)
                    with act.Fori(0, DT // 2) as i:
                        for t in range(2):
                            m = i * 2 + t
                            act.wait_ge(chunk_done, m * 3 + 1)
                            act.wait_ge(ch_out, m * 3 + 3)
                            for half in range(2):
                                act.activation(cs[t][:, half * HALF:(half + 1) * HALF], BANK[half][:, 0:HALF],
                                               ACT.Copy).then_inc(c_out, 1)

                @block.gpsimd
                def _(pool):
                    for s in range(2):
                        pool.memset(ext[s][:, 0:hist], 0.0).then_inc(pads, 1)
                    pool.sem_inc(saved, 4)
                    pool.wait_ge(st_in, 32)
                    with pool.Fori(0, DT // 2) as i:
                        for s in range(2):
                            m = i * 2 + s
                            pool.wait_ge(conv_done, m + 1)
                            pool.wait_ge(saved, m * 2 + 2)
                            history_in(pool, ext[s], state, m, hist, hist_in)
                        for s in range(2):
                            m = i * 2 + s
                            pool.wait_ge(ch_out, m * 3 + 6)
                            history_out(pool, ext[s], new_state, m, hist, saved)

                @block.vector
                def _(dve):
                    dve.sem_inc(ch_out, 3)
                    dve.sem_inc(b_out, 3)
                    dve.sem_inc(conv_done, 2)
                    dve.wait_ge(st_in, 32)
                    dve.wait_ge(pads, 2)
                    with dve.Fori(0, DT // 2) as i:
                        for t in range(2):
                            m = i * 2 + t
                            dve.wait_ge(chunk_done, m * 3 + 2)
                            dve.wait_ge(c_out, m * 2 + 4)
                            dve.wait_ge(conv_done, m + 1)
                            dve.wait_ge(saved, m * 2 + 2)
                            e = ext[t]
                            dve.tensor_tensor(e[:, hist:hist + HALF], cs[t][:, 0:HALF], BANK[2][:, 0:HALF],
                                              ALU.mult).then_inc(ch_out, 1)
                            dve.tensor_tensor(e[:, hist + HALF:hist + SEQ], cs[t][:, HALF:SEQ],
                                              BANK[3][:, 0:SEQ - HALF], ALU.mult).then_inc(ch_out, 1)
                            dve.tensor_tensor(sample_part(e, hist)[:, :, hist:],
                                              cs[t][:, SEQ:TOK].rearrange("p (b t) -> p b t", b=NB),
                                              BANK[3][:, SEQ - HALF:HALF].rearrange("p (b t) -> p b t", b=NB),
                                              ALU.mult).then_inc(ch_out, 1)
                            dve.wait_ge(ch_out, m * 3 + 6)
                            dve.wait_ge(hist_in, m + 1)
                            dve.wait_ge(b_out, m * 3 + 3)
                            tap_run(dve, e, y[t],
                                    lambda j: cw[:, bass.ds(m, 1), j:j + 1].rearrange("p o t -> p (o t)"),
                                    W, m, tap_done, conv_done)
                            dve.wait_ge(conv_done, m + 3)
                            dve.wait_ge(chunk_done, m * 3 + 3)
                            out = BIG[:, bass.ds(m, 1), :].rearrange("p o t -> p (o t)")
                            dve.tensor_tensor(out[:, 0:HALF], y[t][:, 0:HALF], BANK[4][:, 0:HALF],
                                              ALU.mult).then_inc(b_out, 1)
                            dve.tensor_tensor(out[:, HALF:SEQ], y[t][:, HALF:SEQ], BANK[5][:, 0:SEQ - HALF],
                                              ALU.mult).then_inc(b_out, 1)
                            dve.tensor_tensor(out[:, SEQ:TOK].rearrange("p (b t) -> p b t", b=NB),
                                              y[t][:, SEQ + hist:cols].rearrange("p (b t) -> p b t", b=NB)[:, :, 0:NS],
                                              BANK[5][:, SEQ - HALF:HALF].rearrange("p (b t) -> p b t", b=NB),
                                              ALU.mult).then_inc(b_out, 1)

        qkv_phase(0)
        gate_phase()
        block_inverses()
        delta_prompt()
        delta_sample()
        residual_phase(2, lambda k, half: BIG[:, 3 * k + 1, half * HALF:(half + 1) * HALF], X,
                       before=GatedNorm())
        ffn_up(3, X, 0, LayerNorm(0, X))
        residual_phase(4, x_half(BIG), X, 2, begun=FT // 2)
        ple_phase(5, X, Z, 0, LayerNorm(2, X))
        shortconv_phase(6, Z)
        residual_phase(7, x_half(BIG), Z, begun=BEGUN)
        ffn_up(8, Z, 1, LayerNorm(4, Z))
        residual_phase(9, x_half(BIG), Z, 2, begun=FT // 2)
        ple_phase(10, Z, X, 1, LayerNorm(6, Z))
        with nc.Block() as block:
            @block.sync
            def _(sync):
                sync.wait_ge(out_done, outs[0])


_OUTS = {"y": (P, DT, TOK), "dn_conv": (P, QKV_T, 27), "dn_S_prompt": (P, H, P), "dn_S_sample": (H, P, NB, P),
         "sc_conv": (P, DT, 18), "ffn_conv0": (P, 2 * FT, 18), "ffn_conv1": (P, 2 * FT, 18)}


def _tiles(w, kt):
    import numpy as np
    K, N = w.shape
    a = w.reshape(K // (kt * P), kt, P, N // P, P).transpose(3, 0, 2, 1, 4)
    return np.ascontiguousarray(a.reshape(-1, P, kt * P))


def _cols(v):
    import numpy as np
    a = np.asarray(v)
    a = a.reshape(a.shape[:-1] + (a.shape[-1] // P, P))
    return np.ascontiguousarray(np.moveaxis(a, (-1, -2), (0, 1)))


def kernel(**inputs):
    import numpy as np
    import concourse.bacc as bacc
    from concourse.bass_utils import run_bass_kernel_spmd

    a = {k: np.asarray(v) for k, v in inputs.items()}
    f32 = np.float32

    def feat(prompt, sample, n):
        rows = np.concatenate([prompt.reshape(SEQ, -1), sample.reshape(SAMP, -1)])
        return np.ascontiguousarray(rows.T.reshape(n, P, TOK).transpose(1, 0, 2))

    def state(s, order):
        t = _cols(s)[:, order]
        return np.ascontiguousarray(t.reshape(P, len(order), -1))

    w_in = a["dn_w_in"][0]
    qkv_order = [x * H + h for h in range(H) for x in (1, 0, 2)]
    up_order = [x * FT + t for t in range(FT) for x in range(2)]
    sc_order = [x * DT + t for t in range(DT) for x in (1, 2, 0)]
    m = {"x": feat(a["x_prompt"], a["x_sample"], DT)}
    m["w_qkv"] = _tiles(w_in[:, :QKV_T * P], 8)[qkv_order]
    m["w_z"] = _tiles(w_in[:, QKV_T * P:4 * D], 8)
    ba = np.zeros((D, 40), f32)
    ba[:, 0:H] = w_in[:, 4 * D:4 * D + H]
    ba[:, A_ROW:] = w_in[:, 4 * D + H:]
    m["w_ba"] = np.ascontiguousarray(ba.reshape(DT, P, 40).transpose(1, 0, 2))
    m["w_dout"] = _tiles(a["dn_w_out"][0], 8)
    m["w_scin"] = _tiles(a["sc_w_in"][0], 8)[sc_order]
    m["w_scout"] = _tiles(a["sc_w_out"][0], 8)
    for l in range(2):
        m[f"w_up{l}"] = _tiles(a["ffn_w_up"][l], 8)[up_order]
        m[f"w_down{l}"] = _tiles(a["ffn_w_down"][l], 11)
        m[f"w_ple{l}"] = np.ascontiguousarray(np.concatenate(
            [_tiles(a["ple_w_gate"][l], 8), _tiles(a["ple_w_proj"][l], PLE_T)], axis=2))
        m[f"p{l}"] = feat(a["p_prompt"][l], a["p_sample"][l], PLE_T)
        m[f"st_ffn{l}"] = state(a["state_ffn_conv"][l], up_order)
        m[f"cw_ffn{l}"] = np.ascontiguousarray(_cols(a["ffn_conv_w"][l])[:, up_order])
    m["st_dn"] = state(a["state_dn_conv"][0], qkv_order)
    m["cw_dn"] = np.ascontiguousarray(_cols(a["dn_conv_w"][0])[:, qkv_order])
    m["st_sc"] = state(a["state_sc_conv"][0], list(range(DT)))
    m["cw_sc"] = _cols(a["sc_conv_w"][0])
    m["st_S"] = np.ascontiguousarray(a["state_dn_S"][0].transpose(1, 2, 0, 3))
    i, j = np.indices((P, P))
    m["mask_decay"] = np.where(j >= i, 0.0, -1e30).astype(f32)
    m["mask_sample"] = np.where((j >= i) & (j // NS == i // NS), 0.0, -1e30).astype(f32)[:, :SAMP].copy()
    m["mask_levels"] = np.ascontiguousarray(np.stack(
        [((i // s // 2 == j // s // 2) & (i // s % 2 == 1) & (j // s % 2 == 0)) for s in
         [1 << lv for lv in range(SAMP_LEVELS)] + [BL << lv for lv in range(LEVELS)]], axis=1).astype(f32))
    m["identity"] = np.eye(P, dtype=f32)
    m["ones"] = np.ones((P, P), f32)
    sel = np.zeros((P, 2 * H, P), f32)
    for n in range(2 * H):
        sel[n, n] = 1.0
    for h in range(H):
        sel[A_ROW + h, H + h] = 1.0
    m["select"] = sel
    keep = np.ones((H, TOK), f32)
    keep[:, 0:SEQ:CH] = 0.0
    keep[:, SEQ::NS] = 0.0
    m["keep"] = keep
    cv = np.zeros((P, 160), f32)
    for l in range(2):
        for n, name in enumerate(("ln_mix_g", "ln_mix_b", "ln_ffn_g", "ln_ffn_b")):
            at = (4 * l + n) * DT
            cv[:, at:at + DT] = _cols(a[name][l])
    cv[:, 64] = a["dn_norm_g"][0]
    cv[:, 65:69] = [1e-5, 1e-6, 1e-6, 128e-6]
    cv[A_ROW:A_ROW + H, 69] = a["dn_a_log"][0]
    cv[A_ROW:A_ROW + H, 70] = a["dn_dt_bias"][0]
    cv[0:2 * H, 72] = [1.0, 128.0] * H
    cv[0:2 * H, 73] = [1e-6, 128e-6] * H
    cv[:, 95] = 1.0
    m["columns"] = cv

    nc = bacc.Bacc("TRN2", target_bir_lowering=False, num_devices=1)
    I = {k: nc.dram_tensor(f"in_{k}", v.shape, F32, kind="ExternalInput").ap() for k, v in m.items()}
    O = {k: nc.dram_tensor(f"out_{k}", s, F32, kind="ExternalOutput").ap() for k, s in _OUTS.items()}
    build(nc, I, O)
    r = run_bass_kernel_spmd(nc, [{f"in_{k}": np.ascontiguousarray(v) for k, v in m.items()}], core_ids=[0])
    got = {k: np.asarray(r.results[0][f"out_{k}"]) for k in _OUTS}

    y = got["y"].transpose(1, 0, 2).reshape(D, TOK).T

    def rows(s, order, hist):
        t = np.empty_like(s)
        t[:, order] = s
        t = t.transpose(2, 1, 0).reshape(NB + 1, hist, -1)
        return t[0:1], t[1:]

    dn = rows(got["dn_conv"], qkv_order, 3)
    sc = rows(got["sc_conv"], list(range(DT)), 2)
    ff = [rows(got[f"ffn_conv{l}"], up_order, 2) for l in range(2)]
    S_prompt = got["dn_S_prompt"].transpose(1, 0, 2)[None, None]
    S_sample = got["dn_S_sample"].transpose(2, 0, 1, 3)[None]
    return (y[:SEQ].reshape(1, SEQ, D).copy(), y[SEQ:].reshape(NB, NS, D).copy(), dn[0][None], S_prompt.copy(),
            sc[0][None], np.stack([f[0] for f in ff]), dn[1][None], S_sample.copy(), sc[1][None],
            np.stack([f[1] for f in ff]))
```
